# Optimizing a Trainium2 kernel written in Bass

```python
import math
import jax, jax.numpy as jnp
from jax import lax
import numpy as np

D_MODEL = 1024
BATCH = 1
SEQ = 256
DEPTH = 1
DEC_BATCH = 1
DEC_SEQ = 1024
PAST_LEN = 128

D_MIX = D_MODEL
CONV_W = D_MIX // 2
CONV_K = 3
N_HEADS = 4
V_DIM = (D_MIX // 2) // N_HEADS
QK_DIM = V_DIM // 2
QK_W = N_HEADS * QK_DIM
V_W = N_HEADS * V_DIM
N_GATES = 4
CHUNK = 128
N_EXPERTS = 16
EXPERT_FF = 1024
CAPACITY_FACTOR = 2
EPS = 1e-6
SPLITS = (CONV_W, 2 * CONV_W, 3 * CONV_W,
          3 * CONV_W + QK_W, 3 * CONV_W + 2 * QK_W,
          3 * CONV_W + 2 * QK_W + V_W, 3 * CONV_W + 2 * QK_W + 2 * V_W)
D_IN = 3 * CONV_W + 2 * QK_W + 2 * V_W + N_GATES * N_HEADS

kernel_name = "hybrid_conv_mlstm_ec_moe_encoder"

def rms_norm(x, g):
    xf = x.astype(jnp.float32)
    y = xf * lax.rsqrt(jnp.mean(xf * xf, axis=-1, keepdims=True) + EPS)
    return (y * g.astype(jnp.float32)).astype(x.dtype)

def short_conv(u, w):
    up = jnp.pad(u, ((0, 0), (1, 1), (0, 0)))
    s = u.shape[1]
    return up[:, 0:s] * w[0] + up[:, 1:s + 1] * w[1] + up[:, 2:s + 2] * w[2]

def mlstm_scan(q, k, v, li, lf):
    b, s, h, dk = q.shape
    dv = v.shape[-1]
    nc = s // CHUNK

    def chunks(a):
        return jnp.moveaxis(a.reshape(b, nc, CHUNK, h, a.shape[-1]), (1, 3), (0, 2))

    def gchunks(a):
        return jnp.moveaxis(a.reshape(b, nc, CHUNK, h), (1, 3), (0, 2))

    tril = jnp.tril(jnp.ones((CHUNK, CHUNK), dtype=bool))

    def step(carry, xs):
        c_st, n_st, m_st = carry
        qc, kc, vc, lic, lfc = xs
        bcum = jnp.cumsum(lfc, axis=-1)
        g = bcum[..., -1]
        log_d = bcum[..., :, None] - bcum[..., None, :] + lic[..., None, :]
        log_d = jnp.where(tril, log_d, -jnp.inf)
        m_inter = bcum + m_st[..., None]
        m_t = jnp.maximum(m_inter, jnp.max(log_d, axis=-1))
        s_mat = jnp.einsum('bhtk,bhsk->bhts', qc, kc) * jnp.exp(log_d - m_t[..., None])
        scale_inter = jnp.exp(m_inter - m_t)
        num = jnp.einsum('bhts,bhsv->bhtv', s_mat, vc) + \
            scale_inter[..., None] * jnp.einsum('bhtk,bhkv->bhtv', qc, c_st)
        den = jnp.sum(s_mat, axis=-1) + scale_inter * jnp.einsum('bhtk,bhk->bht', qc, n_st)
        h_out = num / jnp.maximum(jnp.abs(den), jnp.exp(-m_t))[..., None]
        log_w = g[..., None] - bcum + lic
        m_new = jnp.maximum(g + m_st, jnp.max(log_w, axis=-1))
        w = jnp.exp(log_w - m_new[..., None])
        decay = jnp.exp(g + m_st - m_new)
        c_new = decay[..., None, None] * c_st + jnp.einsum('bhs,bhsk,bhsv->bhkv', w, kc, vc)
        n_new = decay[..., None] * n_st + jnp.einsum('bhs,bhsk->bhk', w, kc)
        return (c_new, n_new, m_new), h_out

    init = (jnp.zeros((b, h, dk, dv), jnp.float32),
            jnp.zeros((b, h, dk), jnp.float32),
            jnp.zeros((b, h), jnp.float32))
    _, hs = lax.scan(step, init, (chunks(q), chunks(k), chunks(v), gchunks(li), gchunks(lf)))
    return jnp.moveaxis(hs, (0, 2), (1, 3)).reshape(b, s, h, dv)

def mixer_sublayer(x, norm_g, w_in, conv_w, gate_bias, head_norm_g, w_out):
    bsz, s, _ = x.shape
    hn = rms_norm(x, norm_g)
    proj = jnp.einsum('bsd,de->bse', hn, w_in)
    gb, gc, u, q, k, v, o, gates = jnp.split(proj, SPLITS, axis=-1)
    conv_out = gb * short_conv(gc * u, conv_w)
    q = q.astype(jnp.float32).reshape(bsz, s, N_HEADS, QK_DIM) * (QK_DIM ** -0.5)
    k = k.astype(jnp.float32).reshape(bsz, s, N_HEADS, QK_DIM)
    v = v.astype(jnp.float32).reshape(bsz, s, N_HEADS, V_DIM)
    gates = gates.astype(jnp.float32).reshape(bsz, s, N_GATES, N_HEADS) + gate_bias.astype(jnp.float32)
    li_f, lf_f = gates[:, :, 0], jax.nn.log_sigmoid(gates[:, :, 1])
    li_b, lf_b = gates[:, :, 2], jax.nn.log_sigmoid(gates[:, :, 3])
    h_fwd = mlstm_scan(q, k, v, li_f, lf_f)
    flip = lambda a: jnp.flip(a, axis=1)
    h_bwd = flip(mlstm_scan(flip(q), flip(k), flip(v), flip(li_b), flip(lf_b)))
    ht = h_fwd + h_bwd
    ht = ht * lax.rsqrt(jnp.mean(ht * ht, axis=-1, keepdims=True) + EPS)
    ht = ht * head_norm_g.astype(jnp.float32).reshape(N_HEADS, V_DIM)
    mlstm_out = jax.nn.sigmoid(o) * ht.reshape(bsz, s, V_W).astype(x.dtype)
    mix = jnp.concatenate([conv_out, mlstm_out], axis=-1)
    return x + jnp.einsum('bse,ed->bsd', mix, w_out)

def expert_choice_sublayer(x, norm_g, w_router, w_gate, w_up, w_down):
    bsz, s, d = x.shape
    n_tok = bsz * s
    cap = CAPACITY_FACTOR * n_tok // N_EXPERTS
    tokens = rms_norm(x, norm_g).reshape(n_tok, d)
    logits = jnp.einsum('nd,de->ne', tokens.astype(jnp.float32), w_router.astype(jnp.float32))
    affinity = jax.nn.softmax(logits, axis=-1)
    gate, idx = lax.top_k(affinity.T, cap)
    xe = tokens[idx]
    hid = jax.nn.silu(jnp.einsum('ecd,edf->ecf', xe, w_gate)) * jnp.einsum('ecd,edf->ecf', xe, w_up)
    ye = jnp.einsum('ecf,efd->ecd', hid, w_down) * gate[..., None].astype(x.dtype)
    out = jnp.zeros((n_tok, d), x.dtype).at[idx.reshape(-1)].add(ye.reshape(-1, d))
    return x + out.reshape(bsz, s, d)

def setup_inputs(seed: int = 0) -> dict:
    key = jax.random.key(seed)
    ks = jax.random.split(key, 16)
    f32 = jnp.float32
    x_prompt = jax.random.normal(ks[0], (BATCH, SEQ, D_MODEL), f32)
    x_sample = jax.random.normal(ks[1], (DEC_BATCH, DEC_SEQ, D_MODEL), f32)
    norm1_g = 1.0 + 0.05 * jax.random.normal(ks[2], (DEPTH, D_MODEL), f32)
    w_in = jax.random.normal(ks[3], (DEPTH, D_MODEL, D_IN), f32) * D_MODEL ** -0.5
    conv_w = jax.random.normal(ks[4], (DEPTH, CONV_K, CONV_W), f32) * CONV_K ** -0.5
    i_bias = 0.1 * jax.random.normal(ks[5], (DEPTH, 2, N_HEADS), f32)
    f_bias = jnp.linspace(3.0, 6.0, N_HEADS, dtype=f32)[None, None, :] + \
        0.1 * jax.random.normal(ks[6], (DEPTH, 2, N_HEADS), f32)
    gate_bias = jnp.stack([i_bias[:, 0], f_bias[:, 0], i_bias[:, 1], f_bias[:, 1]], axis=1)
    head_norm_g = 1.0 + 0.05 * jax.random.normal(ks[7], (DEPTH, V_W), f32)
    w_out = jax.random.normal(ks[8], (DEPTH, D_MIX, D_MODEL), f32) * D_MIX ** -0.5
    norm2_g = 1.0 + 0.05 * jax.random.normal(ks[9], (DEPTH, D_MODEL), f32)
    w_router = jax.random.normal(ks[10], (DEPTH, D_MODEL, N_EXPERTS), f32) * D_MODEL ** -0.5
    w_gate = jax.random.normal(ks[11], (DEPTH, N_EXPERTS, D_MODEL, EXPERT_FF), f32) * D_MODEL ** -0.5
    w_up = jax.random.normal(ks[12], (DEPTH, N_EXPERTS, D_MODEL, EXPERT_FF), f32) * D_MODEL ** -0.5
    w_down = jax.random.normal(ks[13], (DEPTH, N_EXPERTS, EXPERT_FF, D_MODEL), f32) * EXPERT_FF ** -0.5
    final_g = 1.0 + 0.05 * jax.random.normal(ks[14], (D_MODEL,), f32)
    return {"x_prompt": x_prompt, "x_sample": x_sample, "norm1_g": norm1_g, "w_in": w_in,
            "conv_w": conv_w, "gate_bias": gate_bias, "head_norm_g": head_norm_g, "w_out": w_out,
            "norm2_g": norm2_g, "w_router": w_router, "w_gate": w_gate, "w_up": w_up,
            "w_down": w_down, "final_g": final_g}

def reference(x_prompt, x_sample, norm1_g, w_in, conv_w, gate_bias, head_norm_g, w_out,
              norm2_g, w_router, w_gate, w_up, w_down, final_g):
    xp, xs = x_prompt, x_sample
    for l in range(DEPTH):
        xp = mixer_sublayer(xp, norm1_g[l], w_in[l], conv_w[l], gate_bias[l], head_norm_g[l], w_out[l])
        xs = mixer_sublayer(xs, norm1_g[l], w_in[l], conv_w[l], gate_bias[l], head_norm_g[l], w_out[l])
        xp = expert_choice_sublayer(xp, norm2_g[l], w_router[l], w_gate[l], w_up[l], w_down[l])
        xs = expert_choice_sublayer(xs, norm2_g[l], w_router[l], w_gate[l], w_up[l], w_down[l])
    y_prompt = rms_norm(xp, final_g)
    y_sample = rms_norm(xs, final_g)
    return (y_prompt, y_sample)


_drawn_inputs = setup_inputs


def setup_inputs(seed=0):
    import zlib

    import numpy as np

    out = dict(_drawn_inputs(seed))
    spreads = {}
    factors = {'head_norm_g': 2.889, 'norm2_g': 3.206}
    for name, (base, spread) in spreads.items():
        noise = np.random.default_rng([zlib.crc32(name.encode()), seed]).standard_normal(out[name].shape)
        drawn = base * np.exp(spread * noise) if base else spread * noise
        out[name] = __import__('jax').numpy.asarray(drawn.astype(out[name].dtype))
    for name, factor in factors.items():
        out[name] = (out[name] * factor).astype(out[name].dtype)
    return out
```

```python
from contextlib import ExitStack

import concourse.bass as bass
from concourse import mybir

ALU = mybir.AluOpType
ACT = mybir.ActivationFunctionType
AX_X = mybir.AxisListType.X
F32 = mybir.dt.float32
F32R = mybir.dt.float32r
BF16 = mybir.dt.bfloat16
U32 = mybir.dt.uint32

P = 128
NEG = -1.0e30


class Chain:

    def __init__(self, eng, sem):
        self.eng, self.sem, self.n = eng, sem, 0

    def __call__(self, ins):
        ins.then_inc(self.sem, 1)
        self.n += 1
        self.eng.wait_ge(self.sem, self.n)


def hybrid_conv_mlstm_moe(nc, x_prompt, x_sample, norm1_g, w_in, conv_w, gate_bias, head_norm_g, w_out,
                          norm2_g, w_router, w_gate, w_up, w_down, final_g, y_prompt, y_sample):
    D = x_prompt.shape[2]
    SP_, SS_ = x_prompt.shape[1], x_sample.shape[1]
    T = SP_ + SS_
    KD = D // P
    NT = T // P
    NTP = SP_ // P
    CW = conv_w.shape[2]
    H = gate_bias.shape[2]
    DV = (D // 2) // H
    DK = DV // 2
    QK = H * DK
    VW = H * DV
    NE = w_gate.shape[1]
    FF = w_gate.shape[3]
    KF = FF // P
    CAPP, CAPS = 2 * SP_ // NE, 2 * SS_ // NE
    NC = CAPP + CAPS
    EPS = 1e-6
    VA = DV + 1
    VPAD = DV + 2
    GATE_ROWS = 100
    ROWS = 36
    assert (D, DV, DK, H, CAPS) == (1024, 128, 64, 4, 128) and SP_ % 256 == 0 and SS_ % 512 == 0

    x_chunk = [x_prompt[0, t * P:(t + 1) * P, :] for t in range(NTP)] + \
              [x_sample[0, t * P:(t + 1) * P, :] for t in range(NT - NTP)]
    y_chunk = [y_prompt[0, t * P:(t + 1) * P, :] for t in range(NTP)] + \
              [y_sample[0, t * P:(t + 1) * P, :] for t in range(NT - NTP)]

    qk_d = nc.dram_tensor("qk_d", (4, P, T), F32).ap()
    v_d = nc.dram_tensor("v_d", (T, VW), F32).ap()
    o_d = nc.dram_tensor("o_d", (T, VW), F32).ap()
    conv_d = nc.dram_tensor("conv_d", (CW // P, P, T), F32).ap()
    negm_d = nc.dram_tensor("negm_d", (2 * H, T), F32).ap()
    inter_d = nc.dram_tensor("inter_d", (2 * H, T), F32).ap()
    decay_d = nc.dram_tensor("decay_d", (2 * H, NT), F32).ap()
    state_d = nc.dram_tensor("state_d", (NT, P, 2, 2 * VPAD), F32).ap()
    acc_d = nc.dram_tensor("acc_d", (T, D), F32).ap()
    tok_d = nc.dram_tensor("tok_d", (T, D), F32).ap()

    groups = [(0, SP_)] + [(SP_ + i * 512, 512) for i in range(SS_ // 512)]
    BATCHES = [(0, 2), (2, 6), (6, NT)]

    c_gb, c_gc, c_u = 0, CW, 2 * CW
    c_q, c_k, c_v = 3 * CW, 3 * CW + QK, 3 * CW + 2 * QK
    c_o = c_v + VW
    c_gates = c_o + VW
    CH = 256
    chunks = [("k", c_k, 0), ("q", c_q, 0)] + [("v", c_v + i * CH, i) for i in range(VW // CH)] + \
             [("o", c_o + i * CH, i) for i in range(VW // CH)]
    for i in range(CW // CH):
        chunks += [("gc", c_gc + i * CH, i), ("u", c_u + i * CH, i), ("gb", c_gb + i * CH, i)]
    NCH = len(chunks)
    pgroups = [(-1, "gate", 0, 0, t0, w) for t0, w in groups]
    for j, (kind, _, part) in enumerate(chunks):
        if kind in ("v", "o"):
            pgroups += [(j, kind, part, t, 0, CH) for t in range(NT)]
        else:
            pgroups += [(j, kind, part, m, t0, w) for m in range(2) for t0, w in groups]
    EV_DVE = ("u", "gb")
    ev_at, n_act, n_dve = [], 0, 0
    for g in pgroups:
        if g[1] in EV_DVE:
            n_dve += 1
            ev_at.append(("dve", n_dve))
        else:
            n_act += 1
            ev_at.append(("act", n_act))
    NST = 4
    staged = [i for i, g in enumerate(pgroups) if g[1] in ("k", "q", "v", "o", "gb")]
    stage_no = {i: s for s, i in enumerate(staged)}
    of_chunk = {j: [i for i, g in enumerate(pgroups) if g[0] == j] for j in range(-1, NCH)}

    out = ExitStack()
    with out:
        def sem(name):
            return out.enter_context(nc.semaphore(name))

        def keep(name, shape, dt=F32):
            return out.enter_context(nc.sbuf_tensor(name, shape, dt))

        psum = out.enter_context(nc.psum_tensor("psum", [P, 8, 512], F32))

        ident = keep("ident", [P, P])
        colS = keep("colS", [P, 36, 40])
        small = keep("small", [P, 64])
        zrow = keep("zrow", [ROWS, 1])
        aff = keep("aff", [P, NT, NE])
        logit_max = keep("logit_max", [P, NT, 4])
        AFF = keep("AFF", [48, SS_])
        GV = keep("GV", [48, P])
        GI = keep("GI", [48, P], U32)
        GIF = keep("GIF", [48, P])
        GC = keep("GC", [P, 48])
        IDX = keep("IDX", [P, 48], U32)

        def stage_buffers(specs, *inner):
            got = {}
            with ExitStack() as s:
                for n, shape, dt in specs:
                    got[n] = s.enter_context(nc.sbuf_tensor(n, shape, dt))
                for part in inner:
                    with ExitStack() as t:
                        for n, shape, dt in part:
                            got[n] = t.enter_context(nc.sbuf_tensor(n, shape, dt))
            return got

        b = stage_buffers([
            ("hn_hi", [P, KD, T], F32R), ("hn_lo", [P, KD, T], F32R),
            ("wraw", [P, 2, KD, CH], F32), ("whi", [P, 2, KD, CH], F32R), ("wlo", [P, 2, KD, CH], F32R),
            ("stage", [P, NST, 512], F32),
            ("graw", [P, KD, 4 * H], F32), ("gbias", [P, 1], F32), ("cw", [P, 3, CW // P], F32),
            ("wg_hi", [P, KD, P], F32R), ("wg_lo", [P, KD, P], F32R), ("mst", [ROWS, NT], F32),
            ("st1", [P, 3, NT], F32)],
            [("xa", [P, NT, D], F32), ("g1", [P, D], F32), ("sq1", [P, D], F32)],
            [("R", [ROWS, 5, T], F32), ("GA", [P, T], F32), ("LI", [ROWS, T], F32), ("LF", [ROWS, T], F32),
             ("MM", [ROWS, T], F32), ("TM", [P, T], F32)],
            [("gcS", [P, 2, T], F32), ("CU", [P, 2, T + 4], F32), ("CV", [P, 2, T], F32)])
        d = stage_buffers([
            ("woh", [P, KD, D], F32R), ("wol", [P, KD, D], F32R), ("woraw", [P, 2, D], F32),
            ("masks", [P, 2, P], F32), ("hgb", [P, VW], F32), ("g2b", [P, D], F32), ("wr", [P, KD, NE], F32),
            ("dcb", [P, 2, 2, NT], F32)],
            [("kT1", [P, 2, 2, 2, P], F32), ("v1", [P, 2, 2, H, VPAD], F32), ("wk", [P, 2, H, DK], F32),
             ("ST", [P, 2, 2, 2, VPAD], F32)],
            [("kTs", [P, 2, 2, P], F32), ("qz", [P, 2, H, P], F32), ("vs", [P, 2, H, VPAD], F32),
             ("og", [P, 2, VW], F32), ("negm", [P, 2, 2 * H, P], F32), ("inter", [P, 2, 4, P], F32),
             ("sts", [P, 2, 2, 2, VPAD], F32), ("cvs", [P, 2, CW // P, P], F32), ("xs", [P, 2, D], F32),
             ("X", [P, 2 * H, P], F32), ("E", [P, 2 * H, P], F32), ("SD", [P, 2 * H, P], F32),
             ("qs", [P, 2 * H, P], F32), ("hb", [P, H, DV], F32), ("ht", [P, H, DV], F32), ("junk", [P, D], F32), ("junkh", [P, H, DV], F32),
             ("mix", [P, H, DV], F32), ("mxh", [P, 2, KD, P], F32R), ("mxl", [P, 2, KD, P], F32R),
             ("x1", [P, 2, D], F32), ("tk", [P, 2, D], F32), ("tkT", [P, KD, P], F32), ("sm", [P, 2, 16], F32), ("ms", [P, 2, 3, H], F32),
             ("mt", [P, 2, 3, 1], F32)])
        f = stage_buffers([
            ("eraw", [P, 6, KD, CH], F32), ("ehi", [P, 6, KD, CH], F32R), ("elo", [P, 6, KD, CH], BF16),
            ("xg", [P, D], F32), ("xgp", [CAPP, D], F32),
            ("xc", [P, 2, KD, 2, NC], F32R), ("xb", [P, 2, KD, NC], BF16),
            ("gu", [P, 2, 2, 2, NC], F32), ("sg", [P, 2, NC], F32), ("hid", [P, 2, NC], F32),
            ("hc", [P, KF, 2, NC], F32R), ("hbf", [P, KF, NC], BF16),
            ("ys", [P, 2, NC], F32), ("yt", [P, D], F32), ("yp", [CAPP, D], F32),
            ("idx", [P, 2, 2], U32), ("gcol", [P, 2], F32)])
        z = stage_buffers([("fx", [P, NT, D], F32), ("fq", [P, D], F32), ("gf", [P, D], F32),
                           ("fs", [P, 4, NT], F32)])

        S = {n: sem("s_" + n) for n in (
            "bar act_ch dve_ch pool_ch "
            "x_in0 x_in1 x_in2 g1_in const zeroed small_in sumsq xn_done xT_ps hn_hi hn_lo "
            "w_in0 w_in1 wg_hi wg_lo w_hi w_lo proj ev_act ev_dve st0 st1 st2 st3 "
            "soft rows_t rows_exp rows_nat rows_out colT_ps "
            "cst_in wo_in0 wo_in1 wo_hi wo_lo l1_0 l1_1 kT_ps wk_done u_ps st_upd st_out0 st_out1 "
            "ld0 ld1 ld_mix0 ld_mix1 ld_x0 ld_x1 padded qs_done s_ps x_done e_done sd_done num_ps den_done hb_done ht_done hsum og_done "
            "mix_done mixT_ps mxh_done mxl_done o_ps x1_done x1_out0 x1_out1 sum2 tk_done tk_out0 tk_out1 tkT_ps tkT_done "
            "lg_ps lgmax exps aff_done affT_ps AFF_done topk selT_ps sel_done "
            "er0 er1 er2 er3 er4 er5 ehi elo_dve elo_pool idx_cp gath exT_ps xc_hi xc_lo xb_done "
            "gu_ps gu_add sg_done hid_done hc_hi hc_lo hb_bf dn_ps ys_done yT_ps y_done scat settled "
            "gf_in f_in0 f_in1 f_in2 f_in3 f_in4 f_sum f_y f_out").split()}
        x_in = (S["x_in0"], S["x_in1"], S["x_in2"])
        w_ind, stg, l1, ld = (S["w_in0"], S["w_in1"]), (S["st0"], S["st1"], S["st2"], S["st3"]), (S["l1_0"], S["l1_1"]), (S["ld0"], S["ld1"])
        ld_mix, ld_x = (S["ld_mix0"], S["ld_mix1"]), (S["ld_x0"], S["ld_x1"])
        wo_in, st_out = (S["wo_in0"], S["wo_in1"]), (S["st_out0"], S["st_out1"])
        x1_out, tk_out = (S["x1_out0"], S["x1_out1"]), (S["tk_out0"], S["tk_out1"])
        er = (S["er0"], S["er1"], S["er2"], S["er3"], S["er4"], S["er5"])
        f_in = (S["f_in0"], S["f_in1"], S["f_in2"], S["f_in3"], S["f_in4"])

        def barrier(eng, k):
            eng.drain().then_inc(S["bar"], 1)
            eng.wait_ge(S["bar"], 5 * k)

        def rows_of(row):
            return row.partition_broadcast(P).rearrange("p a n -> p (a n)")

        seqs = [(0, NTP), (NTP, NT)]
        fwd = list(range(NT))
        bwd = [c for lo, hi in seqs for c in range(hi - 1, lo - 1, -1)]
        starts = [lo for lo, _ in seqs]

        def natural(ap2, lo, hi):
            return ap2[:, lo * P:hi * P]

        def reverse(ap2, lo, hi):
            return ap2[:, hi * P - 1:lo * P - 1:-1] if lo else ap2[:, hi * P - 1::-1]

        U_OFF = {0: 1, 1: 3}

        TG = ((0, 3), (3, 3), (6, 2))
        NLD = 8

        def colslot(c, q):
            return 3 * c + q

        NB = 12
        RING = 6
        BY_POOL = [3, 7, 11]
        BY_DVE = [j for j in range(NB) if j not in BY_POOL]

        def wait_split(eng, e, j):
            mine, s = (BY_POOL, S["elo_pool"]) if j in BY_POOL else (BY_DVE, S["elo_dve"])
            eng.wait_ge(s, len(mine) * (e + 1) + mine.index(j) + 1)

        def wait_slot(eng, e, j):
            before = (j + RING) % NB
            mine, s = (BY_POOL, S["elo_pool"]) if before in BY_POOL else (BY_DVE, S["elo_dve"])
            eng.wait_ge(s, len(mine) * (e if j < RING else e + 1) + mine.index(before) + 1)

        block = out.enter_context(nc.Block())

        @block.sync
        def _(sp):
            for i, (lo, hi) in enumerate(BATCHES):
                for n in range(lo, hi):
                    sp.dma_start(b["xa"][:, n, :], x_chunk[n]).then_inc(x_in[i], 16)
                if i == 0:
                    sp.dma_start(b["g1"][:, :], rows_of(norm1_g)).then_inc(S["g1_in"], 16)
                    sp.wait_ge(S["zeroed"], 1)
                    with nc.allow_non_contiguous_dma(reason="gate columns, biases and taps"):
                        sp.dma_start(b["graw"][:, :, :], w_in[0, :, c_gates:c_gates + 4 * H]
                                     .rearrange("(k p) n -> p k n", p=P)).then_inc(S["small_in"], 16)
                        for row, g in ((0, 0), (32, 2), (64, 1), (96, 3)):
                            sp.dma_start(b["gbias"][row:row + H, 0:1], gate_bias[0, g, :]
                                         .rearrange("(h a) -> h a", a=1)).then_inc(S["small_in"], 16)
                        for k in range(3):
                            sp.dma_start(b["cw"][:, k, :], conv_w[0, k, :].rearrange("(c p) -> p c", p=P)
                                         ).then_inc(S["small_in"], 16)
            for j, (_, col, _) in enumerate(chunks):
                if j >= 2:
                    sp.wait_ge(S["w_lo"], j - 1)
                sp.dma_start(b["wraw"][:, j % 2, :, :], w_in[0, :, col:col + CH].rearrange("(k p) n -> p k n", p=P)
                             ).then_inc(w_ind[j % 2], 16)
            barrier(sp, 1)

            with nc.allow_non_contiguous_dma(reason="router columns"):
                sp.dma_start(d["wr"][:, :, :], w_router[0].rearrange("(k p) n -> p k n", p=P)).then_inc(S["cst_in"], 16)
                for half in range(2):
                    for dr in range(2):
                        for pr in range(2):
                            r = 4 * dr + 2 * pr + half
                            sp.dma_start(d["dcb"][64 * half:64 * half + 64, dr, pr, :],
                                         decay_d[r:r + 1, :].partition_broadcast(64).rearrange("p a n -> p (a n)")
                                         ).then_inc(S["cst_in"], 16)
            sp.dma_start(d["hgb"][:, :], rows_of(head_norm_g)).then_inc(S["cst_in"], 16)
            sp.dma_start(d["g2b"][:, :], rows_of(norm2_g)).then_inc(S["cst_in"], 16)
            for i in range(NT):
                if i >= 2:
                    sp.wait_ge(S["u_ps"], i - 1)
                for dr, c in ((0, fwd[i]), (1, bwd[i])):
                    t = slice(c * P, (c + 1) * P)
                    sp.dma_start(d["kT1"][:, i % 2, dr, :, :], qk_d[2:4, :, t].rearrange("r p t -> p r t")
                                 ).then_inc(l1[i % 2], 16)
                    sp.dma_start(d["v1"][:, i % 2, dr, :, 0:DV], v_d[t, :].rearrange("t (h n) -> t h n", h=H)
                                 ).then_inc(l1[i % 2], 16)
                if i < KD:
                    if i >= 2:
                        sp.wait_ge(S["wo_lo"], i - 1)
                    sp.dma_start(d["woraw"][:, i % 2, :], w_out[0, i * P:(i + 1) * P, :]).then_inc(wo_in[i % 2], 16)
            barrier(sp, 2)

            def load_scan(n):
                s, t = n % 2, slice(n * P, (n + 1) * P)
                if n >= 2:
                    sp.wait_ge(S["num_ps"], n - 1)
                sp.dma_start(d["kTs"][:, s, :, :], qk_d[2:4, :, t].rearrange("r p t -> p r t")).then_inc(ld[s], 16)
                for half in range(2):
                    rows = slice(64 * half, 64 * half + 64)
                    sp.dma_start(d["qz"][rows, s, half::2, :], qk_d[0:2, rows, t].rearrange("r p t -> p r t")
                                 ).then_inc(ld[s], 16)
                    sp.dma_start(d["inter"][rows, s, :, :], inter_d.rearrange("(r a) t -> a r t", a=2)[half, :, t]
                                 .partition_broadcast(64)).then_inc(ld[s], 16)
                sp.dma_start(d["negm"][:, s, :, :], negm_d[:, t].partition_broadcast(P)).then_inc(ld[s], 16)
                sp.dma_start(d["vs"][:, s, :, 0:DV], v_d[t, :].rearrange("t (h n) -> t h n", h=H)).then_inc(ld[s], 16)
                sp.dma_start(d["sts"][:, s, :, :, :], state_d[n]).then_inc(ld[s], 16)

            def load_mix(n):
                s, t = n % 2, slice(n * P, (n + 1) * P)
                if n >= 2:
                    sp.wait_ge(S["mxl_done"], n - 1)
                sp.dma_start(d["og"][:, s, :], o_d[t, :]).then_inc(ld_mix[s], 16)
                sp.dma_start(d["cvs"][:, s, :, :], conv_d[:, :, t].rearrange("r p t -> p r t")).then_inc(ld_mix[s], 16)

            def load_x(n):
                if n >= 2:
                    sp.wait_ge(S["x1_done"], 2 * (n - 1))
                sp.dma_start(d["xs"][:, n % 2, :], x_chunk[n]).then_inc(ld_x[n % 2], 16)

            sp.wait_ge(S["padded"], 1)
            for n in range(NT + 1):
                if n < NT:
                    load_scan(n)
                if n >= 1:
                    load_x(n - 1)
                if n < NT:
                    load_mix(n)
            barrier(sp, 3)

            with sp.Fori(0, NE) as e:
                for j in range(NB):
                    wait_slot(sp, e, j)
                    w = (w_gate, w_up)[j % 2] if j < 8 else w_down
                    i = j // 2 if j < 8 else j - 8
                    src = w[0, bass.ds(e, 1), :, i * CH:(i + 1) * CH].rearrange("a (k p) n -> p (a k) n", p=P)
                    sp.dma_start(f["eraw"][:, j % RING, :, :], src).then_inc(er[j % RING], 16)
            barrier(sp, 4)
            sp.dma_start(z["gf"][:, :], rows_of(final_g.rearrange("(a d) -> a d", a=1))).then_inc(S["gf_in"], 16)
            for n in range(NT):
                sp.dma_start(z["fx"][:, n, :], acc_d[n * P:(n + 1) * P, :]).then_inc(f_in[n // 2], 16)
            for n in range(NT):
                sp.wait_ge(S["f_y"], n + 1)
                sp.dma_start(y_chunk[n], z["fx"][:, n, :]).then_inc(S["f_out"], 16)
            sp.wait_ge(S["f_out"], 16 * NT)

        @block.gpsimd
        def _(pool):
            ch = Chain(pool, S["pool_ch"])
            ch(pool.memset(ident[:, :], 0.0))
            pool.affine_select(out=ident[:, :], in_=ident[:, :], compare_op=ALU.not_equal, fill=1.0, base=0,
                               pattern=[[-1, P]], channel_multiplier=1).then_inc(S["const"], 1)
            pool.memset(b["gbias"][:, :], 0.0).then_inc(S["zeroed"], 1)
            ch(pool.memset(zrow[:, :], 0.0))
            pool.memset(b["wg_hi"][:, :, :].bitcast(F32), 0.0).then_inc(S["zeroed"], 1)
            pool.memset(b["wg_lo"][:, :, :].bitcast(F32), 0.0).then_inc(S["zeroed"], 1)
            pool.wait_ge(S["hn_lo"], NT)
            pool.memset(b["R"][:, :, :], 0.0).then_inc(S["zeroed"], 1)
            pool.memset(b["LF"][:, :], 0.0).then_inc(S["zeroed"], 1)
            pool.memset(b["LI"][:, :], 0.0).then_inc(S["zeroed"], 1)

            for i in staged:
                _, kind, part, m, t0, w = pgroups[i]
                s = stage_no[i] % NST
                who, n = ev_at[i]
                pool.wait_ge(S["ev_act"] if who == "act" else S["ev_dve"], n)
                if kind in ("k", "q"):
                    dst = qk_d[(2 if kind == "k" else 0) + m, :, t0:t0 + w]
                elif kind in ("v", "o"):
                    dst = (v_d if kind == "v" else o_d)[m * P:(m + 1) * P, part * CH:(part + 1) * CH]
                else:
                    dst = conv_d[2 * part + m, :, t0:t0 + w]
                pool.dma_start(dst, b["stage"][:, s, 0:w]).then_inc(stg[s], 16)
                if i == of_chunk[1][-1]:
                    pool.wait_ge(S["rows_nat"], 1)
                    pool.wait_ge(S["rows_exp"], 9)
                    with nc.allow_non_contiguous_dma(reason="one decay a chunk"):
                        for dr in range(2):
                            rows, dst = slice(32 * dr, 32 * dr + H), slice(4 * dr, 4 * dr + 4)
                            pool.dma_start(negm_d[dst, :], b["R"][rows, 4, :]).then_inc(S["rows_out"], 16)
                            pool.dma_start(inter_d[dst, :], b["R"][rows, 3, :]).then_inc(S["rows_out"], 16)
                            last = (P - 1, 0)[dr]
                            pool.dma_start(decay_d[dst, :], b["R"][rows, 3, last::P][:, 0:NT]).then_inc(S["rows_out"], 16)
            for s in range(NST):
                pool.wait_ge(stg[s], 16 * len([i for i in staged if stage_no[i] % NST == s]))
            barrier(pool, 1)

            ch(pool.memset(d["masks"][:, :, :], 0.0))
            ch(pool.affine_select(out=d["masks"][:, 0, :], in_=d["masks"][:, 0, :], compare_op=ALU.is_ge, fill=NEG,
                                  base=0, pattern=[[1, P]], channel_multiplier=-1))
            ch(pool.affine_select(out=d["masks"][:, 1, :], in_=d["masks"][:, 1, :], compare_op=ALU.is_ge, fill=NEG,
                                  base=0, pattern=[[-1, P]], channel_multiplier=1))
            for i in range(NT):
                pool.wait_ge(S["st_upd"], i + 1)
                for dr, c in ((0, fwd[i]), (1, bwd[i])):
                    pool.dma_start(state_d[c, :, dr, :], d["ST"][:, i % 2, dr, :, :].rearrange("p a n -> p (a n)")
                                   ).then_inc(st_out[i % 2], 16)
            for s in range(2):
                pool.wait_ge(st_out[s], 32 * (NT // 2))
            barrier(pool, 2)
            pool.memset(d["qz"][:, :, :, :], 0.0).then_inc(S["padded"], 1)

            def scale_queries(n):
                s = n % 2
                pool.wait_ge(ld[s], 16 * NLD * (n // 2 + 1))
                if n >= 1:
                    pool.wait_ge(S["num_ps"], n)
                for dr in range(2):
                    for half in range(2):
                        q = pool.tensor_tensor(d["qs"][:, H * dr + half:H * dr + H:2, :], d["qz"][:, s, half::2, :],
                                               d["inter"][:, s, 2 * dr:2 * dr + 2, :], ALU.mult)
                q.then_inc(S["qs_done"], 1)
                pool.wait_ge(ld_mix[s], 16 * 2 * (n // 2 + 1))
                pool.tensor_tensor(d["og"][:, s, :], d["og"][:, s, :], d["hgb"][:, :], ALU.mult
                                   ).then_inc(S["og_done"], 1)

            scale_queries(0)
            for n in range(NT + 1):
                if n + 1 < NT:
                    scale_queries(n + 1)
                if n >= 1:
                    m = n - 1
                    t = slice(m * P, (m + 1) * P)
                    pool.wait_ge(S["x1_done"], 2 * (m + 1))
                    pool.dma_start(acc_d[t, :], d["x1"][:, m % 2, :]).then_inc(x1_out[m % 2], 16)
                    pool.wait_ge(S["tk_done"], m + 1)
                    pool.dma_start(tok_d[t, :], d["tk"][:, m % 2, :]).then_inc(tk_out[m % 2], 16)
            for s in range(2):
                pool.wait_ge(x1_out[s], 16 * (NT // 2))
                pool.wait_ge(tk_out[s], 16 * (NT // 2))
            barrier(pool, 3)

            for s, credit in ((S["dn_ps"], 8), (S["gu_add"], 2), (S["ys_done"], 2), (S["yT_ps"], 2), (S["hid_done"], 1), (S["hb_bf"], 1), (S["y_done"], 2),
                              (S["elo_dve"], len(BY_DVE)), (S["elo_pool"], len(BY_POOL))):
                pool.sem_inc(s, credit)

            def settle():
                pool.sem_inc(S["settled"], 1)

            def gather(e, copied):
                pool.tensor_copy(f["idx"][:, 0, 0:1], IDX[:, bass.ds(e, 1)]).then_inc(S["idx_cp"], 1)
                pool.tensor_copy(f["idx"][0:CAPP, 1, 0:1], IDX[0:CAPP, bass.ds(e + 32, 1)]).then_inc(S["idx_cp"], 1)
                pool.wait_ge(S["idx_cp"], copied + 2)
                settle()
                pool.indirect_dma_start(f["xg"][:, :], None, tok_d, bass.IndirectOffsetOnAxis(ap=f["idx"][:, 0, 0:1], axis=0)
                                        ).then_inc(S["gath"], 16)
                pool.indirect_dma_start(f["xgp"][:, :], None, tok_d,
                                        bass.IndirectOffsetOnAxis(ap=f["idx"][0:CAPP, 1, 0:1], axis=0)
                                        ).then_inc(S["gath"], 16)

            def split_low(e, j):
                pool.wait_ge(S["ehi"], NB * e + j + 1)
                pool.tensor_tensor(f["elo"][:, j % RING, :, :], f["eraw"][:, j % RING, :, :],
                                   f["ehi"][:, j % RING, :, :].bitcast(F32),
                                   ALU.subtract).then_inc(S["elo_pool"], 1)

            def scatter(e):
                pool.wait_ge(S["y_done"], 2 + 2 * e + 2)
                settle()
                pool.indirect_dma_start(acc_d, bass.IndirectOffsetOnAxis(ap=f["idx"][:, 0, 1:2], axis=0),
                                        f["yt"][:, :], None, compute_op=ALU.add).then_inc(S["scat"], 16)
                pool.indirect_dma_start(acc_d, bass.IndirectOffsetOnAxis(ap=f["idx"][0:CAPP, 1, 1:2], axis=0),
                                        f["yp"][:, :], None, compute_op=ALU.add).then_inc(S["scat"], 16)

            gather(0, 0)
            split_low(0, 3)

            def expert(e, s, first=False, last=False):
                if not last:
                    pool.wait_ge(S["exT_ps"], 3 * e + 3)
                    settle()
                    gather(e + 1, 2 + 6 * e)
                if not first:
                    scatter(e - 1)
                for p in range(4):
                    pool.wait_ge(S["sg_done"], 4 * e + p + 1)
                    pool.wait_ge(S["hc_lo"], 4 + 4 * e + p)
                    pool.wait_ge(S["hb_bf"], 1 + 4 * e + p)
                    pool.tensor_tensor(f["hid"][:, :, :], f["sg"][:, :, :], f["gu"][:, p % 2, :, 1, :], ALU.mult
                                       ).then_inc(S["hid_done"], 1)
                    if p == 1:
                        split_low(e, 7)
                split_low(e, 11)
                pool.wait_ge(S["y_done"], 2 * e + 2)
                if not first:
                    pool.wait_ge(S["scat"], 32 * e)
                settle()
                pool.tensor_copy(f["idx"][:, 0, 1:2], IDX[:, bass.ds(e, 1)]).then_inc(S["idx_cp"], 1)
                pool.tensor_copy(f["idx"][0:CAPP, 1, 1:2], IDX[0:CAPP, bass.ds(e + 32, 1)]).then_inc(S["idx_cp"], 1)
                pool.tensor_copy(f["gcol"][:, 0:1], GC[:, bass.ds(e, 1)]).then_inc(S["idx_cp"], 1)
                pool.tensor_copy(f["gcol"][0:CAPP, 1:2], GC[0:CAPP, bass.ds(e + 32, 1)]).then_inc(S["idx_cp"], 1)
                pool.wait_ge(S["idx_cp"], 2 + 6 * e + (4 if last else 6))
                if not last:
                    split_low(e + 1, 3)

            expert(0, 0, first=True)
            with pool.Fori(0, NE // 2 - 1) as g:
                expert(2 * g + 1, 1)
                expert(2 * g + 2, 0)
            expert(NE - 1, 1, last=True)
            scatter(NE - 1)
            pool.wait_ge(S["scat"], 32 * NE)
            barrier(pool, 4)

        @block.scalar
        def _(act):
            ch = Chain(act, S["act_ch"])

            for i, (lo, hi) in enumerate(BATCHES):
                act.wait_ge(x_in[i], 16 * (hi - lo))
                for n in range(lo, hi):
                    if n >= 1:
                        act.wait_ge(S["sumsq"], n)
                    act.activation(b["sq1"][:, :], b["xa"][:, n, :], ACT.Square, scale=D ** -0.5,
                                   accum_out=b["st1"][:, 0, n:n + 1]).then_inc(S["sumsq"], 1)
            for n in range(NT):
                act.wait_ge(S["xT_ps"], n + 1)
                act.activation(b["hn_hi"][:, :, n * P:(n + 1) * P], psum[:, 2 * (n % 2):2 * (n % 2) + 2, :]
                               .rearrange("p a (k t) -> p (a k) t", k=4), ACT.Copy).then_inc(S["hn_hi"], 1)

            act.wait_ge(S["small_in"], 16 * 8)
            act.wait_ge(S["zeroed"], 3)
            for row, g in ((0, 0), (32, 2), (64, 1), (96, 3)):
                i = act.activation(b["wg_hi"][:, :, row:row + H], b["graw"][:, :, g * H:(g + 1) * H], ACT.Copy)
            i.then_inc(S["wg_hi"], 1)

            def split_high(j):
                act.wait_ge(w_ind[j % 2], 16 * (j // 2 + 1))
                if j >= 2:
                    act.wait_ge(S["proj"], of_chunk[j - 2][-1] + 1)
                act.activation(b["whi"][:, j % 2, :, :], b["wraw"][:, j % 2, :, :], ACT.Copy).then_inc(S["w_hi"], 1)

            split_high(0)
            done = 0
            for j in range(-1, NCH):
                if 0 <= j < NCH - 1:
                    split_high(j + 1)
                for i in of_chunk[j]:
                    _, kind, part, m, t0, w = pgroups[i]
                    if kind in EV_DVE:
                        continue
                    act.wait_ge(S["proj"], i + 1)
                    src = psum[:, 4 + i % 4, 0:w]
                    if kind in ("k", "q", "v", "o"):
                        s = stage_no[i]
                        if s >= NST:
                            act.wait_ge(stg[s % NST], 16 * (s // NST))
                        dst = b["stage"][:, s % NST, 0:w]
                    if kind == "gate":
                        if i == 0:
                            act.wait_ge(S["hn_lo"], NT)
                        e = act.activation(b["GA"][0:GATE_ROWS, t0:t0 + w], psum[0:GATE_ROWS, 4 + i % 4, 0:w],
                                           ACT.Identity, bias=b["gbias"][0:GATE_ROWS, 0:1])
                    elif kind == "q":
                        e = act.activation(dst, src, ACT.Copy, scale=DK ** -0.5)
                    elif kind == "o":
                        e = act.activation(dst, src, ACT.Sigmoid)
                    elif kind == "gc":
                        if part == 0 and m == 0 and t0 == 0:
                            act.wait_ge(S["colT_ps"], 3)
                            act.wait_ge(S["rows_out"], 16 * 6)
                        if part > 0:
                            act.wait_ge(S["ev_dve"], ev_at[of_chunk[j - 2][-1]][1])
                        e = act.activation(b["gcS"][:, m, t0:t0 + w], src, ACT.Copy)
                    else:
                        e = act.activation(dst, src, ACT.Copy)
                    e.then_inc(S["ev_act"], 1)
                    done += 1
                if j == -1:
                    act.wait_ge(S["ev_act"], 3)
                    r = slice(64, GATE_ROWS)
                    ch(act.activation(b["TM"][r, :], b["GA"][r, :], ACT.Abs))
                    ch(act.activation(b["TM"][r, :], b["TM"][r, :], ACT.Exp, scale=-1.0))
                    act.activation(b["TM"][r, :], b["TM"][r, :], ACT.Ln, bias=1.0).then_inc(S["soft"], 1)
                if j == 0:
                    act.wait_ge(S["zeroed"], 4)
                    for k, (q, src, scale) in enumerate(((1, b["GA"], 1.0), (3, b["LI"], 1.0), (2, b["LF"], -1.0))):
                        act.wait_ge(S["rows_t"], k + 1)
                        act.activation(b["R"][0:H, q, :], src[0:H, :], ACT.Exp, scale=scale).then_inc(S["rows_exp"], 1)
                        for lo, hi in seqs:
                            act.activation(reverse(b["R"][32:32 + H, q, :], lo, hi), natural(src[32:32 + H, :], lo, hi),
                                           ACT.Exp, scale=scale).then_inc(S["rows_exp"], 1)
                if j == 1:
                    for k in range(3):
                        act.wait_ge(S["colT_ps"], k + 1)
                        n = min(12, 3 * NT - 12 * k)
                        act.activation(colS[:, 12 * k:12 * k + n, 0:ROWS],
                                       psum[:, k, 0:480].rearrange("p (a c) -> p a c", c=40)[:, 0:n, 0:ROWS], ACT.Copy)
            barrier(act, 1)

            for k in range(KD):
                act.wait_ge(wo_in[k % 2], 16 * (k // 2 + 1))
                act.activation(d["woh"][:, k, :], d["woraw"][:, k % 2, :], ACT.Copy).then_inc(S["wo_hi"], 1)
            barrier(act, 2)

            def exponentials(n):
                act.wait_ge(S["x_done"], n + 1)
                if n >= 1:
                    act.wait_ge(S["sd_done"], n)
                act.activation(d["E"][:, :, :], d["X"][:, :, :], ACT.Exp).then_inc(S["e_done"], 1)

            exponentials(0)
            for n in range(NT + 2):
                if n < NT:
                    act.wait_ge(S["den_done"], n + 1)
                    if n >= 1:
                        act.wait_ge(S["ht_done"], n)
                    for h in range(H):
                        i = act.activation(d["hb"][:, h, :], psum[:, 3 + h // 2, VPAD * (h % 2):VPAD * (h % 2) + DV],
                                           ACT.Copy, scale=d["sm"][:, n % 2, 4 + h:5 + h])
                    i.then_inc(S["hb_done"], 1)
                    if n + 1 < NT:
                        exponentials(n + 1)
                    act.wait_ge(S["ht_done"], n + 1)
                    if n >= 1:
                        act.wait_ge(S["hsum"], n)
                    for h in range(H):
                        i = act.activation(d["junkh"][:, h, :], d["ht"][:, h, :], ACT.Square, scale=DV ** -0.5,
                                           accum_out=d["ms"][:, n % 2, 0, h:h + 1])
                    i.then_inc(S["hsum"], 1)
                    act.wait_ge(ld_mix[n % 2], 16 * 2 * (n // 2 + 1))
                    if n >= 2:
                        act.wait_ge(S["o_ps"], 2 * (n - 1))
                    act.activation(d["mxh"][:, n % 2, 0:4, :], d["cvs"][:, n % 2, :, :], ACT.Copy
                                   ).then_inc(S["mxh_done"], 1)
                if n >= 2:
                    act.wait_ge(S["tkT_ps"], n - 1)
                    if n >= 3:
                        act.wait_ge(S["lg_ps"], n - 2)
                    act.activation(d["tkT"][:, :, :], psum[:, 1:3, :].rearrange("p a (k t) -> p (a k) t", k=4),
                                   ACT.Copy).then_inc(S["tkT_done"], 1)
                if 1 <= n <= NT:
                    m = n - 1
                    act.wait_ge(S["x1_done"], 2 * (m + 1))
                    if m >= 1:
                        act.wait_ge(S["sum2"], m)
                    act.activation(d["junk"][:, :], d["x1"][:, m % 2, :], ACT.Square, scale=D ** -0.5,
                                   accum_out=d["mt"][:, m % 2, 0, :]).then_inc(S["sum2"], 1)
                if n < NT:
                    act.wait_ge(S["mixT_ps"], n + 1)
                    act.activation(d["mxh"][:, n % 2, 4:8, :], psum[:, 5, :].rearrange("p (k t) -> p k t", k=4),
                                   ACT.Copy).then_inc(S["mxh_done"], 1)
                if n >= 2:
                    m = n - 2
                    act.wait_ge(S["lgmax"], m + 1)
                    act.activation(aff[:, m, :], psum[:, 3, 0:NE], ACT.Exp, bias=logit_max[:, m, 0:1],
                                   accum_out=logit_max[:, m, 1:2]).then_inc(S["exps"], 1)
            barrier(act, 3)

            def high(e, j, first=False):
                act.wait_ge(er[j % RING], 16 * (2 * e + j // RING + 1))
                if not first:
                    if j < 2:
                        act.wait_ge(S["gu_ps"], 8 * e)
                    elif j < RING:
                        act.wait_ge(S["dn_ps"], 8 * e + 2 * (j - 2) + 2)
                    else:
                        act.wait_ge(S["gu_ps"], 8 * e + 2 * ((j - RING) // 2) + 2)
                act.activation(f["ehi"][:, j % RING, :, :], f["eraw"][:, j % RING, :, :], ACT.Copy
                               ).then_inc(S["ehi"], 1)

            def narrow_tokens(e, s):
                act.wait_ge(S["xc_hi"], 3 * e + 3)
                act.activation(f["xb"][:, s, :, :], f["xc"][:, s, :, 0, :].bitcast(F32), ACT.Copy
                               ).then_inc(S["xb_done"], 1)

            def tokens_high(e, s, which):
                for g in which:
                    k0, nk = TG[g]
                    act.wait_ge(S["exT_ps"], 3 * e + g + 1)
                    act.activation(f["xc"][:, s, k0:k0 + nk, 0, :], psum[:, 6 + g % 2, 0:nk * NC]
                                   .rearrange("p (k t) -> p k t", k=nk), ACT.Copy).then_inc(S["xc_hi"], 1)

            def y_half(e, h, first=False, last=False):
                act.wait_ge(S["yT_ps"], 2 + 8 * e + 4 * h + 4)
                act.wait_ge(S["idx_cp"], 2 + 6 * e + (4 if last else 6))
                if not first:
                    act.wait_ge(S["scat"], 32 * e)
                act.activation(f["yt"][:, 512 * h:512 * h + 512], psum[:, 6, :], ACT.Copy, scale=f["gcol"][:, 0:1])
                act.activation(f["yp"][:, 512 * h:512 * h + 512], psum[0:CAPP, 7, :], ACT.Copy,
                               scale=f["gcol"][0:CAPP, 1:2]).then_inc(S["y_done"], 1)

            tokens_high(0, 0, (0, 1, 2))
            narrow_tokens(0, 0)
            for j in range(RING):
                high(0, j, True)

            def expert(e, s, first=False, last=False):
                if not first:
                    y_half(e - 1, 1)
                for p in range(4):
                    act.wait_ge(S["gu_add"], 2 + 8 * e + 2 * p + 2)
                    act.wait_ge(S["hid_done"], 1 + 4 * e + p)
                    act.activation(f["sg"][:, :, :], f["gu"][:, p % 2, :, 0, :], ACT.Silu).then_inc(S["sg_done"], 1)
                    if p < 3:
                        high(e, 2 * p + 6)
                    if p in (1, 2) and not last:
                        tokens_high(e + 1, 1 - s, ((0, 1), (2,))[p - 1])
                    act.wait_ge(S["hid_done"], 1 + 4 * e + p + 1)
                    if p == 0:
                        act.wait_ge(S["dn_ps"], 8 * e + 8)
                    act.activation(f["hc"][:, 2 * p:2 * p + 2, 0, :], f["hid"][:, :, :], ACT.Copy
                                   ).then_inc(S["hc_hi"], 1)
                    act.activation(f["hbf"][:, 2 * p:2 * p + 2, :], f["hid"][:, :, :], ACT.Copy
                                   ).then_inc(S["hb_bf"], 1)
                    if p < 3:
                        high(e, 2 * p + 7)
                    elif not last:
                        high(e + 1, 0)
                        high(e + 1, 1)
                    if p == 2 and not last:
                        narrow_tokens(e + 1, 1 - s)
                for q in range(4):
                    if not last:
                        high(e + 1, q + 2)
                    if q == 1:
                        y_half(e, 0, first, last)

            expert(0, 0, first=True)
            with act.Fori(0, NE // 2 - 1) as g:
                expert(2 * g + 1, 1)
                expert(2 * g + 2, 0)
            expert(NE - 1, 1, last=True)
            y_half(NE - 1, 1, last=True)
            barrier(act, 4)

            for n in range(NT):
                act.wait_ge(f_in[n // 2], 16 * 2)
                if n >= 1:
                    act.wait_ge(S["f_sum"], n)
                act.activation(z["fq"][:, :], z["fx"][:, n, :], ACT.Square, scale=D ** -0.5,
                               accum_out=z["fs"][:, 0, n:n + 1]).then_inc(S["f_sum"], 1)

        @block.vector
        def _(dve):
            ch = Chain(dve, S["dve_ch"])

            def inverse_root(r, v, t):
                ch(dve.tensor_scalar(v, v, EPS, None, ALU.add))
                ch(dve.tensor_scalar(r.bitcast(U32), v.bitcast(U32), -0.5, float(0x5f3759df), ALU.mult, ALU.add))
                c = 1.0
                for _ in range(3):
                    ch(dve.tensor_tensor(t, r, r, ALU.mult))
                    ch(dve.tensor_tensor(t, t, v, ALU.mult))
                    ch(dve.scalar_tensor_tensor(r, t, -3.0 * c * c, r, ALU.add, ALU.mult))
                    c = -2.0 * c ** 3
                ch(dve.tensor_scalar(r, r, 1.0 / c, None, ALU.mult))

            for i, (lo, hi) in enumerate(BATCHES):
                dve.wait_ge(S["sumsq"], hi)
                inverse_root(b["st1"][:, 1, lo:hi], b["st1"][:, 0, lo:hi], b["st1"][:, 2, lo:hi])
                dve.wait_ge(S["g1_in"], 16)
                for n in range(lo, hi):
                    dve.scalar_tensor_tensor(b["xa"][:, n, :], b["xa"][:, n, :], b["st1"][:, 1, n:n + 1], b["g1"][:, :],
                                             ALU.mult, ALU.mult).then_inc(S["xn_done"], 1)
            for n in range(NT):
                dve.wait_ge(S["hn_hi"], n + 1)
                dve.tensor_tensor(b["hn_lo"][:, :, n * P:(n + 1) * P], psum[:, 2 * (n % 2):2 * (n % 2) + 2, :]
                                  .rearrange("p a (k t) -> p (a k) t", k=4),
                                  b["hn_hi"][:, :, n * P:(n + 1) * P].bitcast(F32), ALU.subtract).then_inc(S["hn_lo"], 1)

            dve.wait_ge(S["wg_hi"], 1)
            for row, g in ((0, 0), (32, 2), (64, 1), (96, 3)):
                i = dve.tensor_tensor(b["wg_lo"][:, :, row:row + H], b["graw"][:, :, g * H:(g + 1) * H],
                                      b["wg_hi"][:, :, row:row + H].bitcast(F32), ALU.subtract)
            i.then_inc(S["wg_lo"], 1)

            def split_low(j):
                dve.wait_ge(S["w_hi"], j + 1)
                dve.tensor_tensor(b["wlo"][:, j % 2, :, :], b["wraw"][:, j % 2, :, :],
                                  b["whi"][:, j % 2, :, :].bitcast(F32), ALU.subtract).then_inc(S["w_lo"], 1)

            def last_col(t2, c):
                return t2[0:ROWS, (c + 1) * P - 1:(c + 1) * P]

            def by_chunk(t2):
                return t2[0:ROWS, :].rearrange("r (c t) -> r c t", t=P)

            def gate_rows():
                dve.wait_ge(S["zeroed"], 6)
                dve.wait_ge(S["soft"], 1)
                r = slice(64, GATE_ROWS)
                ch(dve.scalar_tensor_tensor(b["GA"][r, :], b["GA"][r, :], 0.0, b["TM"][r, :], ALU.min, ALU.subtract))
                dve.tensor_copy(b["LF"][0:H, :], b["GA"][64:64 + H, :])
                dve.tensor_copy(b["LI"][0:H, :], b["GA"][0:H, :])
                for lo, hi in seqs:
                    dve.tensor_copy(natural(b["LF"][32:32 + H, :], lo, hi), reverse(b["GA"][96:96 + H, :], lo, hi))
                    i = dve.tensor_copy(natural(b["LI"][32:32 + H, :], lo, hi), reverse(b["GA"][32:32 + H, :], lo, hi))
                ch(i)
                zero = zrow[:, 0:1].to_broadcast([ROWS, P])
                for c in range(NT):
                    t = slice(c * P, (c + 1) * P)
                    i = dve.tensor_tensor_scan(b["LF"][:, t], b["LF"][:, t], zero, 0.0, ALU.add, ALU.add)
                ch(i)
                ch(dve.tensor_tensor(b["LI"][:, :], b["LI"][:, :], b["LF"][:, :], ALU.subtract))
                for c in range(NT):
                    t = slice(c * P, (c + 1) * P)
                    if c in starts:
                        ch(dve.memset(b["mst"][:, c:c + 1], 0.0))
                    else:
                        ch(dve.tensor_tensor(b["mst"][:, c:c + 1], last_col(b["MM"], c - 1), last_col(b["LF"], c - 1), ALU.add))
                    ch(dve.tensor_tensor_scan(b["MM"][:, t], b["LI"][:, t], zero, b["mst"][:, c:c + 1], ALU.max, ALU.add))
                ends = by_chunk(b["MM"])[:, :, P - 1:P].to_broadcast([ROWS, NT, P])
                dve.tensor_tensor(by_chunk(b["GA"]), by_chunk(b["LI"]), ends, ALU.subtract).then_inc(S["rows_t"], 1)
                dve.tensor_copy(b["R"][0:H, 0, :], b["LI"][0:H, :])
                dve.tensor_scalar(b["R"][0:H, 4, :], b["MM"][0:H, :], -1.0, None, ALU.mult)
                for lo, hi in seqs:
                    dve.tensor_copy(reverse(b["R"][32:32 + H, 0, :], lo, hi), natural(b["LI"][32:32 + H, :], lo, hi))
                    i = dve.tensor_scalar(reverse(b["R"][32:32 + H, 4, :], lo, hi), natural(b["MM"][32:32 + H, :], lo, hi),
                                          -1.0, None, ALU.mult)
                i.then_inc(S["rows_nat"], 1)
                dve.wait_ge(S["rows_nat"], 1)
                dve.tensor_tensor(by_chunk(b["LI"]), b["mst"][:, :].rearrange("r (c a) -> r c a", a=1)
                                  .to_broadcast([ROWS, NT, P]), by_chunk(b["MM"]), ALU.subtract).then_inc(S["rows_t"], 1)
                dve.tensor_tensor(b["LF"][:, :], b["LF"][:, :], b["MM"][:, :], ALU.add).then_inc(S["rows_t"], 1)

            split_low(0)
            for j in range(-1, NCH):
                if 0 <= j < NCH - 1:
                    split_low(j + 1)
                if j == 0:
                    gate_rows()
                if j >= 0 and chunks[j][0] == "gc" and chunks[j][2] == 0:
                    dve.wait_ge(S["colT_ps"], 3)
                    dve.wait_ge(S["rows_out"], 16 * 6)
                    for m in range(2):
                        for col in (0, SP_ + 1, SP_ + 2, T + 3):
                            i = dve.memset(b["CU"][:, m, col:col + 1], 0.0)
                    ch(i)
                for i in of_chunk[j]:
                    _, kind, part, m, t0, w = pgroups[i]
                    if kind not in EV_DVE:
                        continue
                    dve.wait_ge(S["proj"], i + 1)
                    src = psum[:, 4 + i % 4, 0:w]
                    off = 1 if t0 < SP_ else 3
                    if kind == "u":
                        dve.wait_ge(S["ev_act"], ev_at[of_chunk[j - 1][-1]][1])
                        dve.tensor_tensor(b["CU"][:, m, t0 + off:t0 + off + w], src, b["gcS"][:, m, t0:t0 + w], ALU.mult
                                          ).then_inc(S["ev_dve"], 1)
                        if i == of_chunk[j][-1]:
                            dve.wait_ge(S["ev_dve"], ev_at[i][1])
                            for mm in range(2):
                                for s0, n, o in ((0, SP_, 0), (SP_, SS_, 2)):
                                    cv = b["CV"][:, mm, s0:s0 + n]
                                    tap = [b["cw"][:, k, 2 * part + mm:2 * part + mm + 1] for k in range(3)]
                                    x = [b["CU"][:, mm, s0 + o + k:s0 + o + k + n] for k in range(3)]
                                    ch(dve.tensor_scalar(cv, x[0], tap[0], None, ALU.mult))
                                    ch(dve.scalar_tensor_tensor(cv, x[1], tap[1], cv, ALU.mult, ALU.add))
                                    ch(dve.scalar_tensor_tensor(cv, x[2], tap[2], cv, ALU.mult, ALU.add))
                    else:
                        s = stage_no[i]
                        if s >= NST:
                            dve.wait_ge(stg[s % NST], 16 * (s // NST))
                        dve.tensor_tensor(b["stage"][:, s % NST, 0:w], src, b["CV"][:, m, t0:t0 + w], ALU.mult
                                          ).then_inc(S["ev_dve"], 1)
            barrier(dve, 1)

            dve.memset(d["v1"][:, :, :, :, DV:VPAD], 1.0)
            dve.memset(d["ST"][:, 1, :, :, :], 0.0)
            dve.memset(d["ST"][:, 0, :, :, :], 0.0).then_inc(S["st_upd"], 1)
            dve.wait_ge(S["st_upd"], 1)
            dve.wait_ge(S["cst_in"], 16 * 11)
            for i in range(NT):
                dve.wait_ge(S["kT_ps"], i + 1)
                for dr, c in ((0, fwd[i]), (1, bwd[i])):
                    w = colS[:, colslot(c, 1), 32 * dr:32 * dr + H].rearrange("p (h a) -> p h a", a=1)
                    k = dve.tensor_tensor(d["wk"][:, dr, :, :], psum[:, 0, dr * QK:(dr + 1) * QK]
                                          .rearrange("p (h n) -> p h n", h=H), w.to_broadcast([P, H, DK]), ALU.mult)
                k.then_inc(S["wk_done"], 1)
                dve.wait_ge(S["u_ps"], i + 1)
                if i + 1 < NT:
                    if i >= 1:
                        dve.wait_ge(st_out[(i - 1) % 2], 32 * ((i - 1) // 2 + 1))
                    for dr, c in ((0, fwd[i]), (1, bwd[i])):
                        for pr in range(2):
                            new = d["ST"][:, (i + 1) % 2, dr, pr, 0:VA]
                            if i + 1 in starts:
                                k = dve.memset(new, 0.0)
                            else:
                                k = dve.scalar_tensor_tensor(new, d["ST"][:, i % 2, dr, pr, 0:VA],
                                                             d["dcb"][:, dr, pr, c:c + 1],
                                                             psum[:, 1 + dr, VPAD * pr:VPAD * pr + VA],
                                                             ALU.mult, ALU.add)
                    k.then_inc(S["st_upd"], 1)
                    dve.wait_ge(S["st_upd"], i + 2)
                if i < KD:
                    dve.wait_ge(S["wo_hi"], i + 1)
                    dve.tensor_tensor(d["wol"][:, i, :], d["woraw"][:, i % 2, :], d["woh"][:, i, :].bitcast(F32), ALU.subtract
                                      ).then_inc(S["wo_lo"], 1)
            barrier(dve, 2)

            dve.memset(d["vs"][:, :, :, DV:VPAD], 1.0)
            ch(dve.memset(AFF[:, :], -1.0))

            def residual(n, h):
                dve.wait_ge(S["o_ps"], 2 * n + h + 1)
                if h == 0:
                    dve.wait_ge(ld_x[n % 2], 16 * (n // 2 + 1))
                    if n >= 2:
                        dve.wait_ge(x1_out[n % 2], 16 * (n // 2))
                        dve.wait_ge(S["tk_done"], n - 1)
                dve.tensor_tensor(d["x1"][:, n % 2, 512 * h:512 * h + 512], psum[:, 6 + h, :],
                                  d["xs"][:, n % 2, 512 * h:512 * h + 512], ALU.add).then_inc(S["x1_done"], 1)

            def exponents(n):
                dve.wait_ge(ld[n % 2], 16 * NLD * (n // 2 + 1))
                if n >= 1:
                    dve.wait_ge(S["e_done"], n)
                for r in range(2 * H):
                    dr, h = r // H, r % H
                    i = dve.scalar_tensor_tensor(d["X"][:, r, :], d["negm"][:, n % 2, r, :],
                                                 colS[:, colslot(n, 0), 32 * dr + h:32 * dr + h + 1],
                                                 d["masks"][:, dr, :], ALU.add, ALU.min)
                i.then_inc(S["x_done"], 1)

            def decayed_scores(n):
                dve.wait_ge(S["e_done"], n + 1)
                dve.wait_ge(S["s_ps"], n + 1)
                if n >= 1:
                    dve.wait_ge(S["num_ps"], n)
                for dr in range(2):
                    i = dve.tensor_tensor(d["SD"][:, H * dr:H * dr + H, :], psum[:, 0, :]
                                          .rearrange("p (h t) -> p h t", h=H), d["E"][:, H * dr:H * dr + H, :],
                                          ALU.mult)
                i.then_inc(S["sd_done"], 1)

            exponents(0)
            decayed_scores(0)
            for n in range(NT + 2):
                s = n % 2
                if n < NT:
                    dve.wait_ge(S["num_ps"], n + 1)
                    den = psum[:, 1:5, 0:2 * VPAD].rearrange("p a (b c) -> p a b c", c=VPAD)[:, :, :, DV]
                    floor = colS[:, colslot(n, 2), :]
                    low, inv = d["sm"][:, s, 8:16], d["sm"][:, s, 0:8]
                    for dr in range(2):
                        i = dve.scalar_tensor_tensor(low[:, 4 * dr:4 * dr + 4].rearrange("p (a c) -> p a c", a=2),
                                                     den[:, 2 * dr:2 * dr + 2, :], -1.0,
                                                     floor[:, 32 * dr:32 * dr + H].rearrange("p (a c) -> p a c", a=2),
                                                     ALU.mult, ALU.max)
                    ch(i)
                    ch(dve.tensor_tensor(low.rearrange("p (a c) -> p a c", a=4), den,
                                         low.rearrange("p (a c) -> p a c", a=4), ALU.max))
                    dve.reciprocal(inv, low).then_inc(S["den_done"], 1)
                    if n + 1 < NT:
                        exponents(n + 1)
                    dve.wait_ge(S["den_done"], n + 1)
                    dve.wait_ge(S["hb_done"], n + 1)
                    if n >= 1:
                        dve.wait_ge(S["hsum"], n)
                    for h in range(H):
                        i = dve.scalar_tensor_tensor(d["ht"][:, h, :],
                                                     psum[:, 1 + h // 2, VPAD * (h % 2):VPAD * (h % 2) + DV],
                                                     d["sm"][:, s, h:h + 1], d["hb"][:, h, :], ALU.mult, ALU.add)
                    i.then_inc(S["ht_done"], 1)
                if 1 <= n <= NT:
                    residual(n - 1, 0)
                if n < NT:
                    dve.wait_ge(S["hsum"], n + 1)
                    inverse_root(d["ms"][:, s, 1, :], d["ms"][:, s, 0, :], d["ms"][:, s, 2, :])
                    dve.wait_ge(S["og_done"], n + 1)
                    if n >= 1:
                        dve.wait_ge(S["mixT_ps"], n)
                    for h in range(H):
                        i = dve.scalar_tensor_tensor(d["mix"][:, h, :], d["ht"][:, h, :], d["ms"][:, s, 1, h:h + 1],
                                                     d["og"][:, s, h * DV:(h + 1) * DV], ALU.mult, ALU.mult)
                    i.then_inc(S["mix_done"], 1)
                    if n + 1 < NT:
                        decayed_scores(n + 1)
                if 1 <= n <= NT:
                    residual(n - 1, 1)
                if n < NT:
                    dve.wait_ge(S["mxh_done"], 2 * n + 1)
                    dve.tensor_tensor(d["mxl"][:, s, 0:4, :], d["cvs"][:, s, :, :],
                                      d["mxh"][:, s, 0:4, :].bitcast(F32), ALU.subtract)
                if n >= 2:
                    m = n - 2
                    dve.wait_ge(S["lg_ps"], m + 1)
                    dve.tensor_reduce(logit_max[:, m, 0:1], psum[:, 3, 0:NE], AX_X, ALU.max, negate=True
                                      ).then_inc(S["lgmax"], 1)
                if n < NT:
                    dve.wait_ge(S["mxh_done"], 2 * n + 2)
                    dve.tensor_tensor(d["mxl"][:, s, 4:8, :], psum[:, 5, :].rearrange("p (k t) -> p k t", k=4),
                                      d["mxh"][:, s, 4:8, :].bitcast(F32), ALU.subtract).then_inc(S["mxl_done"], 1)
                if 1 <= n <= NT:
                    m = n - 1
                    q = m % 2
                    dve.wait_ge(S["sum2"], m + 1)
                    inverse_root(d["mt"][:, q, 1, :], d["mt"][:, q, 0, :], d["mt"][:, q, 2, :])
                    if m >= 2:
                        dve.wait_ge(tk_out[q], 16 * (m // 2))
                        dve.wait_ge(S["tkT_ps"], m - 1)
                    dve.scalar_tensor_tensor(d["tk"][:, q, :], d["x1"][:, q, :], d["mt"][:, q, 1, :], d["g2b"][:, :],
                                             ALU.mult, ALU.mult).then_inc(S["tk_done"], 1)
                if n >= 2:
                    m = n - 2
                    dve.wait_ge(S["exps"], m + 1)
                    ch(dve.reciprocal(logit_max[:, m, 2:3], logit_max[:, m, 1:2]))
                    dve.tensor_scalar(aff[:, m, :], aff[:, m, :], logit_max[:, m, 2:3], None, ALU.mult
                                      ).then_inc(S["aff_done"], 1)

            dve.wait_ge(S["affT_ps"], 3)
            ch(dve.tensor_copy(AFF[32:32 + NE, 0:SP_], psum[0:NE, 1, 0:SP_]))
            for i in range(SS_ // 512):
                ch(dve.tensor_copy(AFF[0:NE, 512 * i:512 * i + 512], psum[0:NE, 2 + i, :]))
            for r in range(CAPS // 8):
                best = GV[:, 8 * r:8 * r + 8]
                ch(dve.max(best, AFF[:, :]))
                ch(dve.max_index(GI[:, 8 * r:8 * r + 8], best, AFF[:, :]))
                if r < CAPS // 8 - 1:
                    ch(dve.match_replace(AFF[:, :], best, AFF[:, :], -2.0))
            dve.tensor_copy(GIF[:, :], GI[:, :]).then_inc(S["topk"], 1)
            dve.wait_ge(S["selT_ps"], 2)
            dve.tensor_copy(GC[:, :], psum[:, 4, 0:48])
            dve.tensor_scalar(IDX[:, 0:NE], psum[:, 5, 0:NE], float(SP_), None, ALU.add)
            dve.tensor_copy(IDX[:, 32:32 + NE], psum[:, 5, 32:32 + NE])
            barrier(dve, 3)

            def low(e, j):
                if j in BY_DVE:
                    dve.wait_ge(S["ehi"], NB * e + j + 1)
                    dve.tensor_tensor(f["elo"][:, j % RING, :, :], f["eraw"][:, j % RING, :, :],
                                      f["ehi"][:, j % RING, :, :].bitcast(F32), ALU.subtract
                                      ).then_inc(S["elo_dve"], 1)

            def tokens_low(e, s, which):
                for g in which:
                    k0, nk = TG[g]
                    dve.wait_ge(S["xc_hi"], 3 * e + g + 1)
                    dve.tensor_tensor(f["xc"][:, s, k0:k0 + nk, 1, :], psum[:, 6 + g % 2, 0:nk * NC]
                                      .rearrange("p (k t) -> p k t", k=nk),
                                      f["xc"][:, s, k0:k0 + nk, 0, :].bitcast(F32), ALU.subtract).then_inc(S["xc_lo"], 1)

            tokens_low(0, 0, (0, 1, 2))
            for j in range(4):
                low(0, j)
            dve.sem_inc(S["hc_lo"], 4)

            def expert(e, s, first=False, last=False):
                for p in range(4):
                    for m in range(2):
                        i = 2 * p + m
                        dve.wait_ge(S["gu_ps"], 8 * e + i + 1)
                        if m == 0 and not (first and p < 2):
                            dve.wait_ge(S["hid_done"], 1 + 4 * e + p - 1)
                        base = 2 * (i % 2)
                        both = psum[:, base:base + 2, 0:2 * NC].rearrange("p a (t n) -> p a n t", t=2)
                        dve.tensor_reduce(f["gu"][:, p % 2, m, :, :], both, AX_X, ALU.add).then_inc(S["gu_add"], 1)
                        if m == 0 and p < 3:
                            low(e, 2 * p + 4)
                    if p in (1, 2) and not last:
                        tokens_low(e + 1, 1 - s, ((0, 1), (2,))[p - 1])
                    if p < 3:
                        low(e, 2 * p + 5)
                    dve.wait_ge(S["hc_hi"], 4 * e + p + 1)
                    dve.tensor_tensor(f["hc"][:, 2 * p:2 * p + 2, 1, :], f["hid"][:, :, :],
                                      f["hc"][:, 2 * p:2 * p + 2, 0, :].bitcast(F32), ALU.subtract
                                      ).then_inc(S["hc_lo"], 1)
                low(e, 10)
                for q in range(4):
                    for m in range(2):
                        i = 2 * q + m
                        dve.wait_ge(S["dn_ps"], 8 + 8 * e + i + 1)
                        dve.wait_ge(S["yT_ps"], 8 * e + i + 1)
                        both = psum[:, 4 + i % 2, 0:2 * NC].rearrange("p (t n) -> p n t", t=2)
                        dve.tensor_reduce(f["ys"][:, i % 2, :], both, AX_X, ALU.add).then_inc(S["ys_done"], 1)
                    if not last:
                        low(e + 1, q)

            expert(0, 0, first=True)
            with dve.Fori(0, NE // 2 - 1) as g:
                expert(2 * g + 1, 1)
                expert(2 * g + 2, 0)
            expert(NE - 1, 1, last=True)
            barrier(dve, 4)
            dve.wait_ge(S["gf_in"], 16)
            for n in range(NT):
                if n % 2 == 0:
                    dve.wait_ge(S["f_sum"], n + 2)
                    c = slice(n, n + 2)
                    inverse_root(z["fs"][:, 1, c], z["fs"][:, 0, c], z["fs"][:, 2, c])
                dve.scalar_tensor_tensor(z["fx"][:, n, :], z["fx"][:, n, :], z["fs"][:, 1, n:n + 1], z["gf"][:, :],
                                         ALU.mult, ALU.mult).then_inc(S["f_y"], 1)

        @block.tensor
        def _(pe):
            pe.wait_ge(S["const"], 1)
            for n in range(NT):
                pe.wait_ge(S["xn_done"], n + 1)
                if n >= 2:
                    pe.wait_ge(S["hn_lo"], n - 1)
                for k in range(KD):
                    i = pe.transpose(psum[:, 2 * (n % 2) + k // 4, (k % 4) * P:(k % 4 + 1) * P],
                                     b["xa"][:, n, k * P:(k + 1) * P], ident[:, :])
                i.then_inc(S["xT_ps"], 1)

            pe.wait_ge(S["hn_lo"], NT)
            for i, (j, kind, part, m, t0, w) in enumerate(pgroups):
                if kind == "gate":
                    if i == 0:
                        pe.wait_ge(S["wg_lo"], 1)
                elif i == of_chunk[j][0]:
                    pe.wait_ge(S["w_lo"], j + 1)
                if i >= 4:
                    who, c = ev_at[i - 4]
                    pe.wait_ge(S["ev_act"] if who == "act" else S["ev_dve"], c)
                for k in range(KD):
                    if kind in ("v", "o"):
                        t = slice(m * P, (m + 1) * P)
                        xh, xl = b["hn_hi"][:, k, t], b["hn_lo"][:, k, t]
                        wh, wl = b["whi"][:, j % 2, k, :], b["wlo"][:, j % 2, k, :]
                        pairs = ((xh, wh), (xh, wl), (xl, wh))
                        o = psum[:, 4 + i % 4, 0:w]
                    else:
                        t = slice(t0, t0 + w)
                        xh, xl = b["hn_hi"][:, k, t], b["hn_lo"][:, k, t]
                        if kind == "gate":
                            wh, wl = b["wg_hi"][:, k, 0:GATE_ROWS], b["wg_lo"][:, k, 0:GATE_ROWS]
                            o = psum[0:GATE_ROWS, 4 + i % 4, 0:w]
                        else:
                            c = slice(m * P, (m + 1) * P)
                            wh, wl = b["whi"][:, j % 2, k, c], b["wlo"][:, j % 2, k, c]
                            o = psum[:, 4 + i % 4, 0:w]
                        pairs = ((wh, xh), (wh, xl), (wl, xh))
                    for a, (lhs, rhs) in enumerate(pairs):
                        mm = pe.matmul(o, lhs, rhs, start=(k == 0 and a == 0), stop=(k == KD - 1 and a == 2))
                mm.then_inc(S["proj"], 1)
                if i == of_chunk[1][-1]:
                    pe.wait_ge(S["rows_nat"], 1)
                    pe.wait_ge(S["rows_exp"], 9)
                    for c in range(NT):
                        for q in range(3):
                            a = colslot(c, q)
                            tr = pe.transpose(psum[:, a // 12, (a % 12) * 40:(a % 12) * 40 + ROWS],
                                              b["R"][:, q, c * P:(c + 1) * P], ident[0:ROWS, 0:ROWS])
                            if a % 12 == 11 or a == 3 * NT - 1:
                                tr.then_inc(S["colT_ps"], 1)
            barrier(pe, 1)

            for i in range(NT):
                pe.wait_ge(l1[i % 2], 16 * 4 * (i // 2 + 1))
                if i >= 1:
                    pe.wait_ge(S["wk_done"], i)
                for dr in range(2):
                    for pr in range(2):
                        tr = pe.transpose(psum[:, 0, dr * QK + pr * P:dr * QK + (pr + 1) * P],
                                          d["kT1"][:, i % 2, dr, pr, :], ident[:, :])
                tr.then_inc(S["kT_ps"], 1)
                pe.wait_ge(S["wk_done"], i + 1)
                if i >= 1:
                    pe.wait_ge(S["st_upd"], i + 1)
                for dr in range(2):
                    for pr in range(2):
                        for half in range(2):
                            h = 2 * pr + half
                            mm = pe.matmul(psum[64 * half:64 * half + 64, 1 + dr, VPAD * pr:VPAD * pr + VA],
                                           d["wk"][:, dr, h, :], d["v1"][:, i % 2, dr, h, 0:VA], start=True, stop=True)
                mm.then_inc(S["u_ps"], 1)
            barrier(pe, 2)

            def project(n, h):
                pe.wait_ge(S["mxl_done"], n + 1)
                if n >= 1:
                    pe.wait_ge(S["x1_done"], 2 * (n - 1) + h + 1)
                c = slice(512 * h, 512 * h + 512)
                for k in range(KD):
                    for a, (x, w) in enumerate((("mxh", "woh"), ("mxh", "wol"), ("mxl", "woh"))):
                        mm = pe.matmul(psum[:, 6 + h, :], d[x][:, n % 2, k, :], d[w][:, k, c],
                                       start=(k == 0 and a == 0), stop=(k == KD - 1 and a == 2))
                mm.then_inc(S["o_ps"], 1)

            def scores(n):
                pe.wait_ge(ld[n % 2], 16 * NLD * (n // 2 + 1))
                if n >= 1:
                    pe.wait_ge(S["sd_done"], n)
                for h in range(H):
                    mm = pe.matmul(psum[:, 0, h * P:(h + 1) * P], d["kTs"][:, n % 2, h // 2, :],
                                   d["qz"][:, n % 2, h, :], start=True, stop=True)
                mm.then_inc(S["s_ps"], 1)

            scores(0)
            for n in range(NT + 2):
                s = n % 2
                if n < NT:
                    pe.wait_ge(S["sd_done"], n + 1)
                    pe.wait_ge(S["qs_done"], n + 1)
                    if n >= 1:
                        pe.wait_ge(S["ht_done"], n)
                    if n >= 3:
                        pe.wait_ge(S["exps"], n - 2)
                    for dr in range(2):
                        for h in range(H):
                            o = psum[:, 1 + 2 * dr + h // 2, VPAD * (h % 2):VPAD * (h % 2) + VA]
                            pe.matmul(o, d["SD"][:, H * dr + h, :], d["vs"][:, s, h, 0:VA], start=True, stop=False)
                            mm = pe.matmul(o, d["qs"][:, H * dr + h, :], d["sts"][:, s, dr, h // 2, 0:VA],
                                           start=False, stop=True)
                    mm.then_inc(S["num_ps"], 1)
                if 1 <= n <= NT:
                    project(n - 1, 0)
                if n + 1 < NT:
                    scores(n + 1)
                if n >= 2:
                    m = n - 2
                    pe.wait_ge(S["tk_done"], m + 1)
                    if n < NT:
                        pe.wait_ge(S["ht_done"], n + 1)
                    if m >= 1:
                        pe.wait_ge(S["tkT_done"], m)
                    for k in range(KD):
                        tr = pe.transpose(psum[:, 1 + k // 4, (k % 4) * P:(k % 4 + 1) * P],
                                          d["tk"][:, m % 2, k * P:(k + 1) * P], ident[:, :])
                    tr.then_inc(S["tkT_ps"], 1)
                if 1 <= n <= NT:
                    project(n - 1, 1)
                if n >= 2:
                    pe.wait_ge(S["tkT_done"], m + 1)
                    if m >= 1:
                        pe.wait_ge(S["exps"], m)
                    for k in range(KD):
                        mm = pe.matmul(psum[:, 3, 0:NE], d["tkT"][:, k, :], d["wr"][:, k, :], start=(k == 0),
                                       stop=(k == KD - 1))
                    mm.then_inc(S["lg_ps"], 1)
                if n < NT:
                    if n >= 1:
                        pe.wait_ge(S["mxl_done"], n)
                    pe.wait_ge(S["mix_done"], n + 1)
                    for h in range(H):
                        tr = pe.transpose(psum[:, 5, h * P:(h + 1) * P], d["mix"][:, h, :], ident[:, :])
                    tr.then_inc(S["mixT_ps"], 1)
            pe.wait_ge(S["aff_done"], NT)
            for n in range(NT):
                i, col = (1, n * P) if n < NTP else (2 + (n - NTP) // 4, (n - NTP) % 4 * P)
                tr = pe.transpose(psum[0:NE, i, col:col + P], aff[:, n, :], ident[:, :])
                if n == NTP - 1 or (n >= NTP and (n - NTP) % 4 == 3):
                    tr.then_inc(S["affT_ps"], 1)
            pe.wait_ge(S["topk"], 1)
            pe.transpose(psum[:, 4, 0:48], GV[:, :], ident[0:48, 0:48]).then_inc(S["selT_ps"], 1)
            pe.transpose(psum[:, 5, 0:48], GIF[:, :], ident[0:48, 0:48]).then_inc(S["selT_ps"], 1)
            barrier(pe, 3)

            def token_columns(e, which):
                pe.wait_ge(S["gath"], 32 * e + 32)
                for g in which:
                    k0, nk = TG[g]
                    if g == 2:
                        pe.wait_ge(S["xc_lo"], 3 * e + 1)
                    for k in range(nk):
                        c = slice((k0 + k) * P, (k0 + k + 1) * P)
                        o = psum[:, 6 + g % 2, k * NC:(k + 1) * NC]
                        pe.transpose(o[:, 0:CAPS], f["xg"][:, c], ident[:, :])
                        tr = pe.transpose(o[:, CAPS:NC], f["xgp"][:, c], ident[0:CAPP, 0:CAPP])
                    tr.then_inc(S["exT_ps"], 1)

            def rows_back(e, i):
                pe.wait_ge(S["ys_done"], 2 + 8 * e + i + 1)
                c = slice((i % 4) * P, (i % 4 + 1) * P)
                pe.transpose(psum[:, 6, c], f["ys"][:, i % 2, 0:CAPS], ident[:, :])
                pe.transpose(psum[0:CAPP, 7, c], f["ys"][:, i % 2, CAPS:NC], ident[:, :]).then_inc(S["yT_ps"], 1)

            def products(o, q, c, x, xb, k0=0, k1=KD):
                for k in range(k0, k1):
                    pe.matmul(o[:, 0:2 * NC], f["ehi"][:, q, k, c], x[:, k, :, :].rearrange("p a t -> p (a t)"),
                              start=(k == 0), stop=False, skip_group_check=True)
                for k in range(k0, k1):
                    mm = pe.matmul(o[:, NC:2 * NC], f["elo"][:, q, k, c], xb[:, k, :], start=False,
                                   stop=(k == KD - 1), skip_group_check=True)
                return mm

            token_columns(0, (0, 1, 2))

            def expert(e, s, first=False, last=False):
                pe.wait_ge(S["xc_lo"], 3 * e + 3)
                pe.wait_ge(S["xb_done"], e + 1)
                for p in range(4):
                    wait_split(pe, e, 2 * p)
                    wait_split(pe, e, 2 * p + 1)
                    for m in range(2):
                        i = 2 * p + m
                        pe.wait_ge(S["gu_add"], 8 * e + i + 1)
                        for a in range(2):
                            mm = products(psum[:, 2 * (i % 2) + a, :], (2 * p + a) % RING, slice(m * P, (m + 1) * P),
                                          f["xc"][:, s, :, :, :], f["xb"][:, s, :, :])
                        mm.then_inc(S["gu_ps"], 1)
                        if i == 0 and not first:
                            rows_back(e - 1, KD - 1)
                        if i == 3 and not last:
                            pe.wait_ge(S["y_done"], 2 * e + 2)
                            token_columns(e + 1, (0, 1))
                        if i == 5 and not last:
                            token_columns(e + 1, (2,))
                for q in range(4):
                    wait_split(pe, e, 8 + q)
                    tiles = [(psum[:, 4 + m, :], (8 + q) % RING, slice(m * P, (m + 1) * P), f["hc"], f["hbf"])
                             for m in range(2)]
                    pe.wait_ge(S["ys_done"], 8 * e + 2 * q + 1)
                    if q == 0:
                        pe.wait_ge(S["hc_lo"], 4 + 4 * e + 3)
                        pe.wait_ge(S["hb_bf"], 1 + 4 * e + 3)
                        products(*tiles[0], 0, KF - 2)
                        pe.wait_ge(S["ys_done"], 8 * e + 2 * q + 2)
                        products(*tiles[1], 0, KF - 2)
                        pe.wait_ge(S["hc_lo"], 4 + 4 * e + 4)
                        pe.wait_ge(S["hb_bf"], 1 + 4 * e + 4)
                    for m in range(2):
                        i = 2 * q + m
                        if q > 0 and m == 1:
                            pe.wait_ge(S["ys_done"], 8 * e + i + 1)
                        products(*tiles[m], KF - 2 if q == 0 else 0, KF).then_inc(S["dn_ps"], 1)
                        if i == 1:
                            if last:
                                pe.wait_ge(S["y_done"], 2 * e + 2)
                            else:
                                pe.wait_ge(S["xc_lo"], 3 * (e + 1) + 3)
                        if i == 5:
                            pe.wait_ge(S["y_done"], 2 + 2 * e + 1)
                        if i >= 1:
                            rows_back(e, i - 1)

            expert(0, 0, first=True)
            with pe.Fori(0, NE // 2 - 1) as g:
                expert(2 * g + 1, 1)
                expert(2 * g + 2, 0)
            expert(NE - 1, 1, last=True)
            rows_back(NE - 1, KD - 1)
            barrier(pe, 4)


_INS = ['x_prompt', 'x_sample', 'norm1_g', 'w_in', 'conv_w', 'gate_bias', 'head_norm_g', 'w_out', 'norm2_g',
        'w_router', 'w_gate', 'w_up', 'w_down', 'final_g']


def kernel(**inputs):
    import numpy as _np
    import concourse.bacc as _bacc
    from concourse import mybir as _mybir
    from concourse.bass_utils import run_bass_kernel_spmd as _run

    nc = _bacc.Bacc("TRN2", target_bir_lowering=False, num_devices=1)
    arrays, args = {}, []
    for name in _INS:
        a = _np.ascontiguousarray(inputs[name])
        arrays[f"in_{name}_dram"] = a
        args.append(nc.dram_tensor(f"in_{name}_dram", a.shape, _mybir.dt.from_np(a.dtype), kind="ExternalInput").ap())
    outs = [("y_prompt", inputs["x_prompt"].shape), ("y_sample", inputs["x_sample"].shape)]
    for name, shape in outs:
        args.append(nc.dram_tensor(f"out_{name}_dram", tuple(shape), _mybir.dt.float32, kind="ExternalOutput").ap())
    hybrid_conv_mlstm_moe(nc, *args)
    r = _run(nc, [arrays], core_ids=[0])
    return tuple(r.results[0][f"out_{name}_dram"] for name, _ in outs)
```

```python
from contextlib import ExitStack

import concourse.bass as bass
from concourse import mybir

ALU = mybir.AluOpType
ACT = mybir.ActivationFunctionType
AX_X = mybir.AxisListType.X
F32 = mybir.dt.float32
F32R = mybir.dt.float32r
BF16 = mybir.dt.bfloat16
U32 = mybir.dt.uint32

P = 128
NEG = -1.0e30


class Chain:

    def __init__(self, eng, sem):
        self.eng, self.sem, self.n = eng, sem, 0

    def __call__(self, ins):
        ins.then_inc(self.sem, 1)
        self.n += 1
        self.eng.wait_ge(self.sem, self.n)


def hybrid_conv_mlstm_moe(nc, x_prompt, x_sample, norm1_g, w_in, conv_w, gate_bias, head_norm_g, w_out,
                          norm2_g, w_router, w_gate, w_up, w_down, final_g, y_prompt, y_sample):
    D = x_prompt.shape[2]
    SP_, SS_ = x_prompt.shape[1], x_sample.shape[1]
    T = SP_ + SS_
    KD = D // P
    NT = T // P
    NTP = SP_ // P
    CW = conv_w.shape[2]
    H = gate_bias.shape[2]
    DV = (D // 2) // H
    DK = DV // 2
    QK = H * DK
    VW = H * DV
    NE = w_gate.shape[1]
    FF = w_gate.shape[3]
    KF = FF // P
    CAPP, CAPS = 2 * SP_ // NE, 2 * SS_ // NE
    NC = CAPP + CAPS
    EPS = 1e-6
    VA = DV + 1
    VPAD = DV + 2
    GATE_ROWS = 100
    ROWS = 36
    assert (D, DV, DK, H, CAPS) == (1024, 128, 64, 4, 128) and SP_ % 256 == 0 and SS_ % 512 == 0

    x_chunk = [x_prompt[0, t * P:(t + 1) * P, :] for t in range(NTP)] + \
              [x_sample[0, t * P:(t + 1) * P, :] for t in range(NT - NTP)]
    y_chunk = [y_prompt[0, t * P:(t + 1) * P, :] for t in range(NTP)] + \
              [y_sample[0, t * P:(t + 1) * P, :] for t in range(NT - NTP)]

    qk_d = nc.dram_tensor("qk_d", (4, P, T), F32).ap()
    v_d = nc.dram_tensor("v_d", (T, VW), F32).ap()
    o_d = nc.dram_tensor("o_d", (T, VW), F32).ap()
    conv_d = nc.dram_tensor("conv_d", (CW // P, P, T), F32).ap()
    negm_d = nc.dram_tensor("negm_d", (2 * H, T), F32).ap()
    inter_d = nc.dram_tensor("inter_d", (2 * H, T), F32).ap()
    decay_d = nc.dram_tensor("decay_d", (2 * H, NT), F32).ap()
    state_d = nc.dram_tensor("state_d", (NT, P, 2, 2 * VPAD), F32).ap()
    acc_d = nc.dram_tensor("acc_d", (T, D), F32).ap()
    tok_d = nc.dram_tensor("tok_d", (T, D), F32).ap()

    groups = [(0, SP_)] + [(SP_ + i * 512, 512) for i in range(SS_ // 512)]
    BATCHES = [(0, 2), (2, 6), (6, NT)]

    c_gb, c_gc, c_u = 0, CW, 2 * CW
    c_q, c_k, c_v = 3 * CW, 3 * CW + QK, 3 * CW + 2 * QK
    c_o = c_v + VW
    c_gates = c_o + VW
    CH = 256
    chunks = [("k", c_k, 0), ("q", c_q, 0)] + [("v", c_v + i * CH, i) for i in range(VW // CH)] + \
             [("o", c_o + i * CH, i) for i in range(VW // CH)]
    for i in range(CW // CH):
        chunks += [("gc", c_gc + i * CH, i), ("u", c_u + i * CH, i), ("gb", c_gb + i * CH, i)]
    NCH = len(chunks)
    pgroups = [(-1, "gate", 0, 0, t0, w) for t0, w in groups]
    for j, (kind, _, part) in enumerate(chunks):
        if kind in ("v", "o"):
            pgroups += [(j, kind, part, t, 0, CH) for t in range(NT)]
        else:
            pgroups += [(j, kind, part, m, t0, w) for m in range(2) for t0, w in groups]
    EV_DVE = ("u", "gb")
    ev_at, n_act, n_dve = [], 0, 0
    for g in pgroups:
        if g[1] in EV_DVE:
            n_dve += 1
            ev_at.append(("dve", n_dve))
        else:
            n_act += 1
            ev_at.append(("act", n_act))
    NST = 4
    staged = [i for i, g in enumerate(pgroups) if g[1] in ("k", "q", "v", "o", "gb")]
    stage_no = {i: s for s, i in enumerate(staged)}
    of_chunk = {j: [i for i, g in enumerate(pgroups) if g[0] == j] for j in range(-1, NCH)}
    KEYS_AT = [of_chunk[5][0] + 4 * i for i in range(NT)]
    STATE_AT = [g + 3 for g in KEYS_AT]
    after_v = [i for i in staged if pgroups[i][1] in ("k", "q", "v")]

    out = ExitStack()
    with out:
        def sem(name):
            return out.enter_context(nc.semaphore(name))

        def keep(name, shape, dt=F32):
            return out.enter_context(nc.sbuf_tensor(name, shape, dt))

        psum = out.enter_context(nc.psum_tensor("psum", [P, 8, 512], F32))

        ident = keep("ident", [P, P])
        colS = keep("colS", [P, 36, 40])
        small = keep("small", [P, 64])
        zrow = keep("zrow", [ROWS, 1])
        aff = keep("aff", [P, NT, NE])
        logit_max = keep("logit_max", [P, NT, 4])
        AFF = keep("AFF", [48, SS_])
        GV = keep("GV", [48, P])
        GI = keep("GI", [48, P], U32)
        GIF = keep("GIF", [48, P])
        GC = keep("GC", [P, 48])
        IDX = keep("IDX", [P, 48], U32)

        def stage_buffers(specs, *inner):
            got = {}
            with ExitStack() as s:
                for n, shape, dt in specs:
                    got[n] = s.enter_context(nc.sbuf_tensor(n, shape, dt))
                for part in inner:
                    with ExitStack() as t:
                        for n, shape, dt in part:
                            got[n] = t.enter_context(nc.sbuf_tensor(n, shape, dt))
            return got

        b = stage_buffers([
            ("hn_hi", [P, KD, T], F32R), ("hn_lo", [P, KD, T], F32R),
            ("wraw", [P, 2, KD, CH], F32), ("whi", [P, 2, KD, CH], F32R), ("wlo", [P, 2, KD, CH], F32R),
            ("stage", [P, NST, 512], F32),
            ("graw", [P, KD, 4 * H], F32), ("gbias", [P, 1], F32), ("cw", [P, 3, CW // P], F32),
            ("wg_hi", [P, KD, P], F32R), ("wg_lo", [P, KD, P], F32R), ("mst", [ROWS, NT], F32),
            ("st1", [P, 3, NT], F32)],
            [("xa", [P, NT, D], F32), ("g1", [P, D], F32), ("sq1", [P, D], F32)],
            [("R", [ROWS, 5, T], F32), ("GA", [P, T], F32), ("LI", [ROWS, T], F32), ("LF", [ROWS, T], F32),
             ("MM", [ROWS, T], F32), ("TM", [P, T], F32)],
            [("gcS", [P, 2, T], F32), ("CU", [P, 2, T + 4], F32), ("CV", [P, 2, T], F32),
             ("kT1", [P, 2, 2, 2, P], F32), ("v1", [P, 2, 2, H, VPAD], F32), ("wk", [P, 2, H, DK], F32),
             ("ST", [P, 2, 2, 2, VPAD], F32), ("dcb", [P, 2, 2, NT], F32)])
        d = stage_buffers([
            ("woh", [P, KD, D], F32R), ("wol", [P, KD, D], F32R),
            ("masks", [P, 2, P], F32), ("hgb", [P, VW], F32), ("g2b", [P, D], F32), ("wr", [P, KD, NE], F32),
            ("kTs", [P, 2, 2, P], F32), ("qz", [P, 2, H, P], F32), ("vs", [P, 2, H, VPAD], F32),
            ("og", [P, 2, VW], F32), ("negm", [P, 2, 2 * H, P], F32), ("inter", [P, 2, 4, P], F32),
            ("sts", [P, 2, 2, 2, VPAD], F32), ("cvs", [P, 2, CW // P, P], F32),
            ("X", [P, 2 * H, P], F32), ("E", [P, 2 * H, P], F32), ("SD", [P, 2 * H, P], F32),
            ("qs", [P, 2 * H, P], F32), ("hb", [P, H, DV], F32), ("ht", [P, H, DV], F32), ("junkh", [P, H, DV], F32),
            ("mix", [P, H, DV], F32), ("mxh", [P, 2, KD, P], F32R), ("mxl", [P, 2, KD, P], F32R),
            ("sm", [P, 2, 16], F32), ("ms", [P, 2, 3, H], F32), ("mt", [P, 2, 3, 1], F32)],
            [("woraw", [P, KD, D], F32)],
            [("xs", [P, 2, D], F32), ("x1", [P, 2, D], F32), ("tk", [P, 2, D], F32), ("tkT", [P, KD, P], F32),
             ("junk", [P, D], F32)])
        f = stage_buffers([
            ("eraw", [P, 6, KD, CH], F32), ("ehi", [P, 6, KD, CH], F32R), ("elo", [P, 6, KD, CH], BF16),
            ("xg", [P, D], F32), ("xgp", [CAPP, D], F32),
            ("xc", [P, 2, KD, 2, NC], F32R), ("xb", [P, 2, KD, NC], BF16),
            ("gu", [P, 2, 2, 2, NC], F32), ("sg", [P, 2, NC], F32), ("hid", [P, 2, NC], F32),
            ("hc", [P, KF, 2, NC], F32R), ("hbf", [P, KF, NC], BF16),
            ("ys", [P, 2, NC], F32), ("yt", [P, D], F32), ("yp", [CAPP, D], F32),
            ("idx", [P, 2, 2], U32), ("gcol", [P, 2], F32)])
        z = stage_buffers([("fx", [P, NT, D], F32), ("fq", [P, D], F32), ("gf", [P, D], F32),
                           ("fs", [P, 4, NT], F32)])

        S = {n: sem("s_" + n) for n in (
            "bar act_ch dve_ch pool_ch "
            "x_in0 x_in1 x_in2 g1_in const zeroed small_in sumsq xn_done xT_ps hn_hi hn_lo "
            "w_in0 w_in1 wg_hi wg_lo w_hi w_lo proj ev_act ev_dve st0 st1 st2 st3 "
            "soft rows_t rows_exp rows_nat rows_out colT_ps "
            "cst_in dcb_in col_done wo_in0 wo_in1 wo_hi wo_lo l1_0 l1_1 kT_ps wk_done u_ps st_upd st_out0 st_out1 "
            "ld0 ld1 ld_mix0 ld_mix1 ld_x0 ld_x1 padded qs_done s_ps x_done e_done sd_done num_ps den_done hb_done ht_done hsum og_done "
            "mix_done mixT_ps mxh_done mxl_done o_ps x1_done x1_out0 x1_out1 sum2 tk_done tk_out0 tk_out1 tkT_ps tkT_done "
            "lg_ps lgmax exps aff_done affT_ps AFF_done topk selT_ps sel_done "
            "er0 er1 er2 er3 er4 er5 ehi elo_dve elo_pool idx_cp gath exT_ps xc_hi xc_lo xb_done "
            "gu_ps gu_add sg_done hid_done hc_hi hc_lo hb_bf dn_ps ys_done yT_ps y_done scat settled "
            "gf_in f_in0 f_in1 f_in2 f_in3 f_in4 f_sum f_y f_out").split()}
        x_in = (S["x_in0"], S["x_in1"], S["x_in2"])
        w_ind, stg, l1, ld = (S["w_in0"], S["w_in1"]), (S["st0"], S["st1"], S["st2"], S["st3"]), (S["l1_0"], S["l1_1"]), (S["ld0"], S["ld1"])
        ld_mix, ld_x = (S["ld_mix0"], S["ld_mix1"]), (S["ld_x0"], S["ld_x1"])
        wo_in, st_out = (S["wo_in0"], S["wo_in1"]), (S["st_out0"], S["st_out1"])
        x1_out, tk_out = (S["x1_out0"], S["x1_out1"]), (S["tk_out0"], S["tk_out1"])
        er = (S["er0"], S["er1"], S["er2"], S["er3"], S["er4"], S["er5"])
        f_in = (S["f_in0"], S["f_in1"], S["f_in2"], S["f_in3"], S["f_in4"])

        def barrier(eng, k):
            eng.drain().then_inc(S["bar"], 1)
            eng.wait_ge(S["bar"], 5 * k)

        def rows_of(row):
            return row.partition_broadcast(P).rearrange("p a n -> p (a n)")

        seqs = [(0, NTP), (NTP, NT)]
        fwd = list(range(NT))
        bwd = [c for lo, hi in seqs for c in range(hi - 1, lo - 1, -1)]
        starts = [lo for lo, _ in seqs]

        def natural(ap2, lo, hi):
            return ap2[:, lo * P:hi * P]

        def reverse(ap2, lo, hi):
            return ap2[:, hi * P - 1:lo * P - 1:-1] if lo else ap2[:, hi * P - 1::-1]

        ORDER = list(range(NTP, NT)) + list(range(NTP))
        NS = NT - NTP

        def tokens_of(n):
            return slice(ORDER[n] * P, (ORDER[n] + 1) * P)

        TG = ((0, 3), (3, 3), (6, 2))
        NLD = 8

        def colslot(c, q):
            return 3 * c + q

        NB = 12
        RING = 6
        BY_POOL = [3, 7, 11]
        BY_DVE = [j for j in range(NB) if j not in BY_POOL]

        def wait_split(eng, e, j):
            mine, s = (BY_POOL, S["elo_pool"]) if j in BY_POOL else (BY_DVE, S["elo_dve"])
            eng.wait_ge(s, len(mine) * (e + 1) + mine.index(j) + 1)

        def wait_slot(eng, e, j):
            before = (j + RING) % NB
            mine, s = (BY_POOL, S["elo_pool"]) if before in BY_POOL else (BY_DVE, S["elo_dve"])
            eng.wait_ge(s, len(mine) * (e if j < RING else e + 1) + mine.index(before) + 1)

        block = out.enter_context(nc.Block())

        @block.sync
        def _(sp):
            for i, (lo, hi) in enumerate(BATCHES):
                for n in range(lo, hi):
                    sp.dma_start(b["xa"][:, n, :], x_chunk[n]).then_inc(x_in[i], 16)
                if i == 0:
                    sp.dma_start(b["g1"][:, :], rows_of(norm1_g)).then_inc(S["g1_in"], 16)
                    sp.wait_ge(S["zeroed"], 1)
                    with nc.allow_non_contiguous_dma(reason="gate columns, biases and taps"):
                        sp.dma_start(b["graw"][:, :, :], w_in[0, :, c_gates:c_gates + 4 * H]
                                     .rearrange("(k p) n -> p k n", p=P)).then_inc(S["small_in"], 16)
                        for row, g in ((0, 0), (32, 2), (64, 1), (96, 3)):
                            sp.dma_start(b["gbias"][row:row + H, 0:1], gate_bias[0, g, :]
                                         .rearrange("(h a) -> h a", a=1)).then_inc(S["small_in"], 16)
                        for k in range(3):
                            sp.dma_start(b["cw"][:, k, :], conv_w[0, k, :].rearrange("(c p) -> p c", p=P)
                                         ).then_inc(S["small_in"], 16)

            def load_state_step(i):
                if i == 0:
                    sp.wait_ge(S["colT_ps"], 3)
                    sp.wait_ge(S["rows_out"], 16 * 6)
                    for q in range(NST):
                        sp.wait_ge(stg[q], 16 * len([g for g in after_v if stage_no[g] % NST == q]))
                    with nc.allow_non_contiguous_dma(reason="decays by head"):
                        for half in range(2):
                            for dr in range(2):
                                for pr in range(2):
                                    r = 4 * dr + 2 * pr + half
                                    sp.dma_start(b["dcb"][64 * half:64 * half + 64, dr, pr, :],
                                                 decay_d[r:r + 1, :].partition_broadcast(64)
                                                 .rearrange("p a n -> p (a n)")).then_inc(S["dcb_in"], 16)
                if i >= 2:
                    sp.wait_ge(S["u_ps"], i - 1)
                for dr, c in ((0, fwd[i]), (1, bwd[i])):
                    t = slice(c * P, (c + 1) * P)
                    sp.dma_start(b["kT1"][:, i % 2, dr, :, :], qk_d[2:4, :, t].rearrange("r p t -> p r t")
                                 ).then_inc(l1[i % 2], 16)
                    sp.dma_start(b["v1"][:, i % 2, dr, :, 0:DV], v_d[t, :].rearrange("t (h n) -> t h n", h=H)
                                 ).then_inc(l1[i % 2], 16)

            step_after = [5, 5] + [pgroups[g][0] + 1 for g in STATE_AT[:NT - 2]]
            for j in range(NCH + 1):
                for i in range(NT):
                    if step_after[i] == j - 1:
                        load_state_step(i)
                if j < NCH:
                    if j >= 2:
                        sp.wait_ge(S["w_lo"], j - 1)
                    col = chunks[j][1]
                    sp.dma_start(b["wraw"][:, j % 2, :, :], w_in[0, :, col:col + CH]
                                 .rearrange("(k p) n -> p k n", p=P)).then_inc(w_ind[j % 2], 16)
            barrier(sp, 1)

            def load_scan(n):
                s, t = n % 2, tokens_of(n)
                if n >= 2:
                    sp.wait_ge(S["num_ps"], n - 1)
                sp.dma_start(d["kTs"][:, s, :, :], qk_d[2:4, :, t].rearrange("r p t -> p r t")).then_inc(ld[s], 16)
                for half in range(2):
                    rows = slice(64 * half, 64 * half + 64)
                    sp.dma_start(d["qz"][rows, s, half::2, :], qk_d[0:2, rows, t].rearrange("r p t -> p r t")
                                 ).then_inc(ld[s], 16)
                    sp.dma_start(d["inter"][rows, s, :, :], inter_d.rearrange("(r a) t -> a r t", a=2)[half, :, t]
                                 .partition_broadcast(64)).then_inc(ld[s], 16)
                sp.dma_start(d["negm"][:, s, :, :], negm_d[:, t].partition_broadcast(P)).then_inc(ld[s], 16)
                sp.dma_start(d["vs"][:, s, :, 0:DV], v_d[t, :].rearrange("t (h n) -> t h n", h=H)).then_inc(ld[s], 16)
                sp.dma_start(d["sts"][:, s, :, :, :], state_d[ORDER[n]]).then_inc(ld[s], 16)

            def load_mix(n):
                s, t = n % 2, tokens_of(n)
                if n >= 2:
                    sp.wait_ge(S["mxl_done"], n - 1)
                sp.dma_start(d["og"][:, s, :], o_d[t, :]).then_inc(ld_mix[s], 16)
                sp.dma_start(d["cvs"][:, s, :, :], conv_d[:, :, t].rearrange("r p t -> p r t")).then_inc(ld_mix[s], 16)

            def load_x(n):
                if n >= 2:
                    sp.wait_ge(S["x1_done"], 2 * (n - 1))
                sp.dma_start(d["xs"][:, n % 2, :], x_chunk[ORDER[n]]).then_inc(ld_x[n % 2], 16)

            sp.wait_ge(S["padded"], 1)
            load_scan(0)
            load_mix(0)
            with nc.allow_non_contiguous_dma(reason="router columns"):
                sp.dma_start(d["wr"][:, :, :], w_router[0].rearrange("(k p) n -> p k n", p=P)).then_inc(S["cst_in"], 16)
            sp.dma_start(d["hgb"][:, :], rows_of(head_norm_g)).then_inc(S["cst_in"], 16)
            sp.dma_start(d["g2b"][:, :], rows_of(norm2_g)).then_inc(S["cst_in"], 16)
            for h in range(2):
                sp.dma_start(d["woraw"][:, 4 * h:4 * h + 4, :], w_out[0, 512 * h:512 * h + 512, :]
                             .rearrange("(k p) n -> p k n", p=P)).then_inc(wo_in[h], 16)
                if h == 0:
                    load_scan(1)
            for n in range(1, NT + 1):
                if 1 < n < NT:
                    load_scan(n)
                if n == 1:
                    sp.wait_ge(S["wo_lo"], KD)
                load_x(n - 1)
                if n < NT:
                    load_mix(n)
            barrier(sp, 2)

            with sp.Fori(0, NE) as e:
                for j in range(NB):
                    wait_slot(sp, e, j)
                    w = (w_gate, w_up)[j % 2] if j < 8 else w_down
                    i = j // 2 if j < 8 else j - 8
                    src = w[0, bass.ds(e, 1), :, i * CH:(i + 1) * CH].rearrange("a (k p) n -> p (a k) n", p=P)
                    sp.dma_start(f["eraw"][:, j % RING, :, :], src).then_inc(er[j % RING], 16)
            barrier(sp, 3)
            sp.dma_start(z["gf"][:, :], rows_of(final_g.rearrange("(a d) -> a d", a=1))).then_inc(S["gf_in"], 16)
            for n in range(NT):
                sp.dma_start(z["fx"][:, n, :], acc_d[n * P:(n + 1) * P, :]).then_inc(f_in[n // 2], 16)
            for n in range(NT):
                sp.wait_ge(S["f_y"], n + 1)
                sp.dma_start(y_chunk[n], z["fx"][:, n, :]).then_inc(S["f_out"], 16)
            sp.wait_ge(S["f_out"], 16 * NT)

        @block.gpsimd
        def _(pool):
            ch = Chain(pool, S["pool_ch"])
            ch(pool.memset(ident[:, :], 0.0))
            pool.affine_select(out=ident[:, :], in_=ident[:, :], compare_op=ALU.not_equal, fill=1.0, base=0,
                               pattern=[[-1, P]], channel_multiplier=1).then_inc(S["const"], 1)
            pool.memset(b["gbias"][:, :], 0.0).then_inc(S["zeroed"], 1)
            ch(pool.memset(zrow[:, :], 0.0))
            pool.memset(b["wg_hi"][:, :, :].bitcast(F32), 0.0).then_inc(S["zeroed"], 1)
            pool.memset(b["wg_lo"][:, :, :].bitcast(F32), 0.0).then_inc(S["zeroed"], 1)
            pool.wait_ge(S["hn_lo"], NT)
            pool.memset(b["R"][:, :, :], 0.0).then_inc(S["zeroed"], 1)
            pool.memset(b["LF"][:, :], 0.0).then_inc(S["zeroed"], 1)
            pool.memset(b["LI"][:, :], 0.0).then_inc(S["zeroed"], 1)

            def store_group(i):
                _, kind, part, m, t0, w = pgroups[i]
                s = stage_no[i] % NST
                who, n = ev_at[i]
                pool.wait_ge(S["ev_act"] if who == "act" else S["ev_dve"], n)
                if kind in ("k", "q"):
                    dst = qk_d[(2 if kind == "k" else 0) + m, :, t0:t0 + w]
                elif kind in ("v", "o"):
                    dst = (v_d if kind == "v" else o_d)[m * P:(m + 1) * P, part * CH:(part + 1) * CH]
                else:
                    dst = conv_d[2 * part + m, :, t0:t0 + w]
                pool.dma_start(dst, b["stage"][:, s, 0:w]).then_inc(stg[s], 16)
                if i == of_chunk[1][-1]:
                    pool.wait_ge(S["rows_nat"], 1)
                    pool.wait_ge(S["rows_exp"], 9)
                    with nc.allow_non_contiguous_dma(reason="one decay a chunk"):
                        for dr in range(2):
                            rows, dst = slice(32 * dr, 32 * dr + H), slice(4 * dr, 4 * dr + 4)
                            pool.dma_start(negm_d[dst, :], b["R"][rows, 4, :]).then_inc(S["rows_out"], 16)
                            pool.dma_start(inter_d[dst, :], b["R"][rows, 3, :]).then_inc(S["rows_out"], 16)
                            last = (P - 1, 0)[dr]
                            pool.dma_start(decay_d[dst, :], b["R"][rows, 3, last::P][:, 0:NT]).then_inc(S["rows_out"], 16)

            def store_state(i):
                pool.wait_ge(S["st_upd"], i + 1)
                for dr, c in ((0, fwd[i]), (1, bwd[i])):
                    pool.dma_start(state_d[c, :, dr, :], b["ST"][:, i % 2, dr, :, :].rearrange("p a n -> p (a n)")
                                   ).then_inc(st_out[i % 2], 16)

            at = [(i, 1, store_group, i) for i in staged] + \
                 [(KEYS_AT[0] if i == 0 else STATE_AT[i - 1], 0, store_state, i) for i in range(NT)]
            for _, _, store, i in sorted(at, key=lambda a: a[:2]):
                store(i)
            for s in range(2):
                pool.wait_ge(st_out[s], 32 * (NT // 2))
            for s in range(NST):
                pool.wait_ge(stg[s], 16 * len([i for i in staged if stage_no[i] % NST == s]))
            barrier(pool, 1)

            ch(pool.memset(d["masks"][:, :, :], 0.0))
            ch(pool.affine_select(out=d["masks"][:, 0, :], in_=d["masks"][:, 0, :], compare_op=ALU.is_ge, fill=NEG,
                                  base=0, pattern=[[1, P]], channel_multiplier=-1))
            ch(pool.affine_select(out=d["masks"][:, 1, :], in_=d["masks"][:, 1, :], compare_op=ALU.is_ge, fill=NEG,
                                  base=0, pattern=[[-1, P]], channel_multiplier=1))
            pool.memset(d["qz"][:, :, :, :], 0.0).then_inc(S["padded"], 1)

            def scale_queries(n):
                s = n % 2
                pool.wait_ge(ld[s], 16 * NLD * (n // 2 + 1))
                if n >= 1:
                    pool.wait_ge(S["num_ps"], n)
                for dr in range(2):
                    for half in range(2):
                        q = pool.tensor_tensor(d["qs"][:, H * dr + half:H * dr + H:2, :], d["qz"][:, s, half::2, :],
                                               d["inter"][:, s, 2 * dr:2 * dr + 2, :], ALU.mult)
                q.then_inc(S["qs_done"], 1)
                pool.wait_ge(ld_mix[s], 16 * 2 * (n // 2 + 1))
                if n == 0:
                    pool.wait_ge(S["cst_in"], 16 * 3)
                pool.tensor_tensor(d["og"][:, s, :], d["og"][:, s, :], d["hgb"][:, :], ALU.mult
                                   ).then_inc(S["og_done"], 1)

            scale_queries(0)
            for n in range(NT + 1):
                if n + 1 < NT:
                    scale_queries(n + 1)
                if n >= 1:
                    m = n - 1
                    t = tokens_of(m)
                    pool.wait_ge(S["x1_done"], 2 * (m + 1))
                    pool.dma_start(acc_d[t, :], d["x1"][:, m % 2, :]).then_inc(x1_out[m % 2], 16)
                    pool.wait_ge(S["tk_done"], m + 1)
                    pool.dma_start(tok_d[t, :], d["tk"][:, m % 2, :]).then_inc(tk_out[m % 2], 16)
            for s in range(2):
                pool.wait_ge(x1_out[s], 16 * (NT // 2))
                pool.wait_ge(tk_out[s], 16 * (NT // 2))
            barrier(pool, 2)

            for s, credit in ((S["dn_ps"], 8), (S["gu_add"], 2), (S["ys_done"], 2), (S["yT_ps"], 2), (S["hid_done"], 1), (S["hb_bf"], 1), (S["y_done"], 2),
                              (S["elo_dve"], len(BY_DVE)), (S["elo_pool"], len(BY_POOL))):
                pool.sem_inc(s, credit)

            def settle():
                pool.sem_inc(S["settled"], 1)

            def gather(e, copied):
                pool.tensor_copy(f["idx"][:, 0, 0:1], IDX[:, bass.ds(e, 1)]).then_inc(S["idx_cp"], 1)
                pool.tensor_copy(f["idx"][0:CAPP, 1, 0:1], IDX[0:CAPP, bass.ds(e + 32, 1)]).then_inc(S["idx_cp"], 1)
                pool.wait_ge(S["idx_cp"], copied + 2)
                settle()
                pool.indirect_dma_start(f["xg"][:, :], None, tok_d, bass.IndirectOffsetOnAxis(ap=f["idx"][:, 0, 0:1], axis=0)
                                        ).then_inc(S["gath"], 16)
                pool.indirect_dma_start(f["xgp"][:, :], None, tok_d,
                                        bass.IndirectOffsetOnAxis(ap=f["idx"][0:CAPP, 1, 0:1], axis=0)
                                        ).then_inc(S["gath"], 16)

            def split_low(e, j):
                pool.wait_ge(S["ehi"], NB * e + j + 1)
                pool.tensor_tensor(f["elo"][:, j % RING, :, :], f["eraw"][:, j % RING, :, :],
                                   f["ehi"][:, j % RING, :, :].bitcast(F32),
                                   ALU.subtract).then_inc(S["elo_pool" if j in BY_POOL else "elo_dve"], 1)

            def scatter(e):
                pool.wait_ge(S["y_done"], 2 + 2 * e + 2)
                settle()
                pool.indirect_dma_start(acc_d, bass.IndirectOffsetOnAxis(ap=f["idx"][:, 0, 1:2], axis=0),
                                        f["yt"][:, :], None, compute_op=ALU.add).then_inc(S["scat"], 16)
                pool.indirect_dma_start(acc_d, bass.IndirectOffsetOnAxis(ap=f["idx"][0:CAPP, 1, 1:2], axis=0),
                                        f["yp"][:, :], None, compute_op=ALU.add).then_inc(S["scat"], 16)

            for j in range(4):
                split_low(0, j)
            pool.wait_ge(S["sel_done"], 3)
            settle()
            gather(0, 0)

            def expert(e, s, first=False, last=False):
                if not last:
                    pool.wait_ge(S["exT_ps"], 3 * e + 3)
                    settle()
                    gather(e + 1, 2 + 6 * e)
                if not first:
                    scatter(e - 1)
                for p in range(4):
                    pool.wait_ge(S["sg_done"], 4 * e + p + 1)
                    pool.wait_ge(S["hc_lo"], 4 + 4 * e + p)
                    pool.wait_ge(S["hb_bf"], 1 + 4 * e + p)
                    pool.tensor_tensor(f["hid"][:, :, :], f["sg"][:, :, :], f["gu"][:, p % 2, :, 1, :], ALU.mult
                                       ).then_inc(S["hid_done"], 1)
                    if p == 1:
                        split_low(e, 7)
                split_low(e, 11)
                pool.wait_ge(S["y_done"], 2 * e + 2)
                if not first:
                    pool.wait_ge(S["scat"], 32 * e)
                settle()
                pool.tensor_copy(f["idx"][:, 0, 1:2], IDX[:, bass.ds(e, 1)]).then_inc(S["idx_cp"], 1)
                pool.tensor_copy(f["idx"][0:CAPP, 1, 1:2], IDX[0:CAPP, bass.ds(e + 32, 1)]).then_inc(S["idx_cp"], 1)
                pool.tensor_copy(f["gcol"][:, 0:1], GC[:, bass.ds(e, 1)]).then_inc(S["idx_cp"], 1)
                pool.tensor_copy(f["gcol"][0:CAPP, 1:2], GC[0:CAPP, bass.ds(e + 32, 1)]).then_inc(S["idx_cp"], 1)
                pool.wait_ge(S["idx_cp"], 2 + 6 * e + (4 if last else 6))
                if not last:
                    split_low(e + 1, 3)

            expert(0, 0, first=True)
            with pool.Fori(0, NE // 2 - 1) as g:
                expert(2 * g + 1, 1)
                expert(2 * g + 2, 0)
            expert(NE - 1, 1, last=True)
            scatter(NE - 1)
            pool.wait_ge(S["scat"], 32 * NE)
            barrier(pool, 3)

        @block.scalar
        def _(act):
            ch = Chain(act, S["act_ch"])

            def tokens_high(n):
                act.wait_ge(S["xT_ps"], n + 1)
                act.activation(b["hn_hi"][:, :, n * P:(n + 1) * P], psum[:, 2 * (n % 2):2 * (n % 2) + 2, :]
                               .rearrange("p a (k t) -> p (a k) t", k=4), ACT.Copy).then_inc(S["hn_hi"], 1)

            for i, (lo, hi) in enumerate(BATCHES):
                act.wait_ge(x_in[i], 16 * (hi - lo))
                for n in range(lo, hi):
                    if n >= 1:
                        act.wait_ge(S["sumsq"], n)
                    act.activation(b["sq1"][:, :], b["xa"][:, n, :], ACT.Square, scale=D ** -0.5,
                                   accum_out=b["st1"][:, 0, n:n + 1]).then_inc(S["sumsq"], 1)
                for n in range(*BATCHES[i - 1]) if i else ():
                    tokens_high(n)
                if i == 1:
                    act.wait_ge(S["small_in"], 16 * 8)
                    act.wait_ge(S["zeroed"], 3)
                    for row, g in ((0, 0), (32, 2), (64, 1), (96, 3)):
                        i = act.activation(b["wg_hi"][:, :, row:row + H], b["graw"][:, :, g * H:(g + 1) * H], ACT.Copy)
                    i.then_inc(S["wg_hi"], 1)
            for n in range(*BATCHES[-1]):
                tokens_high(n)

            def split_high(j):
                act.wait_ge(w_ind[j % 2], 16 * (j // 2 + 1))
                if j >= 2:
                    act.wait_ge(S["proj"], of_chunk[j - 2][-1] + 1)
                act.activation(b["whi"][:, j % 2, :, :], b["wraw"][:, j % 2, :, :], ACT.Copy).then_inc(S["w_hi"], 1)

            split_high(0)
            done = 0
            for j in range(-1, NCH):
                if 0 <= j < NCH - 1:
                    split_high(j + 1)
                for i in of_chunk[j]:
                    _, kind, part, m, t0, w = pgroups[i]
                    if kind in EV_DVE:
                        continue
                    act.wait_ge(S["proj"], i + 1)
                    src = psum[:, 4 + i % 4, 0:w]
                    if kind in ("k", "q", "v", "o"):
                        s = stage_no[i]
                        if s >= NST:
                            act.wait_ge(stg[s % NST], 16 * (s // NST))
                        dst = b["stage"][:, s % NST, 0:w]
                    if kind == "gate":
                        if i == 0:
                            act.wait_ge(S["hn_lo"], NT)
                        e = act.activation(b["GA"][0:GATE_ROWS, t0:t0 + w], psum[0:GATE_ROWS, 4 + i % 4, 0:w],
                                           ACT.Identity, bias=b["gbias"][0:GATE_ROWS, 0:1])
                    elif kind == "q":
                        e = act.activation(dst, src, ACT.Copy, scale=DK ** -0.5)
                    elif kind == "o":
                        e = act.activation(dst, src, ACT.Sigmoid)
                    elif kind == "gc":
                        if part == 0 and m == 0 and t0 == 0:
                            act.wait_ge(S["colT_ps"], 3)
                            act.wait_ge(S["rows_out"], 16 * 6)
                        if part > 0:
                            act.wait_ge(S["ev_dve"], ev_at[of_chunk[j - 2][-1]][1])
                        e = act.activation(b["gcS"][:, m, t0:t0 + w], src, ACT.Copy)
                    else:
                        e = act.activation(dst, src, ACT.Copy)
                    e.then_inc(S["ev_act"], 1)
                    done += 1
                if j == -1:
                    act.wait_ge(S["ev_act"], 3)
                    r = slice(64, GATE_ROWS)
                    ch(act.activation(b["TM"][r, :], b["GA"][r, :], ACT.Abs))
                    ch(act.activation(b["TM"][r, :], b["TM"][r, :], ACT.Exp, scale=-1.0))
                    act.activation(b["TM"][r, :], b["TM"][r, :], ACT.Ln, bias=1.0).then_inc(S["soft"], 1)
                if j == 0:
                    act.wait_ge(S["zeroed"], 4)
                    for k, (q, src, scale) in enumerate(((1, b["GA"], 1.0), (3, b["LI"], 1.0), (2, b["LF"], -1.0))):
                        act.wait_ge(S["rows_t"], k + 1)
                        act.activation(b["R"][0:H, q, :], src[0:H, :], ACT.Exp, scale=scale).then_inc(S["rows_exp"], 1)
                        for lo, hi in seqs:
                            act.activation(reverse(b["R"][32:32 + H, q, :], lo, hi), natural(src[32:32 + H, :], lo, hi),
                                           ACT.Exp, scale=scale).then_inc(S["rows_exp"], 1)
                if j == 1:
                    for k in range(3):
                        act.wait_ge(S["colT_ps"], k + 1)
                        n = min(12, 3 * NT - 12 * k)
                        act.activation(colS[:, 12 * k:12 * k + n, 0:ROWS],
                                       psum[:, k, 0:480].rearrange("p (a c) -> p a c", c=40)[:, 0:n, 0:ROWS], ACT.Copy
                                       ).then_inc(S["col_done"], 1)
            barrier(act, 1)

            def exponentials(n):
                act.wait_ge(S["x_done"], n + 1)
                if n >= 1:
                    act.wait_ge(S["sd_done"], n)
                act.activation(d["E"][:, :, :], d["X"][:, :, :], ACT.Exp).then_inc(S["e_done"], 1)

            def out_high(h):
                act.wait_ge(wo_in[h], 16)
                for k in range(4 * h, 4 * h + 4):
                    act.activation(d["woh"][:, k, :], d["woraw"][:, k, :], ACT.Copy).then_inc(S["wo_hi"], 1)

            exponentials(0)
            out_high(0)
            for n in range(NT + 2):
                if n < NT:
                    act.wait_ge(S["den_done"], n + 1)
                    if n >= 1:
                        act.wait_ge(S["ht_done"], n)
                    for h in range(H):
                        i = act.activation(d["hb"][:, h, :], psum[:, 3 + h // 2, VPAD * (h % 2):VPAD * (h % 2) + DV],
                                           ACT.Copy, scale=d["sm"][:, n % 2, 4 + h:5 + h])
                    i.then_inc(S["hb_done"], 1)
                    if n + 1 < NT:
                        exponentials(n + 1)
                    act.wait_ge(S["ht_done"], n + 1)
                    if n >= 1:
                        act.wait_ge(S["hsum"], n)
                    for h in range(H):
                        i = act.activation(d["junkh"][:, h, :], d["ht"][:, h, :], ACT.Square, scale=DV ** -0.5,
                                           accum_out=d["ms"][:, n % 2, 0, h:h + 1])
                    i.then_inc(S["hsum"], 1)
                    if n == 0:
                        out_high(1)
                    act.wait_ge(ld_mix[n % 2], 16 * 2 * (n // 2 + 1))
                    if n >= 2:
                        act.wait_ge(S["o_ps"], 2 * (n - 1))
                    act.activation(d["mxh"][:, n % 2, 0:4, :], d["cvs"][:, n % 2, :, :], ACT.Copy
                                   ).then_inc(S["mxh_done"], 1)
                if n >= 2:
                    act.wait_ge(S["tkT_ps"], n - 1)
                    if n >= 3:
                        act.wait_ge(S["lg_ps"], n - 2)
                    act.activation(d["tkT"][:, :, :], psum[:, 1:3, :].rearrange("p a (k t) -> p (a k) t", k=4),
                                   ACT.Copy).then_inc(S["tkT_done"], 1)
                if 1 <= n <= NT:
                    m = n - 1
                    act.wait_ge(S["x1_done"], 2 * (m + 1))
                    if m >= 1:
                        act.wait_ge(S["sum2"], m)
                    act.activation(d["junk"][:, :], d["x1"][:, m % 2, :], ACT.Square, scale=D ** -0.5,
                                   accum_out=d["mt"][:, m % 2, 0, :]).then_inc(S["sum2"], 1)
                if n < NT:
                    act.wait_ge(S["mixT_ps"], n + 1)
                    act.activation(d["mxh"][:, n % 2, 4:8, :], psum[:, 5, :].rearrange("p (k t) -> p k t", k=4),
                                   ACT.Copy).then_inc(S["mxh_done"], 1)
                if n >= 2:
                    m = n - 2
                    act.wait_ge(S["lgmax"], m + 1)
                    act.activation(aff[:, m, :], psum[:, 3, 0:NE], ACT.Exp, bias=logit_max[:, m, 0:1],
                                   accum_out=logit_max[:, m, 1:2]).then_inc(S["exps"], 1)
            barrier(act, 2)

            def high(e, j, first=False):
                act.wait_ge(er[j % RING], 16 * (2 * e + j // RING + 1))
                if not first:
                    if j < 2:
                        act.wait_ge(S["gu_ps"], 8 * e)
                    elif j < RING:
                        act.wait_ge(S["dn_ps"], 8 * e + 2 * (j - 2) + 2)
                    else:
                        act.wait_ge(S["gu_ps"], 8 * e + 2 * ((j - RING) // 2) + 2)
                act.activation(f["ehi"][:, j % RING, :, :], f["eraw"][:, j % RING, :, :], ACT.Copy
                               ).then_inc(S["ehi"], 1)

            def narrow_tokens(e, s):
                act.wait_ge(S["xc_hi"], 3 * e + 3)
                act.activation(f["xb"][:, s, :, :], f["xc"][:, s, :, 0, :].bitcast(F32), ACT.Copy
                               ).then_inc(S["xb_done"], 1)

            def tokens_high(e, s, which):
                for g in which:
                    k0, nk = TG[g]
                    act.wait_ge(S["exT_ps"], 3 * e + g + 1)
                    act.activation(f["xc"][:, s, k0:k0 + nk, 0, :], psum[:, 6 + g % 2, 0:nk * NC]
                                   .rearrange("p (k t) -> p k t", k=nk), ACT.Copy).then_inc(S["xc_hi"], 1)

            def y_half(e, h, first=False, last=False):
                act.wait_ge(S["yT_ps"], 2 + 8 * e + 4 * h + 4)
                act.wait_ge(S["idx_cp"], 2 + 6 * e + (4 if last else 6))
                if not first:
                    act.wait_ge(S["scat"], 32 * e)
                act.activation(f["yt"][:, 512 * h:512 * h + 512], psum[:, 6, :], ACT.Copy, scale=f["gcol"][:, 0:1])
                act.activation(f["yp"][:, 512 * h:512 * h + 512], psum[0:CAPP, 7, :], ACT.Copy,
                               scale=f["gcol"][0:CAPP, 1:2]).then_inc(S["y_done"], 1)

            for j in range(RING):
                high(0, j, True)
            tokens_high(0, 0, (0, 1, 2))
            narrow_tokens(0, 0)

            def expert(e, s, first=False, last=False):
                if not first:
                    y_half(e - 1, 1)
                for p in range(4):
                    act.wait_ge(S["gu_add"], 2 + 8 * e + 2 * p + 2)
                    act.wait_ge(S["hid_done"], 1 + 4 * e + p)
                    act.activation(f["sg"][:, :, :], f["gu"][:, p % 2, :, 0, :], ACT.Silu).then_inc(S["sg_done"], 1)
                    if p < 3:
                        high(e, 2 * p + 6)
                    if p in (1, 2) and not last:
                        tokens_high(e + 1, 1 - s, ((0, 1), (2,))[p - 1])
                    act.wait_ge(S["hid_done"], 1 + 4 * e + p + 1)
                    if p == 0:
                        act.wait_ge(S["dn_ps"], 8 * e + 8)
                    act.activation(f["hc"][:, 2 * p:2 * p + 2, 0, :], f["hid"][:, :, :], ACT.Copy
                                   ).then_inc(S["hc_hi"], 1)
                    act.activation(f["hbf"][:, 2 * p:2 * p + 2, :], f["hid"][:, :, :], ACT.Copy
                                   ).then_inc(S["hb_bf"], 1)
                    if p < 3:
                        high(e, 2 * p + 7)
                    elif not last:
                        high(e + 1, 0)
                        high(e + 1, 1)
                    if p == 2 and not last:
                        narrow_tokens(e + 1, 1 - s)
                for q in range(4):
                    if not last:
                        high(e + 1, q + 2)
                    if q == 1:
                        y_half(e, 0, first, last)

            expert(0, 0, first=True)
            with act.Fori(0, NE // 2 - 1) as g:
                expert(2 * g + 1, 1)
                expert(2 * g + 2, 0)
            expert(NE - 1, 1, last=True)
            y_half(NE - 1, 1, last=True)
            barrier(act, 3)

            for n in range(NT):
                act.wait_ge(f_in[n // 2], 16 * 2)
                if n >= 1:
                    act.wait_ge(S["f_sum"], n)
                act.activation(z["fq"][:, :], z["fx"][:, n, :], ACT.Square, scale=D ** -0.5,
                               accum_out=z["fs"][:, 0, n:n + 1]).then_inc(S["f_sum"], 1)

        @block.vector
        def _(dve):
            ch = Chain(dve, S["dve_ch"])

            def inverse_root(r, v, t):
                ch(dve.tensor_scalar(v, v, EPS, None, ALU.add))
                ch(dve.tensor_scalar(r.bitcast(U32), v.bitcast(U32), -0.5, float(0x5f3759df), ALU.mult, ALU.add))
                c = 1.0
                for _ in range(3):
                    ch(dve.tensor_tensor(t, r, r, ALU.mult))
                    ch(dve.tensor_tensor(t, t, v, ALU.mult))
                    ch(dve.scalar_tensor_tensor(r, t, -3.0 * c * c, r, ALU.add, ALU.mult))
                    c = -2.0 * c ** 3
                ch(dve.tensor_scalar(r, r, 1.0 / c, None, ALU.mult))

            def tokens_low(n):
                dve.wait_ge(S["hn_hi"], n + 1)
                dve.tensor_tensor(b["hn_lo"][:, :, n * P:(n + 1) * P], psum[:, 2 * (n % 2):2 * (n % 2) + 2, :]
                                  .rearrange("p a (k t) -> p (a k) t", k=4),
                                  b["hn_hi"][:, :, n * P:(n + 1) * P].bitcast(F32), ALU.subtract
                                  ).then_inc(S["hn_lo"], 1)

            for i, (lo, hi) in enumerate(BATCHES):
                dve.wait_ge(S["sumsq"], hi)
                inverse_root(b["st1"][:, 1, lo:hi], b["st1"][:, 0, lo:hi], b["st1"][:, 2, lo:hi])
                dve.wait_ge(S["g1_in"], 16)
                for n in range(lo, hi):
                    dve.scalar_tensor_tensor(b["xa"][:, n, :], b["xa"][:, n, :], b["st1"][:, 1, n:n + 1], b["g1"][:, :],
                                             ALU.mult, ALU.mult).then_inc(S["xn_done"], 1)
                for n in range(*BATCHES[i - 1]) if i else ():
                    tokens_low(n)
                if i == 1:
                    dve.wait_ge(S["wg_hi"], 1)
                    for row, g in ((0, 0), (32, 2), (64, 1), (96, 3)):
                        i = dve.tensor_tensor(b["wg_lo"][:, :, row:row + H], b["graw"][:, :, g * H:(g + 1) * H],
                                              b["wg_hi"][:, :, row:row + H].bitcast(F32), ALU.subtract)
                    i.then_inc(S["wg_lo"], 1)
            for n in range(*BATCHES[-1]):
                tokens_low(n)

            def split_low(j):
                dve.wait_ge(S["w_hi"], j + 1)
                dve.tensor_tensor(b["wlo"][:, j % 2, :, :], b["wraw"][:, j % 2, :, :],
                                  b["whi"][:, j % 2, :, :].bitcast(F32), ALU.subtract).then_inc(S["w_lo"], 1)

            def last_col(t2, c):
                return t2[0:ROWS, (c + 1) * P - 1:(c + 1) * P]

            def by_chunk(t2):
                return t2[0:ROWS, :].rearrange("r (c t) -> r c t", t=P)

            def gate_rows():
                dve.wait_ge(S["zeroed"], 6)
                dve.wait_ge(S["soft"], 1)
                r = slice(64, GATE_ROWS)
                ch(dve.scalar_tensor_tensor(b["GA"][r, :], b["GA"][r, :], 0.0, b["TM"][r, :], ALU.min, ALU.subtract))
                dve.tensor_copy(b["LF"][0:H, :], b["GA"][64:64 + H, :])
                dve.tensor_copy(b["LI"][0:H, :], b["GA"][0:H, :])
                for lo, hi in seqs:
                    dve.tensor_copy(natural(b["LF"][32:32 + H, :], lo, hi), reverse(b["GA"][96:96 + H, :], lo, hi))
                    i = dve.tensor_copy(natural(b["LI"][32:32 + H, :], lo, hi), reverse(b["GA"][32:32 + H, :], lo, hi))
                ch(i)
                zero = zrow[:, 0:1].to_broadcast([ROWS, P])
                for c in range(NT):
                    t = slice(c * P, (c + 1) * P)
                    i = dve.tensor_tensor_scan(b["LF"][:, t], b["LF"][:, t], zero, 0.0, ALU.add, ALU.add)
                ch(i)
                ch(dve.tensor_tensor(b["LI"][:, :], b["LI"][:, :], b["LF"][:, :], ALU.subtract))
                for c in range(NT):
                    t = slice(c * P, (c + 1) * P)
                    if c in starts:
                        ch(dve.memset(b["mst"][:, c:c + 1], 0.0))
                    else:
                        ch(dve.tensor_tensor(b["mst"][:, c:c + 1], last_col(b["MM"], c - 1), last_col(b["LF"], c - 1), ALU.add))
                    ch(dve.tensor_tensor_scan(b["MM"][:, t], b["LI"][:, t], zero, b["mst"][:, c:c + 1], ALU.max, ALU.add))
                ends = by_chunk(b["MM"])[:, :, P - 1:P].to_broadcast([ROWS, NT, P])
                dve.tensor_tensor(by_chunk(b["GA"]), by_chunk(b["LI"]), ends, ALU.subtract).then_inc(S["rows_t"], 1)
                dve.tensor_copy(b["R"][0:H, 0, :], b["LI"][0:H, :])
                dve.tensor_scalar(b["R"][0:H, 4, :], b["MM"][0:H, :], -1.0, None, ALU.mult)
                for lo, hi in seqs:
                    dve.tensor_copy(reverse(b["R"][32:32 + H, 0, :], lo, hi), natural(b["LI"][32:32 + H, :], lo, hi))
                    i = dve.tensor_scalar(reverse(b["R"][32:32 + H, 4, :], lo, hi), natural(b["MM"][32:32 + H, :], lo, hi),
                                          -1.0, None, ALU.mult)
                i.then_inc(S["rows_nat"], 1)
                dve.wait_ge(S["rows_nat"], 1)
                dve.tensor_tensor(by_chunk(b["LI"]), b["mst"][:, :].rearrange("r (c a) -> r c a", a=1)
                                  .to_broadcast([ROWS, NT, P]), by_chunk(b["MM"]), ALU.subtract).then_inc(S["rows_t"], 1)
                dve.tensor_tensor(b["LF"][:, :], b["LF"][:, :], b["MM"][:, :], ALU.add).then_inc(S["rows_t"], 1)

            def weigh_keys(i):
                if i == 0:
                    dve.memset(b["v1"][:, :, :, :, DV:VPAD], 1.0)
                    dve.memset(b["ST"][:, 1, :, :, :], 0.0)
                    dve.memset(b["ST"][:, 0, :, :, :], 0.0).then_inc(S["st_upd"], 1)
                    dve.wait_ge(S["st_upd"], 1)
                    dve.wait_ge(S["col_done"], 3)
                    dve.wait_ge(S["dcb_in"], 16 * 8)
                dve.wait_ge(S["kT_ps"], i + 1)
                for dr, c in ((0, fwd[i]), (1, bwd[i])):
                    w = colS[:, colslot(c, 1), 32 * dr:32 * dr + H].rearrange("p (h a) -> p h a", a=1)
                    k = dve.tensor_tensor(b["wk"][:, dr, :, :], psum[:, 0, dr * QK:(dr + 1) * QK]
                                          .rearrange("p (h n) -> p h n", h=H), w.to_broadcast([P, H, DK]), ALU.mult)
                k.then_inc(S["wk_done"], 1)

            def update_states(i):
                dve.wait_ge(S["u_ps"], i + 1)
                if i + 1 < NT:
                    if i >= 1:
                        dve.wait_ge(st_out[(i - 1) % 2], 32 * ((i - 1) // 2 + 1))
                    for dr, c in ((0, fwd[i]), (1, bwd[i])):
                        for pr in range(2):
                            new = b["ST"][:, (i + 1) % 2, dr, pr, 0:VA]
                            if i + 1 in starts:
                                k = dve.memset(new, 0.0)
                            else:
                                k = dve.scalar_tensor_tensor(new, b["ST"][:, i % 2, dr, pr, 0:VA],
                                                             b["dcb"][:, dr, pr, c:c + 1],
                                                             psum[:, 1 + dr, VPAD * pr:VPAD * pr + VA],
                                                             ALU.mult, ALU.add)
                    k.then_inc(S["st_upd"], 1)
                    dve.wait_ge(S["st_upd"], i + 2)

            split_low(0)
            for j in range(-1, NCH):
                if 0 <= j < NCH - 1:
                    split_low(j + 1)
                if j == 0:
                    gate_rows()
                if j >= 0 and of_chunk[j][0] == KEYS_AT[0]:
                    dve.wait_ge(S["colT_ps"], 3)
                    dve.wait_ge(S["rows_out"], 16 * 6)
                if j >= 0 and chunks[j][0] == "gc" and chunks[j][2] == 0:
                    dve.wait_ge(S["colT_ps"], 3)
                    dve.wait_ge(S["rows_out"], 16 * 6)
                    for m in range(2):
                        for col in (0, SP_ + 1, SP_ + 2, T + 3):
                            i = dve.memset(b["CU"][:, m, col:col + 1], 0.0)
                    ch(i)
                for i in of_chunk[j]:
                    if i in STATE_AT:
                        update_states(STATE_AT.index(i))
                    if i in KEYS_AT:
                        weigh_keys(KEYS_AT.index(i))
                    _, kind, part, m, t0, w = pgroups[i]
                    if kind not in EV_DVE:
                        continue
                    dve.wait_ge(S["proj"], i + 1)
                    src = psum[:, 4 + i % 4, 0:w]
                    off = 1 if t0 < SP_ else 3
                    if kind == "u":
                        dve.wait_ge(S["ev_act"], ev_at[of_chunk[j - 1][-1]][1])
                        dve.tensor_tensor(b["CU"][:, m, t0 + off:t0 + off + w], src, b["gcS"][:, m, t0:t0 + w], ALU.mult
                                          ).then_inc(S["ev_dve"], 1)
                        if i == of_chunk[j][-1]:
                            dve.wait_ge(S["ev_dve"], ev_at[i][1])
                            for mm in range(2):
                                for s0, n, o in ((0, SP_, 0), (SP_, SS_, 2)):
                                    cv = b["CV"][:, mm, s0:s0 + n]
                                    tap = [b["cw"][:, k, 2 * part + mm:2 * part + mm + 1] for k in range(3)]
                                    x = [b["CU"][:, mm, s0 + o + k:s0 + o + k + n] for k in range(3)]
                                    ch(dve.tensor_scalar(cv, x[0], tap[0], None, ALU.mult))
                                    ch(dve.scalar_tensor_tensor(cv, x[1], tap[1], cv, ALU.mult, ALU.add))
                                    ch(dve.scalar_tensor_tensor(cv, x[2], tap[2], cv, ALU.mult, ALU.add))
                    else:
                        s = stage_no[i]
                        if s >= NST:
                            dve.wait_ge(stg[s % NST], 16 * (s // NST))
                        dve.tensor_tensor(b["stage"][:, s % NST, 0:w], src, b["CV"][:, m, t0:t0 + w], ALU.mult
                                          ).then_inc(S["ev_dve"], 1)
            barrier(dve, 1)

            dve.memset(d["vs"][:, :, :, DV:VPAD], 1.0)
            dve.memset(GV[:, :], 0.0)
            ch(dve.memset(GIF[:, :], 0.0))

            def choose(row, width, r0, r1):
                rows = slice(row, row + NE)
                for r in range(r0, r1):
                    best = GV[rows, 8 * r:8 * r + 8]
                    ch(dve.max(best, AFF[rows, 0:width]))
                    ch(dve.max_index(GI[rows, 8 * r:8 * r + 8], best, AFF[rows, 0:width]))
                    ch(dve.match_replace(AFF[rows, 0:width], best, AFF[rows, 0:width], -2.0))

            def residual(n, h):
                dve.wait_ge(S["o_ps"], 2 * n + h + 1)
                if h == 0:
                    dve.wait_ge(ld_x[n % 2], 16 * (n // 2 + 1))
                    if n >= 2:
                        dve.wait_ge(x1_out[n % 2], 16 * (n // 2))
                        dve.wait_ge(S["tk_done"], n - 1)
                dve.tensor_tensor(d["x1"][:, n % 2, 512 * h:512 * h + 512], psum[:, 6 + h, :],
                                  d["xs"][:, n % 2, 512 * h:512 * h + 512], ALU.add).then_inc(S["x1_done"], 1)

            def exponents(n):
                dve.wait_ge(ld[n % 2], 16 * NLD * (n // 2 + 1))
                if n >= 1:
                    dve.wait_ge(S["e_done"], n)
                for r in range(2 * H):
                    dr, h = r // H, r % H
                    i = dve.scalar_tensor_tensor(d["X"][:, r, :], d["negm"][:, n % 2, r, :],
                                                 colS[:, colslot(ORDER[n], 0), 32 * dr + h:32 * dr + h + 1],
                                                 d["masks"][:, dr, :], ALU.add, ALU.min)
                i.then_inc(S["x_done"], 1)

            def decayed_scores(n):
                dve.wait_ge(S["e_done"], n + 1)
                dve.wait_ge(S["s_ps"], n + 1)
                if n >= 1:
                    dve.wait_ge(S["num_ps"], n)
                for dr in range(2):
                    i = dve.tensor_tensor(d["SD"][:, H * dr:H * dr + H, :], psum[:, 0, :]
                                          .rearrange("p (h t) -> p h t", h=H), d["E"][:, H * dr:H * dr + H, :],
                                          ALU.mult)
                i.then_inc(S["sd_done"], 1)

            def out_low(h):
                for k in range(4 * h, 4 * h + 4):
                    dve.wait_ge(S["wo_hi"], k + 1)
                    dve.tensor_tensor(d["wol"][:, k, :], d["woraw"][:, k, :], d["woh"][:, k, :].bitcast(F32),
                                      ALU.subtract).then_inc(S["wo_lo"], 1)

            exponents(0)
            decayed_scores(0)
            out_low(0)
            for n in range(NT + 2):
                s = n % 2
                if n < NT:
                    dve.wait_ge(S["num_ps"], n + 1)
                    den = psum[:, 1:5, 0:2 * VPAD].rearrange("p a (b c) -> p a b c", c=VPAD)[:, :, :, DV]
                    floor = colS[:, colslot(ORDER[n], 2), :]
                    low, inv = d["sm"][:, s, 8:16], d["sm"][:, s, 0:8]
                    for dr in range(2):
                        i = dve.scalar_tensor_tensor(low[:, 4 * dr:4 * dr + 4].rearrange("p (a c) -> p a c", a=2),
                                                     den[:, 2 * dr:2 * dr + 2, :], -1.0,
                                                     floor[:, 32 * dr:32 * dr + H].rearrange("p (a c) -> p a c", a=2),
                                                     ALU.mult, ALU.max)
                    ch(i)
                    ch(dve.tensor_tensor(low.rearrange("p (a c) -> p a c", a=4), den,
                                         low.rearrange("p (a c) -> p a c", a=4), ALU.max))
                    dve.reciprocal(inv, low).then_inc(S["den_done"], 1)
                    if n + 1 < NT:
                        exponents(n + 1)
                    dve.wait_ge(S["den_done"], n + 1)
                    dve.wait_ge(S["hb_done"], n + 1)
                    if n >= 1:
                        dve.wait_ge(S["hsum"], n)
                    for h in range(H):
                        i = dve.scalar_tensor_tensor(d["ht"][:, h, :],
                                                     psum[:, 1 + h // 2, VPAD * (h % 2):VPAD * (h % 2) + DV],
                                                     d["sm"][:, s, h:h + 1], d["hb"][:, h, :], ALU.mult, ALU.add)
                    i.then_inc(S["ht_done"], 1)
                if 1 <= n <= NT:
                    residual(n - 1, 0)
                if n < NT:
                    dve.wait_ge(S["hsum"], n + 1)
                    inverse_root(d["ms"][:, s, 1, :], d["ms"][:, s, 0, :], d["ms"][:, s, 2, :])
                    dve.wait_ge(S["og_done"], n + 1)
                    if n >= 1:
                        dve.wait_ge(S["mixT_ps"], n)
                    for h in range(H):
                        i = dve.scalar_tensor_tensor(d["mix"][:, h, :], d["ht"][:, h, :], d["ms"][:, s, 1, h:h + 1],
                                                     d["og"][:, s, h * DV:(h + 1) * DV], ALU.mult, ALU.mult)
                    i.then_inc(S["mix_done"], 1)
                    if n + 1 < NT:
                        decayed_scores(n + 1)
                    if n == 0:
                        out_low(1)
                if n == NT:
                    dve.wait_ge(S["affT_ps"], 1)
                    for i in range(NS // 4):
                        ch(dve.tensor_copy(AFF[0:NE, 512 * i:512 * i + 512], psum[0:NE, (0, 4)[i], :]))
                    choose(0, SS_, 0, 2)
                if 1 <= n <= NT:
                    residual(n - 1, 1)
                if n < NT:
                    dve.wait_ge(S["mxh_done"], 2 * n + 1)
                    dve.tensor_tensor(d["mxl"][:, s, 0:4, :], d["cvs"][:, s, :, :],
                                      d["mxh"][:, s, 0:4, :].bitcast(F32), ALU.subtract)
                if n >= 2:
                    m = n - 2
                    dve.wait_ge(S["lg_ps"], m + 1)
                    dve.tensor_reduce(logit_max[:, m, 0:1], psum[:, 3, 0:NE], AX_X, ALU.max, negate=True
                                      ).then_inc(S["lgmax"], 1)
                if n < NT:
                    dve.wait_ge(S["mxh_done"], 2 * n + 2)
                    dve.tensor_tensor(d["mxl"][:, s, 4:8, :], psum[:, 5, :].rearrange("p (k t) -> p k t", k=4),
                                      d["mxh"][:, s, 4:8, :].bitcast(F32), ALU.subtract).then_inc(S["mxl_done"], 1)
                if 1 <= n <= NT:
                    m = n - 1
                    q = m % 2
                    dve.wait_ge(S["sum2"], m + 1)
                    if m == 0:
                        dve.wait_ge(S["cst_in"], 16 * 3)
                    inverse_root(d["mt"][:, q, 1, :], d["mt"][:, q, 0, :], d["mt"][:, q, 2, :])
                    if m >= 2:
                        dve.wait_ge(tk_out[q], 16 * (m // 2))
                        dve.wait_ge(S["tkT_ps"], m - 1)
                    dve.scalar_tensor_tensor(d["tk"][:, q, :], d["x1"][:, q, :], d["mt"][:, q, 1, :], d["g2b"][:, :],
                                             ALU.mult, ALU.mult).then_inc(S["tk_done"], 1)
                if n == NT:
                    choose(0, SS_, 2, 4)
                if n >= 2:
                    m = n - 2
                    dve.wait_ge(S["exps"], m + 1)
                    ch(dve.reciprocal(logit_max[:, m, 2:3], logit_max[:, m, 1:2]))
                    dve.tensor_scalar(aff[:, m, :], aff[:, m, :], logit_max[:, m, 2:3], None, ALU.mult
                                      ).then_inc(S["aff_done"], 1)

            barrier(dve, 2)
            choose(0, SS_, 4, CAPS // 8)
            dve.wait_ge(S["affT_ps"], 2)
            ch(dve.tensor_copy(AFF[32:32 + NE, 0:SP_], psum[0:NE, 1, 0:SP_]))
            choose(32, SP_, 0, CAPP // 8)
            dve.tensor_copy(GIF[0:NE, :], GI[0:NE, :]).then_inc(S["topk"], 1)
            dve.tensor_copy(GIF[32:32 + NE, 0:CAPP], GI[32:32 + NE, 0:CAPP]).then_inc(S["topk"], 1)
            dve.wait_ge(S["selT_ps"], 2)
            dve.tensor_copy(GC[:, :], psum[:, 4, 0:48]).then_inc(S["sel_done"], 1)
            dve.tensor_scalar(IDX[:, 0:NE], psum[:, 5, 0:NE], float(SP_), None, ALU.add).then_inc(S["sel_done"], 1)
            dve.tensor_copy(IDX[:, 32:32 + NE], psum[:, 5, 32:32 + NE]).then_inc(S["sel_done"], 1)

            def low(e, j):
                if j in BY_DVE:
                    dve.wait_ge(S["ehi"], NB * e + j + 1)
                    dve.tensor_tensor(f["elo"][:, j % RING, :, :], f["eraw"][:, j % RING, :, :],
                                      f["ehi"][:, j % RING, :, :].bitcast(F32), ALU.subtract
                                      ).then_inc(S["elo_dve"], 1)

            def tokens_low(e, s, which):
                for g in which:
                    k0, nk = TG[g]
                    dve.wait_ge(S["xc_hi"], 3 * e + g + 1)
                    dve.tensor_tensor(f["xc"][:, s, k0:k0 + nk, 1, :], psum[:, 6 + g % 2, 0:nk * NC]
                                      .rearrange("p (k t) -> p k t", k=nk),
                                      f["xc"][:, s, k0:k0 + nk, 0, :].bitcast(F32), ALU.subtract).then_inc(S["xc_lo"], 1)

            tokens_low(0, 0, (0, 1, 2))
            dve.sem_inc(S["hc_lo"], 4)

            def expert(e, s, first=False, last=False):
                for p in range(4):
                    for m in range(2):
                        i = 2 * p + m
                        dve.wait_ge(S["gu_ps"], 8 * e + i + 1)
                        if m == 0 and not (first and p < 2):
                            dve.wait_ge(S["hid_done"], 1 + 4 * e + p - 1)
                        base = 2 * (i % 2)
                        both = psum[:, base:base + 2, 0:2 * NC].rearrange("p a (t n) -> p a n t", t=2)
                        dve.tensor_reduce(f["gu"][:, p % 2, m, :, :], both, AX_X, ALU.add).then_inc(S["gu_add"], 1)
                        if m == 0 and p < 3:
                            low(e, 2 * p + 4)
                    if p < 3:
                        low(e, 2 * p + 5)
                    if p in (1, 2) and not last:
                        tokens_low(e + 1, 1 - s, ((0, 1), (2,))[p - 1])
                    dve.wait_ge(S["hc_hi"], 4 * e + p + 1)
                    dve.tensor_tensor(f["hc"][:, 2 * p:2 * p + 2, 1, :], f["hid"][:, :, :],
                                      f["hc"][:, 2 * p:2 * p + 2, 0, :].bitcast(F32), ALU.subtract
                                      ).then_inc(S["hc_lo"], 1)
                for q in range(4):
                    for m in range(2):
                        i = 2 * q + m
                        dve.wait_ge(S["dn_ps"], 8 + 8 * e + i + 1)
                        dve.wait_ge(S["yT_ps"], 8 * e + i + 1)
                        both = psum[:, 4 + i % 2, 0:2 * NC].rearrange("p (t n) -> p n t", t=2)
                        dve.tensor_reduce(f["ys"][:, i % 2, :], both, AX_X, ALU.add).then_inc(S["ys_done"], 1)
                    if q == 0:
                        low(e, 10)
                    if not last:
                        low(e + 1, q)

            expert(0, 0, first=True)
            with dve.Fori(0, NE // 2 - 1) as g:
                expert(2 * g + 1, 1)
                expert(2 * g + 2, 0)
            expert(NE - 1, 1, last=True)
            barrier(dve, 3)
            dve.wait_ge(S["gf_in"], 16)
            for n in range(NT):
                if n in (0, 2, 6):
                    c = slice(*BATCHES[(0, 2, 6).index(n)])
                    dve.wait_ge(S["f_sum"], c.stop)
                    inverse_root(z["fs"][:, 1, c], z["fs"][:, 0, c], z["fs"][:, 2, c])
                dve.scalar_tensor_tensor(z["fx"][:, n, :], z["fx"][:, n, :], z["fs"][:, 1, n:n + 1], z["gf"][:, :],
                                         ALU.mult, ALU.mult).then_inc(S["f_y"], 1)

        @block.tensor
        def _(pe):
            pe.wait_ge(S["const"], 1)
            def transpose_tokens(n):
                pe.wait_ge(S["xn_done"], n + 1)
                if n >= 2:
                    pe.wait_ge(S["hn_lo"], n - 1)
                for k in range(KD):
                    i = pe.transpose(psum[:, 2 * (n % 2) + k // 4, (k % 4) * P:(k % 4 + 1) * P],
                                     b["xa"][:, n, k * P:(k + 1) * P], ident[:, :])
                i.then_inc(S["xT_ps"], 1)

            def transpose_keys(i):
                pe.wait_ge(l1[i % 2], 16 * 4 * (i // 2 + 1))
                if i == 0:
                    pe.wait_ge(S["col_done"], 3)
                else:
                    pe.wait_ge(S["wk_done"], i)
                for dr in range(2):
                    for pr in range(2):
                        tr = pe.transpose(psum[:, 0, dr * QK + pr * P:dr * QK + (pr + 1) * P],
                                          b["kT1"][:, i % 2, dr, pr, :], ident[:, :])
                tr.then_inc(S["kT_ps"], 1)

            def chunk_sums(i):
                pe.wait_ge(S["wk_done"], i + 1)
                if i >= 1:
                    pe.wait_ge(S["st_upd"], i + 1)
                for dr in range(2):
                    for pr in range(2):
                        for half in range(2):
                            h = 2 * pr + half
                            mm = pe.matmul(psum[64 * half:64 * half + 64, 1 + dr, VPAD * pr:VPAD * pr + VA],
                                           b["wk"][:, dr, h, :], b["v1"][:, i % 2, dr, h, 0:VA], start=True, stop=True)
                mm.then_inc(S["u_ps"], 1)

            for n in range(BATCHES[1][1]):
                transpose_tokens(n)
            for i, (j, kind, part, m, t0, w) in enumerate(pgroups):
                if i in STATE_AT:
                    chunk_sums(STATE_AT.index(i))
                if i in KEYS_AT:
                    transpose_keys(KEYS_AT.index(i))
                if kind == "gate":
                    if i == 0:
                        pe.wait_ge(S["wg_lo"], 1)
                    if i == 1:
                        for n in range(*BATCHES[2]):
                            transpose_tokens(n)
                    pe.wait_ge(S["hn_lo"], (t0 + w) // P)
                elif i == of_chunk[j][0]:
                    pe.wait_ge(S["w_lo"], j + 1)
                if i >= 4:
                    who, c = ev_at[i - 4]
                    pe.wait_ge(S["ev_act"] if who == "act" else S["ev_dve"], c)
                for k in range(KD):
                    if kind in ("v", "o"):
                        t = slice(m * P, (m + 1) * P)
                        xh, xl = b["hn_hi"][:, k, t], b["hn_lo"][:, k, t]
                        wh, wl = b["whi"][:, j % 2, k, :], b["wlo"][:, j % 2, k, :]
                        pairs = ((xh, wh), (xh, wl), (xl, wh))
                        o = psum[:, 4 + i % 4, 0:w]
                    else:
                        t = slice(t0, t0 + w)
                        xh, xl = b["hn_hi"][:, k, t], b["hn_lo"][:, k, t]
                        if kind == "gate":
                            wh, wl = b["wg_hi"][:, k, 0:GATE_ROWS], b["wg_lo"][:, k, 0:GATE_ROWS]
                            o = psum[0:GATE_ROWS, 4 + i % 4, 0:w]
                        else:
                            c = slice(m * P, (m + 1) * P)
                            wh, wl = b["whi"][:, j % 2, k, c], b["wlo"][:, j % 2, k, c]
                            o = psum[:, 4 + i % 4, 0:w]
                        pairs = ((wh, xh), (wh, xl), (wl, xh))
                    for a, (lhs, rhs) in enumerate(pairs):
                        mm = pe.matmul(o, lhs, rhs, start=(k == 0 and a == 0), stop=(k == KD - 1 and a == 2))
                mm.then_inc(S["proj"], 1)
                if i == of_chunk[1][-1]:
                    pe.wait_ge(S["rows_nat"], 1)
                    pe.wait_ge(S["rows_exp"], 9)
                    for c in range(NT):
                        for q in range(3):
                            a = colslot(c, q)
                            tr = pe.transpose(psum[:, a // 12, (a % 12) * 40:(a % 12) * 40 + ROWS],
                                              b["R"][:, q, c * P:(c + 1) * P], ident[0:ROWS, 0:ROWS])
                            if a % 12 == 11 or a == 3 * NT - 1:
                                tr.then_inc(S["colT_ps"], 1)
            barrier(pe, 1)

            def project(n, h):
                pe.wait_ge(S["mxl_done"], n + 1)
                if n >= 1:
                    pe.wait_ge(S["x1_done"], 2 * (n - 1) + h + 1)
                c = slice(512 * h, 512 * h + 512)
                for k in range(KD):
                    for a, (x, w) in enumerate((("mxh", "woh"), ("mxh", "wol"), ("mxl", "woh"))):
                        mm = pe.matmul(psum[:, 6 + h, :], d[x][:, n % 2, k, :], d[w][:, k, c],
                                       start=(k == 0 and a == 0), stop=(k == KD - 1 and a == 2))
                mm.then_inc(S["o_ps"], 1)

            def scores(n):
                pe.wait_ge(ld[n % 2], 16 * NLD * (n // 2 + 1))
                if n >= 1:
                    pe.wait_ge(S["sd_done"], n)
                for h in range(H):
                    mm = pe.matmul(psum[:, 0, h * P:(h + 1) * P], d["kTs"][:, n % 2, h // 2, :],
                                   d["qz"][:, n % 2, h, :], start=True, stop=True)
                mm.then_inc(S["s_ps"], 1)

            scores(0)
            for n in range(NT + 2):
                s = n % 2
                if n < NT:
                    pe.wait_ge(S["sd_done"], n + 1)
                    pe.wait_ge(S["qs_done"], n + 1)
                    if n >= 1:
                        pe.wait_ge(S["ht_done"], n)
                    if n >= 3:
                        pe.wait_ge(S["exps"], n - 2)
                    for dr in range(2):
                        for h in range(H):
                            o = psum[:, 1 + 2 * dr + h // 2, VPAD * (h % 2):VPAD * (h % 2) + VA]
                            pe.matmul(o, d["SD"][:, H * dr + h, :], d["vs"][:, s, h, 0:VA], start=True, stop=False)
                            mm = pe.matmul(o, d["qs"][:, H * dr + h, :], d["sts"][:, s, dr, h // 2, 0:VA],
                                           start=False, stop=True)
                    mm.then_inc(S["num_ps"], 1)
                if 1 <= n <= NT:
                    project(n - 1, 0)
                if n == NT:
                    pe.wait_ge(S["aff_done"], NS)
                    for i in range(NS):
                        tr = pe.transpose(psum[0:NE, (0, 4)[i // 4], (i % 4) * P:(i % 4 + 1) * P], aff[:, i, :],
                                          ident[:, :])
                    tr.then_inc(S["affT_ps"], 1)
                if n + 1 < NT:
                    scores(n + 1)
                if n >= 2:
                    m = n - 2
                    pe.wait_ge(S["tk_done"], m + 1)
                    if n < NT:
                        pe.wait_ge(S["ht_done"], n + 1)
                    if m >= 1:
                        pe.wait_ge(S["tkT_done"], m)
                    for k in range(KD):
                        tr = pe.transpose(psum[:, 1 + k // 4, (k % 4) * P:(k % 4 + 1) * P],
                                          d["tk"][:, m % 2, k * P:(k + 1) * P], ident[:, :])
                    tr.then_inc(S["tkT_ps"], 1)
                if 1 <= n <= NT:
                    project(n - 1, 1)
                if n >= 2:
                    pe.wait_ge(S["tkT_done"], m + 1)
                    if m >= 1:
                        pe.wait_ge(S["exps"], m)
                    for k in range(KD):
                        mm = pe.matmul(psum[:, 3, 0:NE], d["tkT"][:, k, :], d["wr"][:, k, :], start=(k == 0),
                                       stop=(k == KD - 1))
                    mm.then_inc(S["lg_ps"], 1)
                if n < NT:
                    if n >= 1:
                        pe.wait_ge(S["mxl_done"], n)
                    pe.wait_ge(S["mix_done"], n + 1)
                    for h in range(H):
                        tr = pe.transpose(psum[:, 5, h * P:(h + 1) * P], d["mix"][:, h, :], ident[:, :])
                    tr.then_inc(S["mixT_ps"], 1)
            pe.wait_ge(S["aff_done"], NT)
            for i in range(NTP):
                tr = pe.transpose(psum[0:NE, 1, i * P:(i + 1) * P], aff[:, NS + i, :], ident[:, :])
            tr.then_inc(S["affT_ps"], 1)
            barrier(pe, 2)
            pe.wait_ge(S["topk"], 2)
            pe.transpose(psum[:, 4, 0:48], GV[:, :], ident[0:48, 0:48]).then_inc(S["selT_ps"], 1)
            pe.transpose(psum[:, 5, 0:48], GIF[:, :], ident[0:48, 0:48]).then_inc(S["selT_ps"], 1)

            def token_columns(e, which):
                pe.wait_ge(S["gath"], 32 * e + 32)
                for g in which:
                    k0, nk = TG[g]
                    if g == 2:
                        pe.wait_ge(S["xc_lo"], 3 * e + 1)
                    for k in range(nk):
                        c = slice((k0 + k) * P, (k0 + k + 1) * P)
                        o = psum[:, 6 + g % 2, k * NC:(k + 1) * NC]
                        pe.transpose(o[:, 0:CAPS], f["xg"][:, c], ident[:, :])
                        tr = pe.transpose(o[:, CAPS:NC], f["xgp"][:, c], ident[0:CAPP, 0:CAPP])
                    tr.then_inc(S["exT_ps"], 1)

            def rows_back(e, i):
                pe.wait_ge(S["ys_done"], 2 + 8 * e + i + 1)
                c = slice((i % 4) * P, (i % 4 + 1) * P)
                pe.transpose(psum[:, 6, c], f["ys"][:, i % 2, 0:CAPS], ident[:, :])
                pe.transpose(psum[0:CAPP, 7, c], f["ys"][:, i % 2, CAPS:NC], ident[:, :]).then_inc(S["yT_ps"], 1)

            def products(o, q, c, x, xb, k0=0, k1=KD):
                for k in range(k0, k1):
                    pe.matmul(o[:, 0:2 * NC], f["ehi"][:, q, k, c], x[:, k, :, :].rearrange("p a t -> p (a t)"),
                              start=(k == 0), stop=False, skip_group_check=True)
                for k in range(k0, k1):
                    mm = pe.matmul(o[:, NC:2 * NC], f["elo"][:, q, k, c], xb[:, k, :], start=False,
                                   stop=(k == KD - 1), skip_group_check=True)
                return mm

            token_columns(0, (0, 1, 2))

            def expert(e, s, first=False, last=False):
                pe.wait_ge(S["xc_lo"], 3 * e + 3)
                pe.wait_ge(S["xb_done"], e + 1)
                for p in range(4):
                    wait_split(pe, e, 2 * p)
                    wait_split(pe, e, 2 * p + 1)
                    for m in range(2):
                        i = 2 * p + m
                        pe.wait_ge(S["gu_add"], 8 * e + i + 1)
                        for a in range(2):
                            mm = products(psum[:, 2 * (i % 2) + a, :], (2 * p + a) % RING, slice(m * P, (m + 1) * P),
                                          f["xc"][:, s, :, :, :], f["xb"][:, s, :, :])
                        mm.then_inc(S["gu_ps"], 1)
                        if i == 0 and not first:
                            rows_back(e - 1, KD - 1)
                        if i == 3 and not last:
                            pe.wait_ge(S["y_done"], 2 * e + 2)
                            token_columns(e + 1, (0, 1))
                        if i == 5 and not last:
                            token_columns(e + 1, (2,))
                for q in range(4):
                    wait_split(pe, e, 8 + q)
                    tiles = [(psum[:, 4 + m, :], (8 + q) % RING, slice(m * P, (m + 1) * P), f["hc"], f["hbf"])
                             for m in range(2)]
                    pe.wait_ge(S["ys_done"], 8 * e + 2 * q + 1)
                    if q == 0:
                        pe.wait_ge(S["hc_lo"], 4 + 4 * e + 3)
                        pe.wait_ge(S["hb_bf"], 1 + 4 * e + 3)
                        products(*tiles[0], 0, KF - 2)
                        pe.wait_ge(S["ys_done"], 8 * e + 2 * q + 2)
                        products(*tiles[1], 0, KF - 2)
                        pe.wait_ge(S["hc_lo"], 4 + 4 * e + 4)
                        pe.wait_ge(S["hb_bf"], 1 + 4 * e + 4)
                    for m in range(2):
                        i = 2 * q + m
                        if q > 0 and m == 1:
                            pe.wait_ge(S["ys_done"], 8 * e + i + 1)
                        products(*tiles[m], KF - 2 if q == 0 else 0, KF).then_inc(S["dn_ps"], 1)
                        if i == 1:
                            if last:
                                pe.wait_ge(S["y_done"], 2 * e + 2)
                            else:
                                pe.wait_ge(S["xc_lo"], 3 * (e + 1) + 3)
                        if i == 5:
                            pe.wait_ge(S["y_done"], 2 + 2 * e + 1)
                        if i >= 1:
                            rows_back(e, i - 1)

            expert(0, 0, first=True)
            with pe.Fori(0, NE // 2 - 1) as g:
                expert(2 * g + 1, 1)
                expert(2 * g + 2, 0)
            expert(NE - 1, 1, last=True)
            rows_back(NE - 1, KD - 1)
            barrier(pe, 3)


_INS = ['x_prompt', 'x_sample', 'norm1_g', 'w_in', 'conv_w', 'gate_bias', 'head_norm_g', 'w_out', 'norm2_g',
        'w_router', 'w_gate', 'w_up', 'w_down', 'final_g']


def kernel(**inputs):
    import numpy as _np
    import concourse.bacc as _bacc
    from concourse import mybir as _mybir
    from concourse.bass_utils import run_bass_kernel_spmd as _run

    nc = _bacc.Bacc("TRN2", target_bir_lowering=False, num_devices=1)
    arrays, args = {}, []
    for name in _INS:
        a = _np.ascontiguousarray(inputs[name])
        arrays[f"in_{name}_dram"] = a
        args.append(nc.dram_tensor(f"in_{name}_dram", a.shape, _mybir.dt.from_np(a.dtype), kind="ExternalInput").ap())
    outs = [("y_prompt", inputs["x_prompt"].shape), ("y_sample", inputs["x_sample"].shape)]
    for name, shape in outs:
        args.append(nc.dram_tensor(f"out_{name}_dram", tuple(shape), _mybir.dt.float32, kind="ExternalOutput").ap())
    hybrid_conv_mlstm_moe(nc, *args)
    r = _run(nc, [arrays], core_ids=[0])
    return tuple(r.results[0][f"out_{name}_dram"] for name, _ in outs)
```

```python
from contextlib import ExitStack

import concourse.bass as bass
from concourse import mybir

ALU = mybir.AluOpType
ACT = mybir.ActivationFunctionType
AX_X = mybir.AxisListType.X
F32 = mybir.dt.float32
F32R = mybir.dt.float32r
BF16 = mybir.dt.bfloat16
U32 = mybir.dt.uint32

P = 128
NEG = -1.0e30


class Chain:

    def __init__(self, eng, sem):
        self.eng, self.sem, self.n = eng, sem, 0

    def __call__(self, ins):
        ins.then_inc(self.sem, 1)
        self.n += 1
        self.eng.wait_ge(self.sem, self.n)




def hybrid_conv_mlstm_moe(nc, x_prompt, x_sample, norm1_g, w_in, conv_w, gate_bias, head_norm_g, w_out,
                          norm2_g, w_router, w_gate, w_up, w_down, final_g, y_prompt, y_sample):
    D = x_prompt.shape[2]
    SP_, SS_ = x_prompt.shape[1], x_sample.shape[1]
    T = SP_ + SS_
    KD = D // P
    NT = T // P
    NTP = SP_ // P
    CW = conv_w.shape[2]
    H = gate_bias.shape[2]
    DV = (D // 2) // H
    DK = DV // 2
    QK = H * DK
    VW = H * DV
    NE = w_gate.shape[1]
    FF = w_gate.shape[3]
    KF = FF // P
    CAPP, CAPS = 2 * SP_ // NE, 2 * SS_ // NE
    NC = CAPP + CAPS
    EPS = 1e-6
    VA = DV + 1
    VPAD = DV + 2
    GATE_ROWS = 100
    ROWS = 36
    assert (D, DV, DK, H, CAPS) == (1024, 128, 64, 4, 128) and SP_ % 256 == 0 and SS_ % 512 == 0

    x_chunk = [x_prompt[0, t * P:(t + 1) * P, :] for t in range(NTP)] + \
              [x_sample[0, t * P:(t + 1) * P, :] for t in range(NT - NTP)]
    y_chunk = [y_prompt[0, t * P:(t + 1) * P, :] for t in range(NTP)] + \
              [y_sample[0, t * P:(t + 1) * P, :] for t in range(NT - NTP)]

    qk_d = nc.dram_tensor("qk_d", (4, P, T), F32).ap()
    v_d = nc.dram_tensor("v_d", (T, VW), F32).ap()
    o_d = nc.dram_tensor("o_d", (T, VW), F32).ap()
    conv_d = nc.dram_tensor("conv_d", (CW // P, P, T), F32).ap()
    negm_d = nc.dram_tensor("negm_d", (2 * H, T), F32).ap()
    inter_d = nc.dram_tensor("inter_d", (2 * H, T), F32).ap()
    decay_d = nc.dram_tensor("decay_d", (2 * H, NT), F32).ap()
    state_d = nc.dram_tensor("state_d", (NT, P, 2, 2 * VPAD), F32).ap()
    acc_d = nc.dram_tensor("acc_d", (T, D), F32).ap()
    tok_d = nc.dram_tensor("tok_d", (T, D), F32).ap()

    groups = [(0, SP_)] + [(SP_ + i * 512, 512) for i in range(SS_ // 512)]
    BATCHES = [(0, 2), (2, 6), (6, NT)]

    c_gb, c_gc, c_u = 0, CW, 2 * CW
    c_q, c_k, c_v = 3 * CW, 3 * CW + QK, 3 * CW + 2 * QK
    c_o = c_v + VW
    c_gates = c_o + VW
    CH = 256
    chunks = [("k", c_k, 0), ("q", c_q, 0)] + [("v", c_v + i * CH, i) for i in range(VW // CH)] + \
             [("o", c_o + i * CH, i) for i in range(VW // CH)]
    for i in range(CW // CH):
        chunks += [("gc", c_gc + i * CH, i), ("u", c_u + i * CH, i), ("gb", c_gb + i * CH, i)]
    NCH = len(chunks)
    pgroups = [(-1, "gate", 0, 0, t0, w) for t0, w in groups]
    for j, (kind, _, part) in enumerate(chunks):
        if kind in ("v", "o"):
            pgroups += [(j, kind, part, t, 0, CH) for t in range(NT)]
        else:
            pgroups += [(j, kind, part, m, t0, w) for m in range(2) for t0, w in groups]
    EV_DVE = ("u", "gb")
    ev_at, n_act, n_dve = [], 0, 0
    for g in pgroups:
        if g[1] in EV_DVE:
            n_dve += 1
            ev_at.append(("dve", n_dve))
        else:
            n_act += 1
            ev_at.append(("act", n_act))
    NST = 4
    staged = [i for i, g in enumerate(pgroups) if g[1] in ("k", "q", "v", "o", "gb")]
    stage_no = {i: s for s, i in enumerate(staged)}
    of_chunk = {j: [i for i, g in enumerate(pgroups) if g[0] == j] for j in range(-1, NCH)}
    KEYS_AT = [of_chunk[5][0] + 4 * i for i in range(NT)]
    STATE_AT = [g + 3 for g in KEYS_AT]
    after_v = [i for i in staged if pgroups[i][1] in ("k", "q", "v")]

    out = ExitStack()
    with out:
        def sem(name):
            return out.enter_context(nc.semaphore(name))

        def keep(name, shape, dt=F32):
            return out.enter_context(nc.sbuf_tensor(name, shape, dt))

        psum = out.enter_context(nc.psum_tensor("psum", [P, 8, 512], F32))

        ident = keep("ident", [P, P])
        colS = keep("colS", [P, 36, 40])
        zrow = keep("zrow", [ROWS, 1])
        aff = keep("aff", [P, NT, NE])
        logit_max = keep("logit_max", [P, NT, 4])
        HALF2, PROMPT = 32, 64
        SEL = PROMPT + NE
        AFF = keep("AFF", [SEL, SS_ // 2])
        GV = keep("GV", [SEL, P])
        GI = keep("GI", [SEL, P], U32)
        GIF = keep("GIF", [SEL, P])
        GV2 = keep("GV2", [NE, P])
        GI2 = keep("GI2", [NE, P])
        from_first = keep("from_first", [NE, P])
        GC = keep("GC", [P, SEL])
        IDX = keep("IDX", [P, SEL], U32)

        def stage_buffers(specs, *inner):
            got = {}
            with ExitStack() as s:
                for n, shape, dt in specs:
                    got[n] = s.enter_context(nc.sbuf_tensor(n, shape, dt))
                for part in inner:
                    with ExitStack() as t:
                        for n, shape, dt in part:
                            got[n] = t.enter_context(nc.sbuf_tensor(n, shape, dt))
            return got

        b = stage_buffers([
            ("hn_hi", [P, KD, T], F32R), ("hn_lo", [P, KD, T], F32R),
            ("wraw", [P, 2, KD, CH], F32), ("whi", [P, 2, KD, CH], F32R), ("wlo", [P, 2, KD, CH], F32R),
            ("stage", [P, NST, 512], F32),
            ("graw", [P, KD, 4 * H], F32), ("gbias", [P, 1], F32), ("cw", [P, 3, CW // P], F32),
            ("wg_hi", [P, KD, P], F32R), ("wg_lo", [P, KD, P], F32R), ("mst", [ROWS, NT], F32),
            ("st1", [P, 3, NT], F32)],
            [("xa", [P, NT, D], F32), ("g1", [P, D], F32), ("sq1", [P, D], F32)],
            [("R", [ROWS, 5, T], F32), ("GA", [P, T], F32), ("LI", [ROWS, T], F32), ("LF", [ROWS, T], F32),
             ("MM", [ROWS, T], F32), ("TM", [P, T], F32)],
            [("gcS", [P, 2, T], F32), ("CU", [P, 2, T + 4], F32), ("CV", [P, 2, T], F32),
             ("kT1", [P, 2, 2, 2, P], F32), ("v1", [P, 2, 2, H, VPAD], F32), ("wk", [P, 2, H, DK], F32),
             ("ST", [P, 2, 2, 2, VPAD], F32), ("dcb", [P, 2, 2, NT], F32)])
        d = stage_buffers([
            ("woh", [P, KD, D], F32R), ("wol", [P, KD, D], F32R),
            ("masks", [P, 2, P], F32), ("hgb", [P, VW], F32), ("g2b", [P, D], F32), ("wr", [P, KD, NE], F32),
            ("kTs", [P, 2, 2, P], F32), ("qz", [P, 2, H, P], F32), ("vs", [P, 2, H, VPAD], F32),
            ("og", [P, 2, VW], F32), ("negm", [P, 2, 2 * H, P], F32), ("inter", [P, 2, 4, P], F32),
            ("sts", [P, 2, 2, 2, VPAD], F32), ("cvs", [P, 2, CW // P, P], F32),
            ("X", [P, 2 * H, P], F32), ("E", [P, 2 * H, P], F32), ("SD", [P, 2 * H, P], F32),
            ("qs", [P, 2 * H, P], F32), ("hb", [P, H, DV], F32), ("ht", [P, H, DV], F32), ("junkh", [P, H, DV], F32),
            ("mix", [P, H, DV], F32), ("mxh", [P, 2, KD, P], F32R), ("mxl", [P, 2, KD, P], F32R),
            ("sm", [P, 2, 16], F32), ("ms", [P, 2, 3, H], F32), ("mt", [P, 2, 3, 1], F32)],
            [("woraw", [P, KD, D], F32)],
            [("xs", [P, 2, D], F32), ("x1", [P, 2, D], F32), ("tk", [P, 2, D], F32), ("tkT", [P, KD, P], F32),
             ("junk", [P, D], F32)])
        f = stage_buffers([
            ("eraw", [P, 6, KD, CH], F32), ("ehi", [P, 6, KD, CH], F32R), ("elo", [P, 6, KD, CH], BF16),
            ("xg", [P, D], F32), ("xgp", [CAPP, D], F32),
            ("xc", [P, 2, KD, 2, NC], F32R), ("xb", [P, 2, KD, NC], BF16),
            ("gu", [P, 2, 2, 2, NC], F32), ("sg", [P, 2, NC], F32), ("hid", [P, 2, NC], F32),
            ("hc", [P, KF, 2, NC], F32R), ("hbf", [P, KF, NC], BF16),
            ("ys", [P, 4, NC], F32), ("yt", [P, D], F32), ("yp", [CAPP, D], F32),
            ("idx", [P, 2, 2], U32), ("gcol", [P, 2], F32)])
        z = stage_buffers([("fx", [P, NT, D], F32), ("fq", [P, D], F32), ("gf", [P, D], F32),
                           ("fs", [P, 4, NT], F32)])

        S = {n: sem("s_" + n) for n in (
            "bar act_ch dve_ch pool_ch "
            "x_in0 x_in1 x_in2 g1_in xg_done const zeroed small_in sumsq xn_done xT_ps hn_hi hn_lo "
            "w_in0 w_in1 wg_hi wg_lo w_hi w_lo proj ev_act ev_dve st0 st1 st2 st3 "
            "soft rows_t rows_exp rows_nat rows_out colT_ps "
            "cst_in dcb_in col_done wo_in0 wo_in1 wo_hi wo_lo l1_0 l1_1 kT_ps wk_done u_ps st_upd st_out0 st_out1 "
            "ld0 ld1 ld_mix0 ld_mix1 ld_x0 ld_x1 padded masked qs_done s_ps x_done e_done sd_done num_ps "
            "den_done hb_done ht_done hsum og_done mix_done mixT_ps mxh_done mxl_done o_ps x1_done "
            "x1_out0 x1_out1 sum2 tk_done tk_out0 tk_out1 tkT_ps tkT_done "
            "lg_ps lgmax exps aff_done affT_ps topk selT_ps sel_done "
            "er0 er1 er2 er3 er4 er5 ehi elo_dve elo_pool idx_cp gath exT_ps xc_hi xc_lo xb_done "
            "gu_ps gu_add sg_done hid_done hc_hi hc_lo hb_bf dn_ps ys_done yT_ps y_done scat settled "
            "gf_in f_in0 f_in1 f_in2 f_in3 f_in4 f_sum f_y f_out").split()}
        x_in = (S["x_in0"], S["x_in1"], S["x_in2"])
        w_ind, stg = (S["w_in0"], S["w_in1"]), (S["st0"], S["st1"], S["st2"], S["st3"])
        l1, ld = (S["l1_0"], S["l1_1"]), (S["ld0"], S["ld1"])
        ld_mix, ld_x = (S["ld_mix0"], S["ld_mix1"]), (S["ld_x0"], S["ld_x1"])
        wo_in, st_out = (S["wo_in0"], S["wo_in1"]), (S["st_out0"], S["st_out1"])
        x1_out, tk_out = (S["x1_out0"], S["x1_out1"]), (S["tk_out0"], S["tk_out1"])
        er = (S["er0"], S["er1"], S["er2"], S["er3"], S["er4"], S["er5"])
        f_in = (S["f_in0"], S["f_in1"], S["f_in2"], S["f_in3"], S["f_in4"])

        def barrier(eng, k):
            eng.drain().then_inc(S["bar"], 1)
            eng.wait_ge(S["bar"], 5 * k)

        def rows_of(row):
            return row.partition_broadcast(P).rearrange("p a n -> p (a n)")

        seqs = [(0, NTP), (NTP, NT)]
        fwd = list(range(NT))
        bwd = [c for lo, hi in seqs for c in range(hi - 1, lo - 1, -1)]
        starts = [lo for lo, _ in seqs]

        def natural(ap2, lo, hi):
            return ap2[:, lo * P:hi * P]

        def reverse(ap2, lo, hi):
            return ap2[:, hi * P - 1:lo * P - 1:-1] if lo else ap2[:, hi * P - 1::-1]

        ORDER = list(range(NTP, NT)) + list(range(NTP))
        NS = NT - NTP

        def tokens_of(n):
            return slice(ORDER[n] * P, (ORDER[n] + 1) * P)

        TG = ((0, 3), (3, 3), (6, 2))
        NLD = 8

        def colslot(c, q):
            return 3 * c + q

        DOWN_BANK = (4, 5, 3)
        NB = 12
        RING = 6
        BY_POOL = [3, 7, 11]
        BY_DVE = [j for j in range(NB) if j not in BY_POOL]

        def wait_split(eng, e, j):
            mine, s = (BY_POOL, S["elo_pool"]) if j in BY_POOL else (BY_DVE, S["elo_dve"])
            eng.wait_ge(s, len(mine) * (e + 1) + mine.index(j) + 1)

        def wait_slot(eng, e, j):
            before = (j + RING) % NB
            mine, s = (BY_POOL, S["elo_pool"]) if before in BY_POOL else (BY_DVE, S["elo_dve"])
            eng.wait_ge(s, len(mine) * (e if j < RING else e + 1) + mine.index(before) + 1)

        block = out.enter_context(nc.Block())

        @block.sync
        def _(sp):
            for i, (lo, hi) in enumerate(BATCHES):
                for n in range(lo, hi):
                    sp.dma_start(b["xa"][:, n, :], x_chunk[n]).then_inc(x_in[i], 16)
                if i == 0:
                    sp.dma_start(b["g1"][:, :], rows_of(norm1_g)).then_inc(S["g1_in"], 16)
                if i == 1:
                    sp.wait_ge(S["zeroed"], 1)
                    with nc.allow_non_contiguous_dma(reason="gate columns, biases and taps"):
                        sp.dma_start(b["graw"][:, :, :], w_in[0, :, c_gates:c_gates + 4 * H]
                                     .rearrange("(k p) n -> p k n", p=P)).then_inc(S["small_in"], 16)
                        for row, g in ((0, 0), (32, 2), (64, 1), (96, 3)):
                            sp.dma_start(b["gbias"][row:row + H, 0:1], gate_bias[0, g, :]
                                         .rearrange("(h a) -> h a", a=1)).then_inc(S["small_in"], 16)
                        for k in range(3):
                            sp.dma_start(b["cw"][:, k, :], conv_w[0, k, :].rearrange("(c p) -> p c", p=P)
                                         ).then_inc(S["small_in"], 16)

            def load_state_step(i):
                if i == 0:
                    sp.wait_ge(S["colT_ps"], 3)
                    sp.wait_ge(S["rows_out"], 16 * 6)
                    for q in range(NST):
                        sp.wait_ge(stg[q], 16 * len([g for g in after_v if stage_no[g] % NST == q]))
                    with nc.allow_non_contiguous_dma(reason="decays by head"):
                        for half in range(2):
                            for dr in range(2):
                                for pr in range(2):
                                    r = 4 * dr + 2 * pr + half
                                    sp.dma_start(b["dcb"][64 * half:64 * half + 64, dr, pr, :],
                                                 decay_d[r:r + 1, :].partition_broadcast(64)
                                                 .rearrange("p a n -> p (a n)")).then_inc(S["dcb_in"], 16)
                if i >= 2:
                    sp.wait_ge(S["u_ps"], i - 1)
                for dr, c in ((0, fwd[i]), (1, bwd[i])):
                    t = slice(c * P, (c + 1) * P)
                    sp.dma_start(b["kT1"][:, i % 2, dr, :, :], qk_d[2:4, :, t].rearrange("r p t -> p r t")
                                 ).then_inc(l1[i % 2], 16)
                    sp.dma_start(b["v1"][:, i % 2, dr, :, 0:DV], v_d[t, :].rearrange("t (h n) -> t h n", h=H)
                                 ).then_inc(l1[i % 2], 16)

            step_after = [5, 5] + [pgroups[g][0] + 1 for g in STATE_AT[:NT - 2]]
            for j in range(NCH + 1):
                for i in range(NT):
                    if step_after[i] == j - 1:
                        load_state_step(i)
                if j < NCH:
                    if j >= 2:
                        sp.wait_ge(S["w_lo"], j - 1)
                    col = chunks[j][1]
                    sp.dma_start(b["wraw"][:, j % 2, :, :], w_in[0, :, col:col + CH]
                                 .rearrange("(k p) n -> p k n", p=P)).then_inc(w_ind[j % 2], 16)
            barrier(sp, 1)

            def load_scan(n):
                s, t = n % 2, tokens_of(n)
                if n >= 2:
                    sp.wait_ge(S["num_ps"], n - 1)
                sp.dma_start(d["negm"][:, s, :, :], negm_d[:, t].partition_broadcast(P)).then_inc(ld[s], 16)
                sp.dma_start(d["kTs"][:, s, :, :], qk_d[2:4, :, t].rearrange("r p t -> p r t")).then_inc(ld[s], 16)
                if n == 0:
                    sp.wait_ge(S["padded"], 1)
                for half in range(2):
                    rows = slice(64 * half, 64 * half + 64)
                    sp.dma_start(d["qz"][rows, s, half::2, :], qk_d[0:2, rows, t].rearrange("r p t -> p r t")
                                 ).then_inc(ld[s], 16)
                    sp.dma_start(d["inter"][rows, s, :, :], inter_d.rearrange("(r a) t -> a r t", a=2)[half, :, t]
                                 .partition_broadcast(64)).then_inc(ld[s], 16)
                sp.dma_start(d["vs"][:, s, :, 0:DV], v_d[t, :].rearrange("t (h n) -> t h n", h=H)).then_inc(ld[s], 16)
                sp.dma_start(d["sts"][:, s, :, :, :], state_d[ORDER[n]]).then_inc(ld[s], 16)

            def load_mix(n):
                s, t = n % 2, tokens_of(n)
                if n >= 2:
                    sp.wait_ge(S["mxl_done"], n - 1)
                sp.dma_start(d["og"][:, s, :], o_d[t, :]).then_inc(ld_mix[s], 16)
                sp.dma_start(d["cvs"][:, s, :, :], conv_d[:, :, t].rearrange("r p t -> p r t")).then_inc(ld_mix[s], 16)

            def load_x(n):
                if n >= 2:
                    sp.wait_ge(S["x1_done"], 2 * (n - 1))
                sp.dma_start(d["xs"][:, n % 2, :], x_chunk[ORDER[n]]).then_inc(ld_x[n % 2], 16)

            load_scan(0)
            load_mix(0)
            with nc.allow_non_contiguous_dma(reason="router columns"):
                sp.dma_start(d["wr"][:, :, :], w_router[0].rearrange("(k p) n -> p k n", p=P)).then_inc(S["cst_in"], 16)
            sp.dma_start(d["hgb"][:, :], rows_of(head_norm_g)).then_inc(S["cst_in"], 16)
            sp.dma_start(d["g2b"][:, :], rows_of(norm2_g)).then_inc(S["cst_in"], 16)
            for h in range(2):
                sp.dma_start(d["woraw"][:, 4 * h:4 * h + 4, :], w_out[0, 512 * h:512 * h + 512, :]
                             .rearrange("(k p) n -> p k n", p=P)).then_inc(wo_in[h], 16)
                if h == 0:
                    load_scan(1)
            load_mix(1)
            load_scan(2)
            sp.wait_ge(S["wo_lo"], KD)
            load_x(0)
            for n in range(2, NT + 1):
                if 2 < n < NT:
                    load_scan(n)
                load_x(n - 1)
                if n < NT:
                    load_mix(n)
            barrier(sp, 2)

            with sp.Fori(0, NE) as e:
                for j in range(NB):
                    wait_slot(sp, e, j)
                    if j == RING:
                        sp.wait_ge(S["gath"], 32 * e + 32)
                    w = (w_gate, w_up)[j % 2] if j < 8 else w_down
                    i = j // 2 if j < 8 else j - 8
                    src = w[0, bass.ds(e, 1), :, i * CH:(i + 1) * CH].rearrange("a (k p) n -> p (a k) n", p=P)
                    sp.dma_start(f["eraw"][:, j % RING, :, :], src).then_inc(er[j % RING], 16)
            barrier(sp, 3)
            sp.dma_start(z["gf"][:, :], rows_of(final_g.rearrange("(a d) -> a d", a=1))).then_inc(S["gf_in"], 16)
            for n in range(NT):
                sp.dma_start(z["fx"][:, n, :], acc_d[n * P:(n + 1) * P, :]).then_inc(f_in[n // 2], 16)
            for n in range(NT):
                sp.wait_ge(S["f_y"], n + 1)
                sp.dma_start(y_chunk[n], z["fx"][:, n, :]).then_inc(S["f_out"], 16)
            sp.wait_ge(S["f_out"], 16 * NT)

        @block.gpsimd
        def _(pool):
            ch = Chain(pool, S["pool_ch"])
            ch(pool.memset(ident[:, :], 0.0))
            pool.affine_select(out=ident[:, :], in_=ident[:, :], compare_op=ALU.not_equal, fill=1.0, base=0,
                               pattern=[[-1, P]], channel_multiplier=1).then_inc(S["const"], 1)
            pool.memset(b["gbias"][:, :], 0.0).then_inc(S["zeroed"], 1)
            ch(pool.memset(zrow[:, :], 0.0))
            pool.memset(b["wg_hi"][:, :, :].bitcast(F32), 0.0).then_inc(S["zeroed"], 1)
            pool.memset(b["wg_lo"][:, :, :].bitcast(F32), 0.0).then_inc(S["zeroed"], 1)
            pool.wait_ge(S["g1_in"], 16)
            for n in range(NT):
                pool.wait_ge(S["sumsq"], n + 1)
                pool.tensor_tensor(b["xa"][:, n, :], b["xa"][:, n, :], b["g1"][:, :], ALU.mult
                                   ).then_inc(S["xg_done"], 1)
            pool.wait_ge(S["hn_lo"], NT)
            pool.memset(b["R"][:, :, :], 0.0).then_inc(S["zeroed"], 1)
            pool.memset(b["LF"][:, :], 0.0).then_inc(S["zeroed"], 1)
            pool.memset(b["LI"][:, :], 0.0).then_inc(S["zeroed"], 1)

            def store_group(i):
                _, kind, part, m, t0, w = pgroups[i]
                s = stage_no[i] % NST
                who, n = ev_at[i]
                pool.wait_ge(S["ev_act"] if who == "act" else S["ev_dve"], n)
                if kind in ("k", "q"):
                    dst = qk_d[(2 if kind == "k" else 0) + m, :, t0:t0 + w]
                elif kind in ("v", "o"):
                    dst = (v_d if kind == "v" else o_d)[m * P:(m + 1) * P, part * CH:(part + 1) * CH]
                else:
                    dst = conv_d[2 * part + m, :, t0:t0 + w]
                pool.dma_start(dst, b["stage"][:, s, 0:w]).then_inc(stg[s], 16)
                if i == of_chunk[1][-1]:
                    pool.wait_ge(S["rows_nat"], 1)
                    pool.wait_ge(S["rows_exp"], 9)
                    with nc.allow_non_contiguous_dma(reason="one decay a chunk"):
                        for dr in range(2):
                            rows, dst = slice(32 * dr, 32 * dr + H), slice(4 * dr, 4 * dr + 4)
                            pool.dma_start(negm_d[dst, :], b["R"][rows, 4, :]).then_inc(S["rows_out"], 16)
                            pool.dma_start(inter_d[dst, :], b["R"][rows, 3, :]).then_inc(S["rows_out"], 16)
                            last = (P - 1, 0)[dr]
                            pool.dma_start(decay_d[dst, :], b["R"][rows, 3, last::P][:, 0:NT]
                                           ).then_inc(S["rows_out"], 16)

            def store_state(i):
                pool.wait_ge(S["st_upd"], i + 1)
                for dr, c in ((0, fwd[i]), (1, bwd[i])):
                    pool.dma_start(state_d[c, :, dr, :], b["ST"][:, i % 2, dr, :, :].rearrange("p a n -> p (a n)")
                                   ).then_inc(st_out[i % 2], 16)

            at = [(i, 1, store_group, i) for i in staged] + \
                 [(KEYS_AT[0] if i == 0 else STATE_AT[i - 1], 0, store_state, i) for i in range(NT)]
            for _, _, store, i in sorted(at, key=lambda a: a[:2]):
                store(i)
            for s in range(2):
                pool.wait_ge(st_out[s], 32 * (NT // 2))
            for s in range(NST):
                pool.wait_ge(stg[s], 16 * len([i for i in staged if stage_no[i] % NST == s]))
            barrier(pool, 1)

            pool.memset(d["qz"][:, :, :, :], 0.0).then_inc(S["padded"], 1)
            ch(pool.memset(d["masks"][:, :, :], 0.0))
            ch(pool.affine_select(out=d["masks"][:, 0, :], in_=d["masks"][:, 0, :], compare_op=ALU.is_ge, fill=NEG,
                                  base=0, pattern=[[1, P]], channel_multiplier=-1))
            pool.affine_select(out=d["masks"][:, 1, :], in_=d["masks"][:, 1, :], compare_op=ALU.is_ge, fill=NEG,
                               base=0, pattern=[[-1, P]], channel_multiplier=1).then_inc(S["masked"], 1)

            def scale_queries(n):
                s = n % 2
                pool.wait_ge(ld[s], 16 * NLD * (n // 2 + 1))
                if n >= 1:
                    pool.wait_ge(S["num_ps"], n)
                for dr in range(2):
                    for half in range(2):
                        q = pool.tensor_tensor(d["qs"][:, H * dr + half:H * dr + H:2, :], d["qz"][:, s, half::2, :],
                                               d["inter"][:, s, 2 * dr:2 * dr + 2, :], ALU.mult)
                q.then_inc(S["qs_done"], 1)
                pool.wait_ge(ld_mix[s], 16 * 2 * (n // 2 + 1))
                if n == 0:
                    pool.wait_ge(S["cst_in"], 16 * 3)
                pool.tensor_tensor(d["og"][:, s, :], d["og"][:, s, :], d["hgb"][:, :], ALU.mult
                                   ).then_inc(S["og_done"], 1)

            scale_queries(0)
            for n in range(NT + 1):
                if n + 1 < NT:
                    scale_queries(n + 1)
                if n >= 1:
                    m = n - 1
                    t = tokens_of(m)
                    pool.wait_ge(S["x1_done"], 2 * (m + 1))
                    pool.dma_start(acc_d[t, :], d["x1"][:, m % 2, :]).then_inc(x1_out[m % 2], 16)
                    pool.wait_ge(S["tk_done"], m + 1)
                    pool.dma_start(tok_d[t, :], d["tk"][:, m % 2, :]).then_inc(tk_out[m % 2], 16)
            for s in range(2):
                pool.wait_ge(x1_out[s], 16 * (NT // 2))
                pool.wait_ge(tk_out[s], 16 * (NT // 2))
            barrier(pool, 2)

            for s, credit in ((S["dn_ps"], 8), (S["gu_add"], 2), (S["ys_done"], 2), (S["yT_ps"], 4),
                              (S["hid_done"], 1), (S["hb_bf"], 1), (S["y_done"], 2),
                              (S["elo_dve"], len(BY_DVE)), (S["elo_pool"], len(BY_POOL))):
                pool.sem_inc(s, credit)

            def settle():
                pool.sem_inc(S["settled"], 1)

            def gather(e, copied):
                pool.tensor_copy(f["idx"][:, 0, 0:1], IDX[:, bass.ds(e, 1)]).then_inc(S["idx_cp"], 1)
                pool.tensor_copy(f["idx"][0:CAPP, 1, 0:1], IDX[0:CAPP, bass.ds(e + PROMPT, 1)]).then_inc(S["idx_cp"], 1)
                pool.wait_ge(S["idx_cp"], copied + 2)
                settle()
                pool.indirect_dma_start(f["xg"][:, :], None, tok_d,
                                        bass.IndirectOffsetOnAxis(ap=f["idx"][:, 0, 0:1], axis=0)
                                        ).then_inc(S["gath"], 16)
                pool.indirect_dma_start(f["xgp"][:, :], None, tok_d,
                                        bass.IndirectOffsetOnAxis(ap=f["idx"][0:CAPP, 1, 0:1], axis=0)
                                        ).then_inc(S["gath"], 16)

            def split_low(e, j):
                pool.wait_ge(S["ehi"], NB * e + j + 1)
                pool.tensor_tensor(f["elo"][:, j % RING, :, :], f["eraw"][:, j % RING, :, :],
                                   f["ehi"][:, j % RING, :, :].bitcast(F32),
                                   ALU.subtract).then_inc(S["elo_pool" if j in BY_POOL else "elo_dve"], 1)

            def scatter(e):
                pool.wait_ge(S["y_done"], 2 + 2 * e + 2)
                settle()
                pool.indirect_dma_start(acc_d, bass.IndirectOffsetOnAxis(ap=f["idx"][:, 0, 1:2], axis=0),
                                        f["yt"][:, :], None, compute_op=ALU.add).then_inc(S["scat"], 16)
                pool.indirect_dma_start(acc_d, bass.IndirectOffsetOnAxis(ap=f["idx"][0:CAPP, 1, 1:2], axis=0),
                                        f["yp"][:, :], None, compute_op=ALU.add).then_inc(S["scat"], 16)

            for j in range(4):
                split_low(0, j)
            pool.wait_ge(S["sel_done"], 2)
            settle()
            gather(0, 0)

            def expert(e, first=False, last=False):
                if not last:
                    pool.wait_ge(S["exT_ps"], 3 * e + 3)
                    settle()
                    gather(e + 1, 2 + 6 * e)
                if not first:
                    scatter(e - 1)
                for p in range(4):
                    pool.wait_ge(S["sg_done"], 4 * e + p + 1)
                    pool.wait_ge(S["hc_lo"], 4 + 4 * e + p)
                    pool.wait_ge(S["hb_bf"], 1 + 4 * e + p)
                    pool.tensor_tensor(f["hid"][:, :, :], f["sg"][:, :, :], f["gu"][:, p % 2, :, 1, :], ALU.mult
                                       ).then_inc(S["hid_done"], 1)
                    if p == 1:
                        split_low(e, 7)
                split_low(e, 11)
                pool.wait_ge(S["y_done"], 2 * e + 2)
                if first:
                    pool.wait_ge(S["sel_done"], 3)
                else:
                    pool.wait_ge(S["scat"], 32 * e)
                settle()
                pool.tensor_copy(f["idx"][:, 0, 1:2], IDX[:, bass.ds(e, 1)]).then_inc(S["idx_cp"], 1)
                pool.tensor_copy(f["idx"][0:CAPP, 1, 1:2], IDX[0:CAPP, bass.ds(e + PROMPT, 1)]).then_inc(S["idx_cp"], 1)
                pool.tensor_copy(f["gcol"][:, 0:1], GC[:, bass.ds(e, 1)]).then_inc(S["idx_cp"], 1)
                pool.tensor_copy(f["gcol"][0:CAPP, 1:2], GC[0:CAPP, bass.ds(e + PROMPT, 1)]).then_inc(S["idx_cp"], 1)
                pool.wait_ge(S["idx_cp"], 2 + 6 * e + (4 if last else 6))
                if not last:
                    split_low(e + 1, 3)

            expert(0, first=True)
            with pool.Fori(0, NE // 2 - 1) as g:
                expert(2 * g + 1)
                expert(2 * g + 2)
            expert(NE - 1, last=True)
            scatter(NE - 1)
            pool.wait_ge(S["scat"], 32 * NE)
            barrier(pool, 3)

        @block.scalar
        def _(act):
            ch = Chain(act, S["act_ch"])

            def tokens_high(n):
                act.wait_ge(S["xT_ps"], n + 1)
                act.activation(b["hn_hi"][:, :, n * P:(n + 1) * P], psum[:, 2 * (n % 3):2 * (n % 3) + 2, :]
                               .rearrange("p a (k t) -> p (a k) t", k=4), ACT.Copy).then_inc(S["hn_hi"], 1)

            for lo, hi in BATCHES:
                act.wait_ge(x_in[BATCHES.index((lo, hi))], 16 * (hi - lo))
                for n in range(lo, hi):
                    if n >= 1:
                        act.wait_ge(S["sumsq"], n)
                    act.activation(b["sq1"][:, :], b["xa"][:, n, :], ACT.Square, scale=D ** -0.5,
                                   accum_out=b["st1"][:, 0, n:n + 1]).then_inc(S["sumsq"], 1)
                if lo == 0:
                    for n in range(lo, hi):
                        tokens_high(n)
                elif hi < NT:
                    act.wait_ge(S["small_in"], 16 * 8)
                    act.wait_ge(S["zeroed"], 3)
                    for row, g in ((0, 0), (32, 2), (64, 1), (96, 3)):
                        w = act.activation(b["wg_hi"][:, :, row:row + H], b["graw"][:, :, g * H:(g + 1) * H], ACT.Copy)
                    w.then_inc(S["wg_hi"], 1)
            for n in range(BATCHES[0][1], NT):
                tokens_high(n)

            def split_high(j):
                act.wait_ge(w_ind[j % 2], 16 * (j // 2 + 1))
                if j >= 2:
                    act.wait_ge(S["proj"], of_chunk[j - 2][-1] + 1)
                act.activation(b["whi"][:, j % 2, :, :], b["wraw"][:, j % 2, :, :], ACT.Copy).then_inc(S["w_hi"], 1)

            split_high(0)
            for j in range(-1, NCH):
                if 0 <= j < NCH - 1:
                    split_high(j + 1)
                for i in of_chunk[j]:
                    _, kind, part, m, t0, w = pgroups[i]
                    if kind in EV_DVE:
                        continue
                    act.wait_ge(S["proj"], i + 1)
                    src = psum[:, 4 + (i + 2) % 4, 0:w]
                    if kind in ("k", "q", "v", "o"):
                        s = stage_no[i]
                        if s >= NST:
                            act.wait_ge(stg[s % NST], 16 * (s // NST))
                        dst = b["stage"][:, s % NST, 0:w]
                    if kind == "gate":
                        if i == 0:
                            act.wait_ge(S["hn_lo"], NT)
                        e = act.activation(b["GA"][0:GATE_ROWS, t0:t0 + w], psum[0:GATE_ROWS, 4 + (i + 2) % 4, 0:w],
                                           ACT.Identity, bias=b["gbias"][0:GATE_ROWS, 0:1])
                    elif kind == "q":
                        e = act.activation(dst, src, ACT.Copy, scale=DK ** -0.5)
                    elif kind == "o":
                        e = act.activation(dst, src, ACT.Sigmoid)
                    elif kind == "gc":
                        if part == 0 and m == 0 and t0 == 0:
                            act.wait_ge(S["colT_ps"], 3)
                            act.wait_ge(S["rows_out"], 16 * 6)
                        if part > 0:
                            act.wait_ge(S["ev_dve"], ev_at[of_chunk[j - 2][-1]][1])
                        e = act.activation(b["gcS"][:, m, t0:t0 + w], src, ACT.Copy)
                    else:
                        e = act.activation(dst, src, ACT.Copy)
                    e.then_inc(S["ev_act"], 1)
                if j == -1:
                    act.wait_ge(S["ev_act"], 3)
                    r = slice(64, GATE_ROWS)
                    ch(act.activation(b["TM"][r, :], b["GA"][r, :], ACT.Abs))
                    ch(act.activation(b["TM"][r, :], b["TM"][r, :], ACT.Exp, scale=-1.0))
                    act.activation(b["TM"][r, :], b["TM"][r, :], ACT.Ln, bias=1.0).then_inc(S["soft"], 1)
                if j == 0:
                    act.wait_ge(S["zeroed"], 4)
                    for k, (q, src, scale) in enumerate(((1, b["GA"], 1.0), (3, b["LI"], 1.0), (2, b["LF"], -1.0))):
                        act.wait_ge(S["rows_t"], k + 1)
                        act.activation(b["R"][0:H, q, :], src[0:H, :], ACT.Exp, scale=scale).then_inc(S["rows_exp"], 1)
                        for lo, hi in seqs:
                            act.activation(reverse(b["R"][32:32 + H, q, :], lo, hi), natural(src[32:32 + H, :], lo, hi),
                                           ACT.Exp, scale=scale).then_inc(S["rows_exp"], 1)
                if j == 1:
                    for k in range(3):
                        act.wait_ge(S["colT_ps"], k + 1)
                        n = min(12, 3 * NT - 12 * k)
                        act.activation(colS[:, 12 * k:12 * k + n, 0:ROWS],
                                       psum[:, k, 0:480].rearrange("p (a c) -> p a c", c=40)[:, 0:n, 0:ROWS], ACT.Copy
                                       ).then_inc(S["col_done"], 1)
            barrier(act, 1)

            def exponentials(n):
                act.wait_ge(S["x_done"], n + 1)
                if n >= 1:
                    act.wait_ge(S["sd_done"], n)
                act.activation(d["E"][:, :, :], d["X"][:, :, :], ACT.Exp).then_inc(S["e_done"], 1)

            def out_high(h):
                act.wait_ge(wo_in[h], 16)
                for k in range(4 * h, 4 * h + 4):
                    act.activation(d["woh"][:, k, :], d["woraw"][:, k, :], ACT.Copy).then_inc(S["wo_hi"], 1)

            exponentials(0)
            out_high(0)
            for n in range(NT + 2):
                if n < NT:
                    act.wait_ge(S["den_done"], n + 1)
                    if n >= 1:
                        act.wait_ge(S["ht_done"], n)
                    for h in range(H):
                        i = act.activation(d["hb"][:, h, :], psum[:, 3 + h // 2, VPAD * (h % 2):VPAD * (h % 2) + DV],
                                           ACT.Copy, scale=d["sm"][:, n % 2, 4 + h:5 + h])
                    i.then_inc(S["hb_done"], 1)
                    if n + 1 < NT:
                        exponentials(n + 1)
                    act.wait_ge(S["ht_done"], n + 1)
                    if n >= 1:
                        act.wait_ge(S["hsum"], n)
                    for h in range(H):
                        i = act.activation(d["junkh"][:, h, :], d["ht"][:, h, :], ACT.Square, scale=DV ** -0.5,
                                           accum_out=d["ms"][:, n % 2, 0, h:h + 1])
                    i.then_inc(S["hsum"], 1)
                    if n == 0:
                        out_high(1)
                    act.wait_ge(ld_mix[n % 2], 16 * 2 * (n // 2 + 1))
                    if n >= 2:
                        act.wait_ge(S["o_ps"], 2 * (n - 1))
                    act.activation(d["mxh"][:, n % 2, 0:4, :], d["cvs"][:, n % 2, :, :], ACT.Copy
                                   ).then_inc(S["mxh_done"], 1)
                if n >= 2:
                    act.wait_ge(S["tkT_ps"], n - 1)
                    if n >= 3:
                        act.wait_ge(S["lg_ps"], n - 2)
                    act.activation(d["tkT"][:, :, :], psum[:, 1:3, :].rearrange("p a (k t) -> p (a k) t", k=4),
                                   ACT.Copy).then_inc(S["tkT_done"], 1)
                if n >= 2:
                    m = n - 2
                    act.wait_ge(S["lgmax"], m + 1)
                    act.activation(aff[:, m, :], psum[:, 3, 0:NE], ACT.Exp, bias=logit_max[:, m, 0:1],
                                   accum_out=logit_max[:, m, 1:2]).then_inc(S["exps"], 1)
                if 1 <= n <= NT:
                    m = n - 1
                    act.wait_ge(S["x1_done"], 2 * (m + 1))
                    if m >= 1:
                        act.wait_ge(S["sum2"], m)
                    act.activation(d["junk"][:, :], d["x1"][:, m % 2, :], ACT.Square, scale=D ** -0.5,
                                   accum_out=d["mt"][:, m % 2, 0, :]).then_inc(S["sum2"], 1)
                if n < NT:
                    act.wait_ge(S["mixT_ps"], n + 1)
                    act.activation(d["mxh"][:, n % 2, 4:8, :], psum[:, 5, :].rearrange("p (k t) -> p k t", k=4),
                                   ACT.Copy).then_inc(S["mxh_done"], 1)
            barrier(act, 2)

            def high(e, j, first=False):
                act.wait_ge(er[j % RING], 16 * (2 * e + j // RING + 1))
                if not first:
                    if j < 2:
                        act.wait_ge(S["gu_ps"], 8 * e)
                    elif j < RING:
                        act.wait_ge(S["dn_ps"], 8 * e + 2 * (j - 2) + 2)
                    else:
                        act.wait_ge(S["gu_ps"], 8 * e + 2 * ((j - RING) // 2) + 2)
                act.activation(f["ehi"][:, j % RING, :, :], f["eraw"][:, j % RING, :, :], ACT.Copy
                               ).then_inc(S["ehi"], 1)

            def narrow_tokens(e, s):
                act.wait_ge(S["xc_hi"], 3 * e + 3)
                act.activation(f["xb"][:, s, :, :], f["xc"][:, s, :, 0, :].bitcast(F32), ACT.Copy
                               ).then_inc(S["xb_done"], 1)

            def tokens_high(e, s, which):
                for g in which:
                    k0, nk = TG[g]
                    act.wait_ge(S["exT_ps"], 3 * e + g + 1)
                    act.activation(f["xc"][:, s, k0:k0 + nk, 0, :], psum[:, 6 + g % 2, 0:nk * NC]
                                   .rearrange("p (k t) -> p k t", k=nk), ACT.Copy).then_inc(S["xc_hi"], 1)

            def y_half(e, h, first=False, last=False):
                act.wait_ge(S["yT_ps"], 4 + 8 * e + 4 * h + 4)
                act.wait_ge(S["idx_cp"], 2 + 6 * e + (4 if last else 6))
                if not first:
                    act.wait_ge(S["scat"], 32 * e)
                act.activation(f["yt"][:, 512 * h:512 * h + 512], psum[:, 6, :], ACT.Copy, scale=f["gcol"][:, 0:1])
                act.activation(f["yp"][:, 512 * h:512 * h + 512], psum[0:CAPP, 7, :], ACT.Copy,
                               scale=f["gcol"][0:CAPP, 1:2]).then_inc(S["y_done"], 1)

            for j in range(RING):
                high(0, j, True)
            tokens_high(0, 0, (0, 1, 2))
            narrow_tokens(0, 0)

            def expert(e, s, first=False, last=False):
                if not first:
                    y_half(e - 1, 1)
                for p in range(4):
                    act.wait_ge(S["gu_add"], 2 + 8 * e + 2 * p + 2)
                    act.wait_ge(S["hid_done"], 1 + 4 * e + p)
                    act.activation(f["sg"][:, :, :], f["gu"][:, p % 2, :, 0, :], ACT.Silu).then_inc(S["sg_done"], 1)
                    if p < 3:
                        high(e, 2 * p + 6)
                    if p == 1 and not last:
                        tokens_high(e + 1, 1 - s, (0,))
                    act.wait_ge(S["hid_done"], 1 + 4 * e + p + 1)
                    if p == 0:
                        act.wait_ge(S["dn_ps"], 8 * e + 8)
                    act.activation(f["hc"][:, 2 * p:2 * p + 2, 0, :], f["hid"][:, :, :], ACT.Copy
                                   ).then_inc(S["hc_hi"], 1)
                    act.activation(f["hbf"][:, 2 * p:2 * p + 2, :], f["hid"][:, :, :], ACT.Copy
                                   ).then_inc(S["hb_bf"], 1)
                    if p < 3:
                        high(e, 2 * p + 7)
                    elif not last:
                        tokens_high(e + 1, 1 - s, (1, 2))
                        high(e + 1, 0)
                        high(e + 1, 1)
                        narrow_tokens(e + 1, 1 - s)
                for q in range(4):
                    if not last:
                        high(e + 1, q + 2)
                    if q == 2:
                        y_half(e, 0, first, last)

            expert(0, 0, first=True)
            with act.Fori(0, NE // 2 - 1) as g:
                expert(2 * g + 1, 1)
                expert(2 * g + 2, 0)
            expert(NE - 1, 1, last=True)
            y_half(NE - 1, 1, last=True)
            barrier(act, 3)

            for n in range(NT):
                act.wait_ge(f_in[n // 2], 16 * 2)
                if n >= 1:
                    act.wait_ge(S["f_sum"], n)
                act.activation(z["fq"][:, :], z["fx"][:, n, :], ACT.Square, scale=D ** -0.5,
                               accum_out=z["fs"][:, 0, n:n + 1]).then_inc(S["f_sum"], 1)

        @block.vector
        def _(dve):
            ch = Chain(dve, S["dve_ch"])

            def inverse_root(r, v, t):
                ch(dve.tensor_scalar(v, v, EPS, None, ALU.add))
                ch(dve.tensor_scalar(r.bitcast(U32), v.bitcast(U32), -0.5, float(0x5f3759df), ALU.mult, ALU.add))
                c = 1.0
                for _ in range(3):
                    ch(dve.tensor_tensor(t, r, r, ALU.mult))
                    ch(dve.tensor_tensor(t, t, v, ALU.mult))
                    ch(dve.scalar_tensor_tensor(r, t, -3.0 * c * c, r, ALU.add, ALU.mult))
                    c = -2.0 * c ** 3
                ch(dve.tensor_scalar(r, r, 1.0 / c, None, ALU.mult))

            def tokens_low(n):
                dve.wait_ge(S["hn_hi"], n + 1)
                dve.tensor_tensor(b["hn_lo"][:, :, n * P:(n + 1) * P], psum[:, 2 * (n % 3):2 * (n % 3) + 2, :]
                                  .rearrange("p a (k t) -> p (a k) t", k=4),
                                  b["hn_hi"][:, :, n * P:(n + 1) * P].bitcast(F32), ALU.subtract
                                  ).then_inc(S["hn_lo"], 1)

            for lo, hi in BATCHES:
                dve.wait_ge(S["sumsq"], hi)
                inverse_root(b["st1"][:, 1, lo:hi], b["st1"][:, 0, lo:hi], b["st1"][:, 2, lo:hi])
                for n in range(lo, hi):
                    dve.wait_ge(S["xg_done"], n + 1)
                    dve.tensor_scalar(b["xa"][:, n, :], b["xa"][:, n, :], b["st1"][:, 1, n:n + 1], None, ALU.mult
                                      ).then_inc(S["xn_done"], 1)
                if 0 < lo and hi < NT:
                    dve.wait_ge(S["wg_hi"], 1)
                    for row, g in ((0, 0), (32, 2), (64, 1), (96, 3)):
                        w = dve.tensor_tensor(b["wg_lo"][:, :, row:row + H], b["graw"][:, :, g * H:(g + 1) * H],
                                              b["wg_hi"][:, :, row:row + H].bitcast(F32), ALU.subtract)
                    w.then_inc(S["wg_lo"], 1)
                if hi < NT:
                    for n in range(lo, hi):
                        tokens_low(n)
            for n in range(*BATCHES[-1]):
                tokens_low(n)

            def split_low(j):
                dve.wait_ge(S["w_hi"], j + 1)
                dve.tensor_tensor(b["wlo"][:, j % 2, :, :], b["wraw"][:, j % 2, :, :],
                                  b["whi"][:, j % 2, :, :].bitcast(F32), ALU.subtract).then_inc(S["w_lo"], 1)

            def last_col(t2, c):
                return t2[0:ROWS, (c + 1) * P - 1:(c + 1) * P]

            def by_chunk(t2):
                return t2[0:ROWS, :].rearrange("r (c t) -> r c t", t=P)

            def gate_rows():
                dve.wait_ge(S["zeroed"], 6)
                dve.wait_ge(S["soft"], 1)
                r = slice(64, GATE_ROWS)
                ch(dve.scalar_tensor_tensor(b["GA"][r, :], b["GA"][r, :], 0.0, b["TM"][r, :], ALU.min, ALU.subtract))
                dve.tensor_copy(b["LF"][0:H, :], b["GA"][64:64 + H, :])
                dve.tensor_copy(b["LI"][0:H, :], b["GA"][0:H, :])
                for lo, hi in seqs:
                    dve.tensor_copy(natural(b["LF"][32:32 + H, :], lo, hi), reverse(b["GA"][96:96 + H, :], lo, hi))
                    i = dve.tensor_copy(natural(b["LI"][32:32 + H, :], lo, hi),
                                        reverse(b["GA"][32:32 + H, :], lo, hi))
                ch(i)
                zero = zrow[:, 0:1].to_broadcast([ROWS, P])
                for c in range(NT):
                    t = slice(c * P, (c + 1) * P)
                    i = dve.tensor_tensor_scan(b["LF"][:, t], b["LF"][:, t], zero, 0.0, ALU.add, ALU.add)
                ch(i)
                ch(dve.tensor_tensor(b["LI"][:, :], b["LI"][:, :], b["LF"][:, :], ALU.subtract))
                for c in range(NT):
                    t = slice(c * P, (c + 1) * P)
                    if c in starts:
                        ch(dve.memset(b["mst"][:, c:c + 1], 0.0))
                    else:
                        ch(dve.tensor_tensor(b["mst"][:, c:c + 1], last_col(b["MM"], c - 1),
                                             last_col(b["LF"], c - 1), ALU.add))
                    ch(dve.tensor_tensor_scan(b["MM"][:, t], b["LI"][:, t], zero, b["mst"][:, c:c + 1],
                                              ALU.max, ALU.add))
                ends = by_chunk(b["MM"])[:, :, P - 1:P].to_broadcast([ROWS, NT, P])
                dve.tensor_tensor(by_chunk(b["GA"]), by_chunk(b["LI"]), ends, ALU.subtract).then_inc(S["rows_t"], 1)
                dve.tensor_copy(b["R"][0:H, 0, :], b["LI"][0:H, :])
                dve.tensor_scalar(b["R"][0:H, 4, :], b["MM"][0:H, :], -1.0, None, ALU.mult)
                for lo, hi in seqs:
                    dve.tensor_copy(reverse(b["R"][32:32 + H, 0, :], lo, hi), natural(b["LI"][32:32 + H, :], lo, hi))
                    i = dve.tensor_scalar(reverse(b["R"][32:32 + H, 4, :], lo, hi),
                                          natural(b["MM"][32:32 + H, :], lo, hi), -1.0, None, ALU.mult)
                i.then_inc(S["rows_nat"], 1)
                dve.wait_ge(S["rows_nat"], 1)
                dve.tensor_tensor(by_chunk(b["LI"]), b["mst"][:, :].rearrange("r (c a) -> r c a", a=1)
                                  .to_broadcast([ROWS, NT, P]), by_chunk(b["MM"]), ALU.subtract
                                  ).then_inc(S["rows_t"], 1)
                dve.tensor_tensor(b["LF"][:, :], b["LF"][:, :], b["MM"][:, :], ALU.add).then_inc(S["rows_t"], 1)

            def weigh_keys(i):
                if i == 0:
                    dve.memset(b["v1"][:, :, :, :, DV:VPAD], 1.0)
                    dve.memset(b["ST"][:, 1, :, :, :], 0.0)
                    dve.memset(b["ST"][:, 0, :, :, :], 0.0).then_inc(S["st_upd"], 1)
                    dve.wait_ge(S["st_upd"], 1)
                    dve.wait_ge(S["col_done"], 3)
                    dve.wait_ge(S["dcb_in"], 16 * 8)
                dve.wait_ge(S["kT_ps"], i + 1)
                for dr, c in ((0, fwd[i]), (1, bwd[i])):
                    w = colS[:, colslot(c, 1), 32 * dr:32 * dr + H].rearrange("p (h a) -> p h a", a=1)
                    k = dve.tensor_tensor(b["wk"][:, dr, :, :], psum[:, 0, dr * QK:(dr + 1) * QK]
                                          .rearrange("p (h n) -> p h n", h=H), w.to_broadcast([P, H, DK]), ALU.mult)
                k.then_inc(S["wk_done"], 1)

            def update_states(i):
                dve.wait_ge(S["u_ps"], i + 1)
                if i + 1 < NT:
                    if i >= 1:
                        dve.wait_ge(st_out[(i - 1) % 2], 32 * ((i - 1) // 2 + 1))
                    for dr, c in ((0, fwd[i]), (1, bwd[i])):
                        for pr in range(2):
                            new = b["ST"][:, (i + 1) % 2, dr, pr, 0:VA]
                            if i + 1 in starts:
                                k = dve.memset(new, 0.0)
                            else:
                                k = dve.scalar_tensor_tensor(new, b["ST"][:, i % 2, dr, pr, 0:VA],
                                                             b["dcb"][:, dr, pr, c:c + 1],
                                                             psum[:, 1 + dr, VPAD * pr:VPAD * pr + VA],
                                                             ALU.mult, ALU.add)
                    k.then_inc(S["st_upd"], 1)
                    dve.wait_ge(S["st_upd"], i + 2)

            split_low(0)
            for j in range(-1, NCH):
                if 0 <= j < NCH - 1:
                    split_low(j + 1)
                if j == 0:
                    gate_rows()
                if j >= 0 and of_chunk[j][0] == KEYS_AT[0]:
                    dve.wait_ge(S["colT_ps"], 3)
                    dve.wait_ge(S["rows_out"], 16 * 6)
                if j >= 0 and chunks[j][0] == "gc" and chunks[j][2] == 0:
                    dve.wait_ge(S["colT_ps"], 3)
                    dve.wait_ge(S["rows_out"], 16 * 6)
                    for m in range(2):
                        for col in (0, SP_ + 1, SP_ + 2, T + 3):
                            i = dve.memset(b["CU"][:, m, col:col + 1], 0.0)
                    ch(i)
                for i in of_chunk[j]:
                    if i in STATE_AT:
                        update_states(STATE_AT.index(i))
                    if i in KEYS_AT:
                        weigh_keys(KEYS_AT.index(i))
                    _, kind, part, m, t0, w = pgroups[i]
                    if kind not in EV_DVE:
                        continue
                    dve.wait_ge(S["proj"], i + 1)
                    src = psum[:, 4 + (i + 2) % 4, 0:w]
                    off = 1 if t0 < SP_ else 3
                    if kind == "u":
                        dve.wait_ge(S["ev_act"], ev_at[of_chunk[j - 1][-1]][1])
                        dve.tensor_tensor(b["CU"][:, m, t0 + off:t0 + off + w], src, b["gcS"][:, m, t0:t0 + w], ALU.mult
                                          ).then_inc(S["ev_dve"], 1)
                        if i == of_chunk[j][-1]:
                            dve.wait_ge(S["ev_dve"], ev_at[i][1])
                            for mm in range(2):
                                for s0, n, o in ((0, SP_, 0), (SP_, SS_, 2)):
                                    cv = b["CV"][:, mm, s0:s0 + n]
                                    tap = [b["cw"][:, k, 2 * part + mm:2 * part + mm + 1] for k in range(3)]
                                    x = [b["CU"][:, mm, s0 + o + k:s0 + o + k + n] for k in range(3)]
                                    ch(dve.tensor_scalar(cv, x[0], tap[0], None, ALU.mult))
                                    ch(dve.scalar_tensor_tensor(cv, x[1], tap[1], cv, ALU.mult, ALU.add))
                                    ch(dve.scalar_tensor_tensor(cv, x[2], tap[2], cv, ALU.mult, ALU.add))
                    else:
                        s = stage_no[i]
                        if s >= NST:
                            dve.wait_ge(stg[s % NST], 16 * (s // NST))
                        dve.tensor_tensor(b["stage"][:, s % NST, 0:w], src, b["CV"][:, m, t0:t0 + w], ALU.mult
                                          ).then_inc(S["ev_dve"], 1)
            barrier(dve, 1)

            dve.memset(d["vs"][:, :, :, DV:VPAD], 1.0)
            dve.memset(GV[:, :], 0.0)
            ch(dve.memset(GIF[:, :], 0.0))

            ch(dve.memset(AFF[0:HALF2 + NE, :], -1.0))

            both_halves, half = slice(0, HALF2 + NE), SS_ // 2

            def choose(rows, width, count, r0, r1):
                for r in range(r0, r1):
                    best = GV[rows, 8 * r:8 * r + 8]
                    ch(dve.max(best, AFF[rows, 0:width]))
                    ch(dve.max_index(GI[rows, 8 * r:8 * r + 8], best, AFF[rows, 0:width]))
                    if (r + 1) * 8 < count:
                        ch(dve.match_replace(AFF[rows, 0:width], best, AFF[rows, 0:width], -2.0))

            def residual(n, h):
                dve.wait_ge(S["o_ps"], 2 * n + h + 1)
                if h == 0:
                    dve.wait_ge(ld_x[n % 2], 16 * (n // 2 + 1))
                    if n >= 2:
                        dve.wait_ge(x1_out[n % 2], 16 * (n // 2))
                        dve.wait_ge(S["tk_done"], n - 1)
                dve.tensor_tensor(d["x1"][:, n % 2, 512 * h:512 * h + 512], psum[:, 6 + h, :],
                                  d["xs"][:, n % 2, 512 * h:512 * h + 512], ALU.add).then_inc(S["x1_done"], 1)

            def exponents(n):
                dve.wait_ge(ld[n % 2], 16 * NLD * (n // 2 + 1))
                if n >= 1:
                    dve.wait_ge(S["e_done"], n)
                for r in range(2 * H):
                    dr, h = r // H, r % H
                    i = dve.scalar_tensor_tensor(d["X"][:, r, :], d["negm"][:, n % 2, r, :],
                                                 colS[:, colslot(ORDER[n], 0), 32 * dr + h:32 * dr + h + 1],
                                                 d["masks"][:, dr, :], ALU.add, ALU.min)
                i.then_inc(S["x_done"], 1)

            def decayed_scores(n):
                dve.wait_ge(S["e_done"], n + 1)
                dve.wait_ge(S["s_ps"], n + 1)
                if n >= 1:
                    dve.wait_ge(S["num_ps"], n)
                for dr in range(2):
                    i = dve.tensor_tensor(d["SD"][:, H * dr:H * dr + H, :], psum[:, 0, :]
                                          .rearrange("p (h t) -> p h t", h=H), d["E"][:, H * dr:H * dr + H, :],
                                          ALU.mult)
                i.then_inc(S["sd_done"], 1)

            def out_low(h):
                for k in range(4 * h, 4 * h + 4):
                    dve.wait_ge(S["wo_hi"], k + 1)
                    dve.tensor_tensor(d["wol"][:, k, :], d["woraw"][:, k, :], d["woh"][:, k, :].bitcast(F32),
                                      ALU.subtract).then_inc(S["wo_lo"], 1)

            dve.wait_ge(S["masked"], 1)
            exponents(0)
            decayed_scores(0)
            out_low(0)
            for n in range(NT + 2):
                s = n % 2
                if n < NT:
                    dve.wait_ge(S["num_ps"], n + 1)
                    den = psum[:, 1:5, 0:2 * VPAD].rearrange("p a (b c) -> p a b c", c=VPAD)[:, :, :, DV]
                    floor = colS[:, colslot(ORDER[n], 2), :]
                    low, inv = d["sm"][:, s, 8:16], d["sm"][:, s, 0:8]
                    for dr in range(2):
                        i = dve.scalar_tensor_tensor(low[:, 4 * dr:4 * dr + 4].rearrange("p (a c) -> p a c", a=2),
                                                     den[:, 2 * dr:2 * dr + 2, :], -1.0,
                                                     floor[:, 32 * dr:32 * dr + H].rearrange("p (a c) -> p a c", a=2),
                                                     ALU.mult, ALU.max)
                    ch(i)
                    ch(dve.tensor_tensor(low.rearrange("p (a c) -> p a c", a=4), den,
                                         low.rearrange("p (a c) -> p a c", a=4), ALU.max))
                    dve.reciprocal(inv, low).then_inc(S["den_done"], 1)
                    if n + 1 < NT:
                        exponents(n + 1)
                    dve.wait_ge(S["den_done"], n + 1)
                    dve.wait_ge(S["hb_done"], n + 1)
                    if n >= 1:
                        dve.wait_ge(S["hsum"], n)
                    for h in range(H):
                        i = dve.scalar_tensor_tensor(d["ht"][:, h, :],
                                                     psum[:, 1 + h // 2, VPAD * (h % 2):VPAD * (h % 2) + DV],
                                                     d["sm"][:, s, h:h + 1], d["hb"][:, h, :], ALU.mult, ALU.add)
                    i.then_inc(S["ht_done"], 1)
                    if n + 1 < NT:
                        decayed_scores(n + 1)
                if 1 <= n <= NT:
                    residual(n - 1, 0)
                if n < NT:
                    dve.wait_ge(S["hsum"], n + 1)
                    inverse_root(d["ms"][:, s, 1, :], d["ms"][:, s, 0, :], d["ms"][:, s, 2, :])
                    dve.wait_ge(S["og_done"], n + 1)
                    if n >= 1:
                        dve.wait_ge(S["mixT_ps"], n)
                    for h in range(H):
                        i = dve.scalar_tensor_tensor(d["mix"][:, h, :], d["ht"][:, h, :], d["ms"][:, s, 1, h:h + 1],
                                                     d["og"][:, s, h * DV:(h + 1) * DV], ALU.mult, ALU.mult)
                    i.then_inc(S["mix_done"], 1)
                    if n == 0:
                        out_low(1)
                if n == NT:
                    dve.wait_ge(S["affT_ps"], 1)
                    for i in range(NS // 4):
                        ch(dve.tensor_copy(AFF[HALF2 * i:HALF2 * i + NE, :], psum[0:NE, (0, 4)[i], :]))
                    choose(both_halves, half, CAPS, 0, 4)
                if n >= 2:
                    m = n - 2
                    dve.wait_ge(S["lg_ps"], m + 1)
                    dve.tensor_reduce(logit_max[:, m, 0:1], psum[:, 3, 0:NE], AX_X, ALU.max, negate=True
                                      ).then_inc(S["lgmax"], 1)
                if 1 <= n <= NT:
                    residual(n - 1, 1)
                if n < NT:
                    dve.wait_ge(S["mxh_done"], 2 * n + 1)
                    dve.tensor_tensor(d["mxl"][:, s, 0:4, :], d["cvs"][:, s, :, :],
                                      d["mxh"][:, s, 0:4, :].bitcast(F32), ALU.subtract)
                if n < NT:
                    dve.wait_ge(S["mxh_done"], 2 * n + 2)
                    dve.tensor_tensor(d["mxl"][:, s, 4:8, :], psum[:, 5, :].rearrange("p (k t) -> p k t", k=4),
                                      d["mxh"][:, s, 4:8, :].bitcast(F32), ALU.subtract).then_inc(S["mxl_done"], 1)
                if 1 <= n <= NT:
                    m = n - 1
                    q = m % 2
                    dve.wait_ge(S["sum2"], m + 1)
                    if m == 0:
                        dve.wait_ge(S["cst_in"], 16 * 3)
                    inverse_root(d["mt"][:, q, 1, :], d["mt"][:, q, 0, :], d["mt"][:, q, 2, :])
                    if m >= 2:
                        dve.wait_ge(tk_out[q], 16 * (m // 2))
                        dve.wait_ge(S["tkT_ps"], m - 1)
                    dve.scalar_tensor_tensor(d["tk"][:, q, :], d["x1"][:, q, :], d["mt"][:, q, 1, :], d["g2b"][:, :],
                                             ALU.mult, ALU.mult).then_inc(S["tk_done"], 1)
                if n == NT:
                    choose(both_halves, half, CAPS, 4, 8)
                if n >= 2:
                    m = n - 2
                    dve.wait_ge(S["exps"], m + 1)
                    ch(dve.reciprocal(logit_max[:, m, 2:3], logit_max[:, m, 1:2]))
                    dve.tensor_scalar(aff[:, m, :], aff[:, m, :], logit_max[:, m, 2:3], None, ALU.mult
                                      ).then_inc(S["aff_done"], 1)

            barrier(dve, 2)
            choose(both_halves, half, CAPS, 8, CAPS // 8)
            dve.tensor_copy(GIF[0:NE, :], GI[0:NE, :])
            dve.tensor_copy(GV2[:, :], GV[HALF2:HALF2 + NE, ::-1])
            ch(dve.tensor_scalar(GI2[:, :], GI[HALF2:HALF2 + NE, ::-1], float(half), None, ALU.add))
            dve.tensor_tensor(from_first[:, :], GV[0:NE, :], GV2[:, :], ALU.is_ge)
            ch(dve.tensor_tensor(GIF[0:NE, :], GIF[0:NE, :], GI2[:, :], ALU.subtract))
            ch(dve.tensor_tensor(GV[0:NE, :], GV[0:NE, :], GV2[:, :], ALU.max))
            ch(dve.tensor_tensor(GIF[0:NE, :], GIF[0:NE, :], from_first[:, :], ALU.mult))
            dve.tensor_tensor(GIF[0:NE, :], GIF[0:NE, :], GI2[:, :], ALU.add).then_inc(S["topk"], 1)
            dve.wait_ge(S["affT_ps"], 2)
            ch(dve.tensor_copy(AFF[PROMPT:SEL, 0:SP_], psum[0:NE, 1, 0:SP_]))
            choose(slice(PROMPT, SEL), SP_, CAPP, 0, CAPP // 8)
            dve.tensor_copy(GIF[PROMPT:SEL, 0:CAPP], GI[PROMPT:SEL, 0:CAPP]).then_inc(S["topk"], 1)
            dve.wait_ge(S["selT_ps"], 1)
            dve.tensor_scalar(IDX[:, 0:NE], psum[:, 5, 0:NE], float(SP_), None, ALU.add).then_inc(S["sel_done"], 1)
            dve.tensor_copy(IDX[:, PROMPT:SEL], psum[:, 5, PROMPT:SEL]).then_inc(S["sel_done"], 1)
            dve.wait_ge(S["selT_ps"], 2)
            dve.tensor_copy(GC[:, :], psum[:, 4, 0:SEL]).then_inc(S["sel_done"], 1)

            def low(e, j):
                if j in BY_DVE:
                    dve.wait_ge(S["ehi"], NB * e + j + 1)
                    dve.tensor_tensor(f["elo"][:, j % RING, :, :], f["eraw"][:, j % RING, :, :],
                                      f["ehi"][:, j % RING, :, :].bitcast(F32), ALU.subtract
                                      ).then_inc(S["elo_dve"], 1)

            def tokens_low(e, s, which):
                for g in which:
                    k0, nk = TG[g]
                    dve.wait_ge(S["xc_hi"], 3 * e + g + 1)
                    dve.tensor_tensor(f["xc"][:, s, k0:k0 + nk, 1, :], psum[:, 6 + g % 2, 0:nk * NC]
                                      .rearrange("p (k t) -> p k t", k=nk),
                                      f["xc"][:, s, k0:k0 + nk, 0, :].bitcast(F32), ALU.subtract
                                      ).then_inc(S["xc_lo"], 1)

            tokens_low(0, 0, (0, 1, 2))
            dve.sem_inc(S["hc_lo"], 4)

            def expert(e, s, first=False, last=False):
                for p in range(4):
                    for m in range(2):
                        i = 2 * p + m
                        dve.wait_ge(S["gu_ps"], 8 * e + i + 1)
                        if m == 0 and not (first and p < 2):
                            dve.wait_ge(S["hid_done"], 1 + 4 * e + p - 1)
                        base = 2 * (i % 2)
                        both = psum[:, base:base + 2, 0:2 * NC].rearrange("p a (t n) -> p a n t", t=2)
                        dve.tensor_reduce(f["gu"][:, p % 2, m, :, :], both, AX_X, ALU.add).then_inc(S["gu_add"], 1)
                        if m == 0 and p < 3:
                            low(e, 2 * p + 4)
                    if p < 3:
                        low(e, 2 * p + 5)
                    if p == 1 and not last:
                        tokens_low(e + 1, 1 - s, (0,))
                    dve.wait_ge(S["hc_hi"], 4 * e + p + 1)
                    dve.tensor_tensor(f["hc"][:, 2 * p:2 * p + 2, 1, :], f["hid"][:, :, :],
                                      f["hc"][:, 2 * p:2 * p + 2, 0, :].bitcast(F32), ALU.subtract
                                      ).then_inc(S["hc_lo"], 1)
                if not last:
                    tokens_low(e + 1, 1 - s, (1, 2))
                for q in range(4):
                    for m in range(2):
                        i = 2 * q + m
                        dve.wait_ge(S["dn_ps"], 8 + 8 * e + i + 1)
                        dve.wait_ge(S["yT_ps"], 8 * e + i + 1)
                        both = psum[:, DOWN_BANK[i % 3], 0:2 * NC].rearrange("p (t n) -> p n t", t=2)
                        dve.tensor_reduce(f["ys"][:, i % 4, :], both, AX_X, ALU.add).then_inc(S["ys_done"], 1)
                    if q == 0:
                        low(e, 10)
                    elif not last:
                        low(e + 1, q - 1)

            expert(0, 0, first=True)
            with dve.Fori(0, NE // 2 - 1) as g:
                expert(2 * g + 1, 1)
                expert(2 * g + 2, 0)
            expert(NE - 1, 1, last=True)
            barrier(dve, 3)

            dve.wait_ge(S["gf_in"], 16)
            for n in range(NT):
                if n in [lo for lo, _ in BATCHES]:
                    c = slice(*[batch for batch in BATCHES if batch[0] == n][0])
                    dve.wait_ge(S["f_sum"], c.stop)
                    inverse_root(z["fs"][:, 1, c], z["fs"][:, 0, c], z["fs"][:, 2, c])
                dve.scalar_tensor_tensor(z["fx"][:, n, :], z["fx"][:, n, :], z["fs"][:, 1, n:n + 1], z["gf"][:, :],
                                         ALU.mult, ALU.mult).then_inc(S["f_y"], 1)

        @block.tensor
        def _(pe):
            pe.wait_ge(S["const"], 1)

            def transpose_tokens(n):
                pe.wait_ge(S["xn_done"], n + 1)
                if n >= 3:
                    pe.wait_ge(S["hn_lo"], n - 2)
                for k in range(KD):
                    i = pe.transpose(psum[:, 2 * (n % 3) + k // 4, (k % 4) * P:(k % 4 + 1) * P],
                                     b["xa"][:, n, k * P:(k + 1) * P], ident[:, :])
                i.then_inc(S["xT_ps"], 1)

            def transpose_keys(i):
                pe.wait_ge(l1[i % 2], 16 * 4 * (i // 2 + 1))
                if i == 0:
                    pe.wait_ge(S["col_done"], 3)
                else:
                    pe.wait_ge(S["wk_done"], i)
                for dr in range(2):
                    for pr in range(2):
                        tr = pe.transpose(psum[:, 0, dr * QK + pr * P:dr * QK + (pr + 1) * P],
                                          b["kT1"][:, i % 2, dr, pr, :], ident[:, :])
                tr.then_inc(S["kT_ps"], 1)

            def chunk_sums(i):
                pe.wait_ge(S["wk_done"], i + 1)
                if i >= 1:
                    pe.wait_ge(S["st_upd"], i + 1)
                for dr in range(2):
                    for pr in range(2):
                        for half in range(2):
                            h = 2 * pr + half
                            mm = pe.matmul(psum[64 * half:64 * half + 64, 1 + dr, VPAD * pr:VPAD * pr + VA],
                                           b["wk"][:, dr, h, :], b["v1"][:, i % 2, dr, h, 0:VA], start=True, stop=True)
                mm.then_inc(S["u_ps"], 1)

            for n in range(BATCHES[1][1]):
                transpose_tokens(n)
            for i, (j, kind, part, m, t0, w) in enumerate(pgroups):
                if i in STATE_AT:
                    chunk_sums(STATE_AT.index(i))
                if i in KEYS_AT:
                    transpose_keys(KEYS_AT.index(i))
                if kind == "gate":
                    if i == 0:
                        pe.wait_ge(S["wg_lo"], 1)
                    if i == 1:
                        for n in range(*BATCHES[2]):
                            transpose_tokens(n)
                    pe.wait_ge(S["hn_lo"], (t0 + w) // P)
                elif i == of_chunk[j][0]:
                    pe.wait_ge(S["w_lo"], j + 1)
                if i >= 4:
                    who, c = ev_at[i - 4]
                    pe.wait_ge(S["ev_act"] if who == "act" else S["ev_dve"], c)
                for k in range(KD):
                    if kind in ("v", "o"):
                        t = slice(m * P, (m + 1) * P)
                        xh, xl = b["hn_hi"][:, k, t], b["hn_lo"][:, k, t]
                        wh, wl = b["whi"][:, j % 2, k, :], b["wlo"][:, j % 2, k, :]
                        pairs = ((xh, wh), (xh, wl), (xl, wh))
                        o = psum[:, 4 + (i + 2) % 4, 0:w]
                    else:
                        t = slice(t0, t0 + w)
                        xh, xl = b["hn_hi"][:, k, t], b["hn_lo"][:, k, t]
                        if kind == "gate":
                            wh, wl = b["wg_hi"][:, k, 0:GATE_ROWS], b["wg_lo"][:, k, 0:GATE_ROWS]
                            o = psum[0:GATE_ROWS, 4 + (i + 2) % 4, 0:w]
                        else:
                            c = slice(m * P, (m + 1) * P)
                            wh, wl = b["whi"][:, j % 2, k, c], b["wlo"][:, j % 2, k, c]
                            o = psum[:, 4 + (i + 2) % 4, 0:w]
                        pairs = ((wh, xh), (wh, xl), (wl, xh))
                    for a, (lhs, rhs) in enumerate(pairs):
                        mm = pe.matmul(o, lhs, rhs, start=(k == 0 and a == 0), stop=(k == KD - 1 and a == 2))
                mm.then_inc(S["proj"], 1)
                if i == of_chunk[1][-1]:
                    pe.wait_ge(S["rows_nat"], 1)
                    pe.wait_ge(S["rows_exp"], 9)
                    for c in range(NT):
                        for q in range(3):
                            a = colslot(c, q)
                            tr = pe.transpose(psum[:, a // 12, (a % 12) * 40:(a % 12) * 40 + ROWS],
                                              b["R"][:, q, c * P:(c + 1) * P], ident[0:ROWS, 0:ROWS])
                            if a % 12 == 11 or a == 3 * NT - 1:
                                tr.then_inc(S["colT_ps"], 1)
            barrier(pe, 1)

            def project(n, h, k0=0, k1=KD):
                if k0 == 0:
                    pe.wait_ge(S["mxl_done"], n + 1)
                    if n >= 1:
                        pe.wait_ge(S["x1_done"], 2 * (n - 1) + h + 1)
                c = slice(512 * h, 512 * h + 512)
                for k in range(k0, k1):
                    for a, (x, w) in enumerate((("mxh", "woh"), ("mxh", "wol"), ("mxl", "woh"))):
                        mm = pe.matmul(psum[:, 6 + h, :], d[x][:, n % 2, k, :], d[w][:, k, c],
                                       start=(k == 0 and a == 0), stop=(k == KD - 1 and a == 2))
                if k1 == KD:
                    mm.then_inc(S["o_ps"], 1)

            def scores(n):
                pe.wait_ge(ld[n % 2], 16 * NLD * (n // 2 + 1))
                if n >= 1:
                    pe.wait_ge(S["sd_done"], n)
                for h in range(H):
                    mm = pe.matmul(psum[:, 0, h * P:(h + 1) * P], d["kTs"][:, n % 2, h // 2, :],
                                   d["qz"][:, n % 2, h, :], start=True, stop=True)
                mm.then_inc(S["s_ps"], 1)

            scores(0)
            for n in range(NT + 2):
                s = n % 2
                if n < NT:
                    pe.wait_ge(S["sd_done"], n + 1)
                    pe.wait_ge(S["qs_done"], n + 1)
                    if n >= 1:
                        pe.wait_ge(S["ht_done"], n)
                    if n >= 3:
                        pe.wait_ge(S["exps"], n - 2)
                    for dr in range(2):
                        for h in range(H):
                            o = psum[:, 1 + 2 * dr + h // 2, VPAD * (h % 2):VPAD * (h % 2) + VA]
                            pe.matmul(o, d["SD"][:, H * dr + h, :], d["vs"][:, s, h, 0:VA], start=True, stop=False)
                            mm = pe.matmul(o, d["qs"][:, H * dr + h, :], d["sts"][:, s, dr, h // 2, 0:VA],
                                           start=False, stop=True)
                    mm.then_inc(S["num_ps"], 1)
                if n + 1 < NT:
                    scores(n + 1)
                if 1 <= n <= NT:
                    project(n - 1, 0)
                if n == NT:
                    pe.wait_ge(S["aff_done"], NS)
                    for i in range(NS):
                        tr = pe.transpose(psum[0:NE, (0, 4)[i // 4], (i % 4) * P:(i % 4 + 1) * P], aff[:, i, :],
                                          ident[:, :])
                    tr.then_inc(S["affT_ps"], 1)
                if 1 <= n <= NT:
                    project(n - 1, 1, 0, 2)
                if n >= 2:
                    m = n - 2
                    pe.wait_ge(S["tk_done"], m + 1)
                    if n < NT:
                        pe.wait_ge(S["ht_done"], n + 1)
                    if m >= 1:
                        pe.wait_ge(S["tkT_done"], m)
                    for k in range(KD):
                        tr = pe.transpose(psum[:, 1 + k // 4, (k % 4) * P:(k % 4 + 1) * P],
                                          d["tk"][:, m % 2, k * P:(k + 1) * P], ident[:, :])
                    tr.then_inc(S["tkT_ps"], 1)
                if 1 <= n <= NT:
                    project(n - 1, 1, 2, 6)
                if n >= 2:
                    pe.wait_ge(S["tkT_done"], m + 1)
                    if m >= 1:
                        pe.wait_ge(S["exps"], m)
                    for k in range(KD):
                        mm = pe.matmul(psum[:, 3, 0:NE], d["tkT"][:, k, :], d["wr"][:, k, :], start=(k == 0),
                                       stop=(k == KD - 1))
                    mm.then_inc(S["lg_ps"], 1)
                if 1 <= n <= NT:
                    project(n - 1, 1, 6, KD)
                if n < NT:
                    if n >= 1:
                        pe.wait_ge(S["mxl_done"], n)
                    pe.wait_ge(S["mix_done"], n + 1)
                    for h in range(H):
                        tr = pe.transpose(psum[:, 5, h * P:(h + 1) * P], d["mix"][:, h, :], ident[:, :])
                    tr.then_inc(S["mixT_ps"], 1)
            pe.wait_ge(S["aff_done"], NT)
            for i in range(NTP):
                tr = pe.transpose(psum[0:NE, 1, i * P:(i + 1) * P], aff[:, NS + i, :], ident[:, :])
            tr.then_inc(S["affT_ps"], 1)
            barrier(pe, 2)
            pe.wait_ge(S["topk"], 2)
            pe.transpose(psum[:, 5, 0:SEL], GIF[:, :], ident[0:SEL, 0:SEL]).then_inc(S["selT_ps"], 1)
            pe.transpose(psum[:, 4, 0:SEL], GV[:, :], ident[0:SEL, 0:SEL]).then_inc(S["selT_ps"], 1)

            def token_columns(e, which):
                pe.wait_ge(S["gath"], 32 * e + 32)
                for g in which:
                    k0, nk = TG[g]
                    if g == 2:
                        pe.wait_ge(S["xc_lo"], 3 * e + 1)
                    for k in range(nk):
                        c = slice((k0 + k) * P, (k0 + k + 1) * P)
                        o = psum[:, 6 + g % 2, k * NC:(k + 1) * NC]
                        pe.transpose(o[:, 0:CAPS], f["xg"][:, c], ident[:, :])
                        tr = pe.transpose(o[:, CAPS:NC], f["xgp"][:, c], ident[0:CAPP, 0:CAPP])
                    tr.then_inc(S["exT_ps"], 1)

            def rows_back(e, i):
                pe.wait_ge(S["ys_done"], 2 + 8 * e + i + 1)
                c = slice((i % 4) * P, (i % 4 + 1) * P)
                pe.transpose(psum[:, 6, c], f["ys"][:, i % 4, 0:CAPS], ident[:, :])
                pe.transpose(psum[0:CAPP, 7, c], f["ys"][:, i % 4, CAPS:NC], ident[:, :]).then_inc(S["yT_ps"], 1)

            def second_half_back(e):
                pe.wait_ge(S["y_done"], 2 + 2 * e + 1)
                for i in range(4, KD):
                    rows_back(e, i)

            def products(o, q, c, x, xb, k0=0, k1=KD):
                for k in range(k0, k1):
                    pe.matmul(o[:, 0:2 * NC], f["ehi"][:, q, k, c], x[:, k, :, :].rearrange("p a t -> p (a t)"),
                              start=(k == 0), stop=False, skip_group_check=True)
                for k in range(k0, k1):
                    mm = pe.matmul(o[:, NC:2 * NC], f["elo"][:, q, k, c], xb[:, k, :], start=False,
                                   stop=(k == KD - 1), skip_group_check=True)
                return mm

            token_columns(0, (0, 1, 2))

            def expert(e, s, first=False, last=False):
                pe.wait_ge(S["xc_lo"], 3 * e + 3)
                pe.wait_ge(S["xb_done"], e + 1)
                for p in range(4):
                    wait_split(pe, e, 2 * p)
                    wait_split(pe, e, 2 * p + 1)
                    for m in range(2):
                        i = 2 * p + m
                        pe.wait_ge(S["gu_add"], 8 * e + i + 1)
                        if i == 1 and not first:
                            pe.wait_ge(S["ys_done"], 2 + 8 * e)
                        for a in range(2):
                            mm = products(psum[:, 2 * (i % 2) + a, :], (2 * p + a) % RING, slice(m * P, (m + 1) * P),
                                          f["xc"][:, s, :, :, :], f["xb"][:, s, :, :])
                        mm.then_inc(S["gu_ps"], 1)
                        if i == 0 and not first:
                            second_half_back(e - 1)
                        if i == 3 and not last:
                            pe.wait_ge(S["y_done"], 2 * e + 2)
                            token_columns(e + 1, (0,))
                        if i == 7 and not last:
                            token_columns(e + 1, (1, 2))
                for q in range(4):
                    wait_split(pe, e, 8 + q)
                    tiles = [(psum[:, DOWN_BANK[(2 * q + m) % 3], :], (8 + q) % RING, slice(m * P, (m + 1) * P),
                              f["hc"], f["hbf"]) for m in range(2)]
                    if q == 0:
                        pe.wait_ge(S["ys_done"], 8 * e + 1)
                        pe.wait_ge(S["hc_lo"], 4 + 4 * e + 3)
                        pe.wait_ge(S["hb_bf"], 1 + 4 * e + 3)
                        products(*tiles[0], 0, KF - 2)
                        pe.wait_ge(S["ys_done"], 8 * e + 2)
                        products(*tiles[1], 0, KF - 2)
                        pe.wait_ge(S["hc_lo"], 4 + 4 * e + 4)
                        pe.wait_ge(S["hb_bf"], 1 + 4 * e + 4)
                    for m in range(2):
                        i = 2 * q + m
                        if i == 2:
                            pe.wait_ge(S["gu_add"], 2 + 8 * e + 8)
                        elif i > 2:
                            pe.wait_ge(S["ys_done"], 8 * e + i)
                        products(*tiles[m], KF - 2 if q == 0 else 0, KF).then_inc(S["dn_ps"], 1)
                        if i == 2:
                            if last:
                                pe.wait_ge(S["y_done"], 2 * e + 2)
                            else:
                                pe.wait_ge(S["xc_lo"], 3 * (e + 1) + 3)
                        if 2 <= i < 6:
                            rows_back(e, i - 2)

            expert(0, 0, first=True)
            with pe.Fori(0, NE // 2 - 1) as g:
                expert(2 * g + 1, 1)
                expert(2 * g + 2, 0)
            expert(NE - 1, 1, last=True)
            second_half_back(NE - 1)
            barrier(pe, 3)


_INS = ['x_prompt', 'x_sample', 'norm1_g', 'w_in', 'conv_w', 'gate_bias', 'head_norm_g', 'w_out', 'norm2_g',
        'w_router', 'w_gate', 'w_up', 'w_down', 'final_g']


def kernel(**inputs):
    import numpy as _np
    import concourse.bacc as _bacc
    from concourse import mybir as _mybir
    from concourse.bass_utils import run_bass_kernel_spmd as _run

    nc = _bacc.Bacc("TRN2", target_bir_lowering=False, num_devices=1)
    arrays, args = {}, []
    for name in _INS:
        a = _np.ascontiguousarray(inputs[name])
        arrays[f"in_{name}_dram"] = a
        args.append(nc.dram_tensor(f"in_{name}_dram", a.shape, _mybir.dt.from_np(a.dtype), kind="ExternalInput").ap())
    outs = [("y_prompt", inputs["x_prompt"].shape), ("y_sample", inputs["x_sample"].shape)]
    for name, shape in outs:
        args.append(nc.dram_tensor(f"out_{name}_dram", tuple(shape), _mybir.dt.float32, kind="ExternalOutput").ap())
    hybrid_conv_mlstm_moe(nc, *args)
    r = _run(nc, [arrays], core_ids=[0])
    return tuple(r.results[0][f"out_{name}_dram"] for name, _ in outs)
```
